# Optimizing a Trainium2 kernel written in Bass

```python
import math
import jax, jax.numpy as jnp
from jax import lax
import numpy as np

D_MODEL = 2048
BATCH = 1
SEQ = 256
DEPTH = 1

ML_HEADS = 8
ML_QK_DIM = D_MODEL // 2 // ML_HEADS
ML_V_DIM = D_MODEL // ML_HEADS
ML_QK_WIDTH = ML_HEADS * ML_QK_DIM
ML_WIDTH = ML_HEADS * ML_V_DIM
GATE_SOFTCAP = 15.0
DN_HEADS = 16
DN_HEAD_DIM = D_MODEL // DN_HEADS
DN_WIDTH = DN_HEADS * DN_HEAD_DIM
CONV_WIDTH = 4
CHUNK = 64
NORM_EPS = 1e-6

IN_SIZES = (ML_QK_WIDTH, ML_QK_WIDTH, ML_WIDTH, ML_WIDTH, ML_WIDTH, ML_HEADS, ML_HEADS,
            3 * DN_WIDTH, DN_WIDTH, DN_HEADS, DN_HEADS,
            D_MODEL, D_MODEL)
IN_DIM = sum(IN_SIZES)
OUT_DIM = ML_WIDTH + DN_WIDTH


def _rmsnorm(x, w=None):
    xf = x.astype(jnp.float32)
    y = xf * lax.rsqrt(jnp.mean(xf * xf, axis=-1, keepdims=True) + NORM_EPS)
    return y if w is None else y * w.astype(jnp.float32)

def _l2norm(x):
    return x * lax.rsqrt(jnp.sum(x * x, axis=-1, keepdims=True) + NORM_EPS)

def _heads(t, n):
    b, s, _ = t.shape
    return t.reshape(b, s, n, -1).transpose(0, 2, 1, 3)

def _merge_heads(t):
    b, h, s, d = t.shape
    return t.transpose(0, 2, 1, 3).reshape(b, s, h * d)

def _chunks(t):
    b, h, s = t.shape[:3]
    t = t.reshape(b, h, s // CHUNK, CHUNK, *t.shape[3:])
    return jnp.moveaxis(t, 2, 0)

def _unchunk(t):
    nc, b, h, l, d = t.shape
    return jnp.moveaxis(t, 0, 2).reshape(b, h, nc * l, d)

def _softcap(t):
    return GATE_SOFTCAP * jnp.tanh(t / GATE_SOFTCAP)

def _mlstm_chunkwise(q, k, v, i_pre, logf):
    b_, h_, s_, dk = q.shape
    dv = v.shape[-1]
    q = q * (dk ** -0.5)
    qc, kc, vc = _chunks(q), _chunks(k), _chunks(v)
    ic, fc = _chunks(i_pre), _chunks(logf)
    bcum = jnp.cumsum(fc, axis=-1)
    causal = jnp.tril(jnp.ones((CHUNK, CHUNK), dtype=bool))
    dmat = bcum[..., :, None] - bcum[..., None, :] + ic[..., None, :]
    dmat = jnp.where(causal, dmat, -jnp.inf)
    dmax = jnp.max(dmat, axis=-1)
    scores = jnp.einsum('cbhtd,cbhsd->cbhts', qc, kc)
    w_end = bcum[..., -1:] - bcum + ic
    w_end_max = jnp.max(w_end, axis=-1)

    def step(carry, inp):
        C, n, m = carry
        q_c, k_c, v_c, b_c, dm_c, dmax_c, sc_c, we_c, wem_c = inp
        inter_log = b_c + m[..., None]
        m_t = jnp.maximum(inter_log, dmax_c)
        inter_w = jnp.exp(inter_log - m_t)
        intra_w = jnp.exp(dm_c - m_t[..., None]) * sc_c
        num = (inter_w[..., None] * jnp.einsum('bhtd,bhde->bhte', q_c, C)
               + jnp.einsum('bhts,bhse->bhte', intra_w, v_c))
        den = inter_w * jnp.einsum('bhtd,bhd->bht', q_c, n) + jnp.sum(intra_w, axis=-1)
        h = num / jnp.maximum(jnp.abs(den), jnp.exp(-m_t))[..., None]
        m_new = jnp.maximum(b_c[..., -1] + m, wem_c)
        decay = jnp.exp(b_c[..., -1] + m - m_new)
        kw = k_c * jnp.exp(we_c - m_new[..., None])[..., None]
        C_new = decay[..., None, None] * C + jnp.einsum('bhsd,bhse->bhde', kw, v_c)
        n_new = decay[..., None] * n + jnp.sum(kw, axis=-2)
        return (C_new, n_new, m_new), h

    init = (jnp.zeros((b_, h_, dk, dv), jnp.float32),
            jnp.zeros((b_, h_, dk), jnp.float32),
            jnp.zeros((b_, h_), jnp.float32))
    _, hs = lax.scan(step, init, (qc, kc, vc, bcum, dmat, dmax, scores, w_end, w_end_max))
    return _unchunk(hs)

def _gated_delta_chunkwise(q, k, v, beta, g):
    b_, h_, s_, dk = q.shape
    dv = v.shape[-1]
    q = q * (dk ** -0.5)
    qc, kc, vc = _chunks(q), _chunks(k), _chunks(v)
    bc, gc = _chunks(beta), _chunks(g)
    gam = jnp.cumsum(gc, axis=-1)
    incl = jnp.tril(jnp.ones((CHUNK, CHUNK), dtype=bool))
    strict = jnp.tril(jnp.ones((CHUNK, CHUNK), dtype=bool), k=-1)
    rel = gam[..., :, None] - gam[..., None, :]
    decay_mat = jnp.where(incl, jnp.exp(jnp.where(incl, rel, 0.0)), 0.0)
    kk = jnp.einsum('cbhtd,cbhsd->cbhts', kc, kc)
    a_mat = jnp.where(strict, bc[..., :, None] * kk * decay_mat, 0.0)
    lhs = a_mat + jnp.eye(CHUNK, dtype=a_mat.dtype)
    rhs = jnp.concatenate([vc * bc[..., None], kc * (bc * jnp.exp(gam))[..., None]], axis=-1)
    sol = lax.linalg.triangular_solve(lhs, rhs, left_side=True, lower=True, unit_diagonal=True)
    w_val, w_k = sol[..., :dv], sol[..., dv:]
    qk = jnp.einsum('cbhtd,cbhsd->cbhts', qc, kc) * decay_mat
    q_dec = qc * jnp.exp(gam)[..., None]
    k_end = kc * jnp.exp(gam[..., -1:] - gam)[..., None]
    g_end = jnp.exp(gam[..., -1])

    def step(S, inp):
        wv, wk, qk_c, qd, ke, ge = inp
        u = wv - jnp.einsum('bhtd,bhde->bhte', wk, S)
        o = jnp.einsum('bhtd,bhde->bhte', qd, S) + jnp.einsum('bhts,bhse->bhte', qk_c, u)
        S_new = ge[..., None, None] * S + jnp.einsum('bhsd,bhse->bhde', ke, u)
        return S_new, o

    S0 = jnp.zeros((b_, h_, dk, dv), jnp.float32)
    _, os_ = lax.scan(step, S0, (w_val, w_k, qk, q_dec, k_end, g_end))
    return _unchunk(os_)

def _causal_conv_silu(x, w):
    kw = w.shape[0]
    s = x.shape[1]
    xp = jnp.pad(x, ((0, 0), (kw - 1, 0), (0, 0)))
    y = sum(w[j].astype(jnp.float32) * xp[:, j:j + s] for j in range(kw))
    return jax.nn.silu(y)

def _hybrid_layer(h, norm_w, w_in, ml_i_bias, ml_f_bias, ml_norm_w,
                  dn_conv_w, dn_a_log, dn_dt_bias, dn_norm_w, w_out):
    u = _rmsnorm(h, norm_w)
    proj = jnp.matmul(u, w_in.astype(jnp.float32))
    idx = np.cumsum(IN_SIZES)[:-1].tolist()
    (ml_q, ml_k, ml_v, ml_o, ml_z, ml_i, ml_f,
     dn_qkv, dn_z, dn_b, dn_a, gate_a, gate_b) = jnp.split(proj, idx, axis=-1)

    i_pre = _softcap(ml_i + ml_i_bias).transpose(0, 2, 1)
    logf = jax.nn.log_sigmoid(_softcap(ml_f + ml_f_bias)).transpose(0, 2, 1)
    h_a = _mlstm_chunkwise(_heads(ml_q, ML_HEADS), _heads(ml_k, ML_HEADS),
                           _heads(ml_v, ML_HEADS), i_pre, logf)
    h_a = _merge_heads(_rmsnorm(h_a)) * ml_norm_w.astype(jnp.float32)
    h_a = h_a * jax.nn.sigmoid(ml_o) * jax.nn.silu(ml_z)

    qkv = _causal_conv_silu(dn_qkv, dn_conv_w)
    dq, dk_, dv_ = jnp.split(qkv, 3, axis=-1)
    dq = _l2norm(_heads(dq, DN_HEADS))
    dk_ = _l2norm(_heads(dk_, DN_HEADS))
    dv_ = _heads(dv_, DN_HEADS)
    beta = jax.nn.sigmoid(dn_b).transpose(0, 2, 1)
    g = (-jnp.exp(dn_a_log.astype(jnp.float32))
         * jax.nn.softplus(dn_a + dn_dt_bias)).transpose(0, 2, 1)
    h_b = _gated_delta_chunkwise(dq, dk_, dv_, beta, g)
    h_b = _rmsnorm(h_b, dn_norm_w)
    h_b = _merge_heads(h_b) * jax.nn.silu(dn_z)

    w_out = w_out.astype(jnp.float32)
    y_a = jnp.matmul(h_a, w_out[:ML_WIDTH])
    y_b = jnp.matmul(h_b, w_out[ML_WIDTH:])
    return jax.nn.sigmoid(gate_a) * y_a + jax.nn.sigmoid(gate_b) * y_b

def first_inputs(seed: int = 0) -> dict:
    key = jax.random.key(seed)
    ks = jax.random.split(key, 13)
    x = jax.random.normal(ks[0], (BATCH, SEQ, D_MODEL), jnp.float32)
    norm_w = 1.0 + 0.05 * jax.random.normal(ks[1], (DEPTH, D_MODEL), jnp.float32)
    w_in = jax.random.normal(ks[2], (DEPTH, D_MODEL, IN_DIM), jnp.float32) * D_MODEL ** -0.5
    ml_i_bias = 0.1 * jax.random.normal(ks[3], (DEPTH, ML_HEADS), jnp.float32)
    ml_f_bias = 3.0 + 0.5 * jax.random.normal(ks[4], (DEPTH, ML_HEADS), jnp.float32)
    ml_norm_w = 1.0 + 0.05 * jax.random.normal(ks[5], (DEPTH, ML_WIDTH), jnp.float32)
    dn_conv_w = jax.random.normal(ks[6], (DEPTH, CONV_WIDTH, 3 * DN_WIDTH), jnp.float32) * CONV_WIDTH ** -0.5
    dn_a_log = jnp.log(jax.random.uniform(ks[7], (DEPTH, DN_HEADS), jnp.float32, 1.0, 16.0))
    dt = jnp.exp(jax.random.uniform(ks[8], (DEPTH, DN_HEADS), jnp.float32,
                                    math.log(1e-3), math.log(1e-1)))
    dn_dt_bias = dt + jnp.log(-jnp.expm1(-dt))
    dn_norm_w = 1.0 + 0.05 * jax.random.normal(ks[9], (DEPTH, DN_HEAD_DIM), jnp.float32)
    w_out = jax.random.normal(ks[10], (DEPTH, OUT_DIM, D_MODEL), jnp.float32) * OUT_DIM ** -0.5
    final_norm_w = 1.0 + 0.05 * jax.random.normal(ks[11], (D_MODEL,), jnp.float32)
    return {"x": x, "norm_w": norm_w, "w_in": w_in, "ml_i_bias": ml_i_bias,
            "ml_f_bias": ml_f_bias, "ml_norm_w": ml_norm_w, "dn_conv_w": dn_conv_w,
            "dn_a_log": dn_a_log, "dn_dt_bias": dn_dt_bias, "dn_norm_w": dn_norm_w,
            "w_out": w_out, "final_norm_w": final_norm_w}

def first_block(x, norm_w, w_in, ml_i_bias, ml_f_bias, ml_norm_w, dn_conv_w,
              dn_a_log, dn_dt_bias, dn_norm_w, w_out, final_norm_w):
    h = x
    for l in range(DEPTH):
        y = _hybrid_layer(h, norm_w[l], w_in[l], ml_i_bias[l], ml_f_bias[l], ml_norm_w[l],
                          dn_conv_w[l], dn_a_log[l], dn_dt_bias[l], dn_norm_w[l], w_out[l])
        h = h + y.astype(h.dtype)
    return _rmsnorm(h, final_norm_w).astype(x.dtype)


DEPTH_2 = 2

LEFT_CHUNKS = 8
BAND = (LEFT_CHUNKS + 1) * CHUNK
MAX_REL = 128
N_MEM = 256

MIX_WIDTH = D_MODEL
A_WIDTH = MIX_WIDTH // 2
A_HEADS = 8
A_HEAD_DIM = A_WIDTH // A_HEADS
B_WIDTH = MIX_WIDTH // 4
B_HEADS = 4
B_DV = B_WIDTH // B_HEADS
B_DK = B_DV // 2
B_KEY_WIDTH = B_HEADS * B_DK
GATE_RANK = 16
GATE_TAU = 16.0
M_WIDTH = MIX_WIDTH // 4
M_HEADS = 4
M_HEAD_DIM = M_WIDTH // M_HEADS

IN_SPLITS = (A_WIDTH, A_WIDTH, A_WIDTH, A_WIDTH,
             B_KEY_WIDTH, B_KEY_WIDTH, B_WIDTH, B_WIDTH, GATE_RANK,
             M_WIDTH, M_WIDTH)
IN_WIDTH = sum(IN_SPLITS)
VALUE_SPLITS = (2, 6)

DEEPNORM_ALPHA = (2.0 * DEPTH_2) ** 0.25
DEEPNORM_BETA = (8.0 * DEPTH_2) ** -0.25
LN_EPS = 1e-5
RMS_EPS = 1e-6
NEG_INF = -1e30


def layer_norm(x, g, b):
    xf = x.astype(jnp.float32)
    mu = jnp.mean(xf, axis=-1, keepdims=True)
    var = jnp.mean(jnp.square(xf - mu), axis=-1, keepdims=True)
    y = (xf - mu) * lax.rsqrt(var + LN_EPS) * g.astype(jnp.float32) + b.astype(jnp.float32)
    return y.astype(x.dtype)

def chunk_band_attention(q, k, v, rel_table):
    B, S, H, Dh = q.shape
    nc = S // CHUNK
    qc = q.reshape(B, nc, CHUNK, H, Dh)
    pad = ((0, 0), (LEFT_CHUNKS * CHUNK, 0), (0, 0), (0, 0))
    kp = jnp.pad(k, pad).reshape(B, nc + LEFT_CHUNKS, CHUNK, H, Dh)
    vp = jnp.pad(v, pad).reshape(B, nc + LEFT_CHUNKS, CHUNK, H, Dh)
    k_band = jnp.concatenate([kp[:, i:i + nc] for i in range(LEFT_CHUNKS + 1)], axis=2)
    v_band = jnp.concatenate([vp[:, i:i + nc] for i in range(LEFT_CHUNKS + 1)], axis=2)
    scores = jnp.einsum('bnqhd,bnkhd->bnhqk', qc, k_band).astype(jnp.float32) * (Dh ** -0.5)
    dist = jnp.arange(CHUNK)[:, None] + LEFT_CHUNKS * CHUNK - jnp.arange(BAND)[None, :]
    rel_idx = jnp.clip(dist, -MAX_REL, MAX_REL) + MAX_REL
    bias = rel_table[:, rel_idx].astype(jnp.float32)
    key_chunk = jnp.arange(nc)[:, None] - LEFT_CHUNKS + (jnp.arange(BAND) // CHUNK)[None, :]
    valid = key_chunk >= 0
    scores = jnp.where(valid[None, :, None, None, :], scores + bias[None, None], NEG_INF)
    p = jax.nn.softmax(scores, axis=-1).astype(v.dtype)
    out = jnp.einsum('bnhqk,bnkhd->bnqhd', p, v_band)
    return out.reshape(B, S, H, Dh)

def gla_chunk_recurrence(q, k, v, log_g):
    B, S, H, DK = q.shape
    DV = v.shape[-1]
    nc = S // CHUNK
    f32 = jnp.float32

    def to_chunks(t):
        return jnp.moveaxis(t.astype(f32).reshape(B, nc, CHUNK, H, t.shape[-1]), 1, 0)

    qs = to_chunks(q * (DK ** -0.5))
    ks, vs, gs = to_chunks(k), to_chunks(v), to_chunks(log_g)

    def step(state, inp):
        qc, kc, vc, gc = inp
        b = jnp.cumsum(gc, axis=1)
        decay = jnp.exp(-jnp.abs(b[:, :, None] - b[:, None, :]))
        attn = jnp.einsum('bihd,bjhd,bijhd->bhij', qc, kc, decay)
        o_intra = jnp.einsum('bhij,bjhv->bihv', attn, vc)
        o_inter = jnp.einsum('bihd,bhdv->bihv', qc * jnp.exp(b), state)
        b_last = b[:, -1]
        k_dec = kc * jnp.exp(b_last[:, None] - b)
        new_state = jnp.exp(b_last)[..., None] * state + jnp.einsum('bjhd,bjhv->bhdv', k_dec, vc)
        return new_state, o_intra + o_inter

    state0 = jnp.zeros((B, H, DK, DV), f32)
    _, out = lax.scan(step, state0, (qs, ks, vs, gs))
    return jnp.moveaxis(out, 0, 1).reshape(B, S, H, DV)

def memory_attention(q, mk, mv):
    s = jnp.einsum('bshd,bmhd->bhsm', q, mk).astype(jnp.float32) * (q.shape[-1] ** -0.5)
    p = jax.nn.softmax(s, axis=-1).astype(mv.dtype)
    return jnp.einsum('bhsm,bmhd->bshd', p, mv)

def hybrid_layer(x, mem, w_in, rel_table, gate_w, gate_b, gla_norm_g, w_mem_kv, w_out, ln_g, ln_b):
    B, S, _ = x.shape
    h = x @ w_in
    cuts = [int(c) for c in np.cumsum(IN_SPLITS)[:-1]]
    a_q, a_k, a_v, a_z, b_q, b_k, b_v, b_z, b_lr, m_q, m_z = jnp.split(h, cuts, axis=-1)

    heads_a = lambda t: t.reshape(B, S, A_HEADS, A_HEAD_DIM)
    y_a = chunk_band_attention(heads_a(a_q), heads_a(a_k), heads_a(a_v), rel_table).reshape(B, S, A_WIDTH)

    gate_logit = (b_lr @ gate_w + gate_b).astype(jnp.float32)
    log_g = jax.nn.log_sigmoid(gate_logit) / GATE_TAU
    heads_k = lambda t: t.reshape(B, S, B_HEADS, B_DK)
    o_b = gla_chunk_recurrence(heads_k(b_q), heads_k(b_k), b_v.reshape(B, S, B_HEADS, B_DV), heads_k(log_g))
    o_b = o_b * lax.rsqrt(jnp.mean(jnp.square(o_b), axis=-1, keepdims=True) + RMS_EPS) * gla_norm_g.astype(jnp.float32)
    y_b = o_b.reshape(B, S, B_WIDTH).astype(x.dtype)

    mkv = mem @ w_mem_kv
    mk, mv = jnp.split(mkv, 2, axis=-1)
    heads_m = lambda t: t.reshape(t.shape[0], t.shape[1], M_HEADS, M_HEAD_DIM)
    y_m = memory_attention(heads_m(m_q), heads_m(mk), heads_m(mv)).reshape(B, S, M_WIDTH)

    y = jnp.concatenate([y_a * jax.nn.silu(a_z), y_b * jax.nn.silu(b_z), y_m * jax.nn.silu(m_z)], axis=-1)
    out = y @ w_out
    return layer_norm(DEEPNORM_ALPHA * x + out, ln_g, ln_b)

def second_inputs(seed: int = 0) -> dict:
    key = jax.random.key(seed)
    ks = jax.random.split(key, 12)
    f32 = jnp.float32
    x = jax.random.normal(ks[0], (BATCH, SEQ, D_MODEL), f32)
    mem = jax.random.normal(ks[1], (N_MEM, D_MODEL), f32)[None].repeat(BATCH, axis=0) \
        + 0.1 * jax.random.normal(ks[2], (BATCH, N_MEM, D_MODEL), f32)
    col_scale = jnp.concatenate([
        jnp.full((n,), DEEPNORM_BETA if i in VALUE_SPLITS else 1.0, f32) for i, n in enumerate(IN_SPLITS)])
    w_in = jax.random.normal(ks[3], (DEPTH_2, D_MODEL, IN_WIDTH), f32) * (D_MODEL ** -0.5) * col_scale
    a_rel_bias = 0.1 * jax.random.normal(ks[4], (DEPTH_2, A_HEADS, 2 * MAX_REL + 1), f32)
    b_gate_w = jax.random.normal(ks[5], (DEPTH_2, GATE_RANK, B_KEY_WIDTH), f32) * (GATE_RANK ** -0.5)
    b_gate_b = 0.1 * jax.random.normal(ks[6], (DEPTH_2, B_KEY_WIDTH), f32)
    b_norm_g = 1.0 + 0.02 * jax.random.normal(ks[7], (DEPTH_2, B_DV), f32)
    kv_scale = jnp.concatenate([jnp.ones((M_WIDTH,), f32), jnp.full((M_WIDTH,), DEEPNORM_BETA, f32)])
    w_mem_kv = jax.random.normal(ks[8], (DEPTH_2, D_MODEL, 2 * M_WIDTH), f32) * (D_MODEL ** -0.5) * kv_scale
    w_out = jax.random.normal(ks[9], (DEPTH_2, MIX_WIDTH, D_MODEL), f32) * (MIX_WIDTH ** -0.5) * DEEPNORM_BETA
    ln_g = 1.0 + 0.02 * jax.random.normal(ks[10], (DEPTH_2, D_MODEL), f32)
    ln_b = 0.02 * jax.random.normal(ks[11], (DEPTH_2, D_MODEL), f32)
    return {"x": x, "mem": mem, "w_in": w_in, "a_rel_bias": a_rel_bias, "b_gate_w": b_gate_w,
            "b_gate_b": b_gate_b, "b_norm_g": b_norm_g, "w_mem_kv": w_mem_kv, "w_out": w_out,
            "ln_g": ln_g, "ln_b": ln_b}

def second_block(x, mem, w_in, a_rel_bias, b_gate_w, b_gate_b, b_norm_g, w_mem_kv, w_out, ln_g, ln_b):
    h = x
    for l in range(DEPTH_2):
        h = hybrid_layer(h, mem, w_in[l], a_rel_bias[l], b_gate_w[l], b_gate_b[l], b_norm_g[l],
                         w_mem_kv[l], w_out[l], ln_g[l], ln_b[l])
    return h


def setup_inputs(seed=0):
    out = dict(first_inputs(seed))
    for name, value in second_inputs(seed + 1).items():
        if name != "x":
            out[name + "_2"] = value
    return out


def reference(
    x, norm_w, w_in, ml_i_bias, ml_f_bias, ml_norm_w, dn_conv_w, dn_a_log, dn_dt_bias,
    dn_norm_w, w_out, final_norm_w, mem_2, w_in_2, a_rel_bias_2, b_gate_w_2, b_gate_b_2,
    b_norm_g_2, w_mem_kv_2, w_out_2, ln_g_2, ln_b_2,
):
    x = first_block(
        x, norm_w, w_in, ml_i_bias, ml_f_bias, ml_norm_w, dn_conv_w, dn_a_log, dn_dt_bias,
        dn_norm_w, w_out, final_norm_w,
    )
    return second_block(
        x, mem_2, w_in_2, a_rel_bias_2, b_gate_w_2, b_gate_b_2, b_norm_g_2, w_mem_kv_2, w_out_2,
        ln_g_2, ln_b_2,
    )


_drawn_inputs = setup_inputs


def setup_inputs(seed=0):
    import zlib

    import numpy as np

    out = dict(_drawn_inputs(seed))
    spreads = {}
    factors = {'ml_i_bias': 8.0,
     'ml_norm_w': 8.0,
     'dn_norm_w': 4.518,
     'mem_2': 7.32,
     'a_rel_bias_2': 24.295,
     'b_gate_w_2': 3.794,
     'b_gate_b_2': 8.0,
     'b_norm_g_2': 8.0,
     'w_mem_kv_2': 6.209}
    for name, (base, spread) in spreads.items():
        noise = np.random.default_rng([zlib.crc32(name.encode()), seed]).standard_normal(out[name].shape)
        drawn = base * np.exp(spread * noise) if base else spread * noise
        out[name] = __import__('jax').numpy.asarray(drawn.astype(out[name].dtype))
    for name, factor in factors.items():
        out[name] = (out[name] * factor).astype(out[name].dtype)
    return out
```

```python
from contextlib import ExitStack

import numpy as np
import concourse.bass as bass
from concourse import mybir

F32 = mybir.dt.float32
F32R = mybir.dt.float32r
U32 = mybir.dt.uint32
ACT = mybir.ActivationFunctionType
ALU = mybir.AluOpType
AX = mybir.AxisListType

P = 128
S = 256
M = S // P
D = 2048
KT = D // P
NBLK = 512
CH = 2
NCH = KT // CH
RING = 4
AHEAD = 2
U = 1024
EPS = 1e-6
LN_EPS = 1e-5
NEG = -1e30
ML_H, DN_H, A_H, GL_H, M_H = 8, 16, 8, 4, 4
ALPHA = (2.0 * 2) ** 0.25

C_MLQ, C_MLK, C_MLV, C_MLO, C_MLZ, C_IF = 0, 1024, 2048, 4096, 6144, 8192
C_DN, C_DNZ, C_BA, C_GA, C_GB = 8208, 14352, 16400, 16432, 18480
C_AQ, C_AK, C_AV, C_AZ, C_BQ, C_BV, C_BZ, C_LR, C_MQ, C_MZ = 0, 1024, 2048, 3072, 4096, 4608, 5120, 5632, 5648, 6160
BIASW = 384


def steps_of(sem, names):
    return sem, {name: i + 1 for i, name in enumerate(names)}, [0]


def signal(steps, name):
    sem, place, at = steps
    assert place[name] == at[0] + 1, name
    at[0] = (at[0] + 1) % len(place)
    return sem, 1


def done(steps, name, g=0):
    sem, place, _ = steps
    return sem, g * len(place) + place[name]


def build(nc, x, norm_w, w_in, ml_i_bias, ml_f_bias, ml_norm_w, dn_conv_w, dn_a_log, dn_dt_bias, dn_norm_w,
          w_out, final_norm_w, mem, w_in2, rel, gate_w, gate_b, gla_g, w_mkv, w_out2, ln_g, ln_b, out):
    IN1, IN2 = w_in.shape[2], w_in2.shape[2]
    x2 = x.rearrange("b (m p) d -> p (b m) d", p=P)
    mem2 = mem.rearrange("b (m p) d -> p (b m) d", p=P)
    out2 = out.rearrange("b (m p) d -> p (b m) d", p=P)
    rows_d = nc.dram_tensor("rows_scratch", (40, S), F32, kind="Internal").ap()
    mkv_d = nc.dram_tensor("mkv_scratch", (S, 2048), F32, kind="Internal").ap()
    rel_d = nc.dram_tensor("rel_scratch", (A_H, BIASW), F32, kind="Internal").ap()

    with ExitStack() as ctx:
        def sb(name, shape, dt=F32):
            return ctx.enter_context(nc.sbuf_tensor(name, shape, dt))

        def sem(name):
            return ctx.enter_context(nc.semaphore(name))

        XH = sb("x_high", [P, KT, S], F32R)
        XL = sb("x_low", [P, KT, S], F32R)
        YH = sb("y_high", [P, KT, S], F32R)
        YL = sb("y_low", [P, KT, S], F32R)
        RAW = sb("w_raw", [P, RING, CH * NBLK])
        WH = sb("w_high", [P, RING, CH * NBLK], F32R)
        WL = sb("w_low", [P, RING, CH * NBLK], F32R)
        RES = sb("residual", [P, M, D])
        PR = sb("proj", [P, M, 4 * NBLK])
        WK = sb("work", [P, 12 * U])
        ident = sb("ident", [P, P])
        ones = sb("ones", [P, P])
        flip = sb("flip", [P, P])
        upper = sb("upper", [P, P])
        strict = sb("strict", [P, P])
        LV = sb("level_masks", [P, 7, P])
        SY = sb("sym_masks", [P, 6, P])
        CW = sb("conv_cols", [P, 4 * 48])
        NC_ = sb("norm_cols", [P, 40])
        GT = sb("gates", [P, M, 48])
        BIA = sb("gate_bias", [P, 48])
        TI = sb("tanh_if", [P, M, 16])
        NA = sb("neg_abs", [P, M, 32])
        LNB = sb("ln_beta", [P, M, 16])
        LG = sb("log_gates", [P, M, 24])
        EA = sb("exp_alog", [P, 16])
        CS = sb("cumsums", [P, M, 24])
        AS = sb("a_cols", [P, ML_H, M])
        EMT = sb("exp_neg_m", [P, ML_H, M])
        GAM = sb("gamma_cols", [P, DN_H, M])
        EG = sb("exp_gamma", [P, DN_H, M])
        NEB = sb("neg_beta_exp_gamma", [P, DN_H, M])
        HB = sb("half_beta", [P, DN_H, M])
        KD = sb("key_end_decay", [P, DN_H])
        RS = sb("row_sources", [P, M, 40])
        RT = sb("rows", [40, S])
        MT = sb("cummax", [40, S])
        ST = sb("stats", [P, 64])
        BN = sb("bn_stats", [P, M, 4, 6])
        LR = sb("low_rank", [P, M, 17])
        LRT, GW = MT[0:17, :], RT[0:17, :]
        SP_ = ctx.enter_context(nc.psum_tensor("stream_psum", [P, 4, NBLK], F32))
        H = ctx.enter_context(nc.psum_tensor("heads_psum", [P, 4, NBLK], F32))

        EPSC = sb("eps_consts", [P, 5])
        eps_c, eps16_c, eps512_c, eps4_c, epsln_c = [EPSC[:, i:i + 1] for i in range(5)]

        def wk(u, n=U):
            return WK[:, int(u * U):int(u * U) + n]

        loaded = [sem(f"chunk_loaded{i}") for i in range(RING)]
        hi_done, lo_done, used, evac = sem("w_high_done"), sem("w_low_done"), sem("chunk_used"), sem("block_evacuated")
        consts, small_in, mem_in, x_in = sem("consts"), sem("small_in"), sem("mem_in"), sem("x_in")
        cols_pe, cols_v = sem("cols_transposed"), sem("cols_copied")
        m_pe = sem("mem_transposed")
        x_pe, x_hi, x_lo = sem("x_transposed"), sem("x_high_done"), sem("x_low_done")
        out_pe, out_hi, out_lo = sem("y_transposed"), sem("y_high_done"), sem("y_low_done")
        m_hi, m_lo = out_hi, out_lo
        mkv_out = [sem(f"mkv_block{b}_stored") for b in range(4)]
        rows_out, rows_in, kv_in = sem("rows_stored"), sem("rows_loaded"), sem("kv_loaded")
        rel_in, rel_s, rel_st, rel_bw, rel_m = [sem(n) for n in ("rel_in", "rel_reversed", "rel_stored", "rel_loaded", "rel_masked")]
        lw_in, gw_in, fin_out = sem("ln_rows_in"), sem("gate_w_in"), sem("out_stored")
        passed = sem("waits_passed")
        g_tanh, norm_s = sem("gates_tanh"), sem("norm_act")

        G_PE = steps_of(sem("gates_pe"), ["cumsum", "rows", "negm"])
        W_GATE, W_LR = 4 * 48, 4 * 16
        G_ACT = steps_of(sem("gates_act"), ["mini0", "mini1", "tanh", "expf", "lnf", "expab", "lnab", "alog", "eg", "eb",
                                         "hb", "kd", "emt"])
        G_V = steps_of(sem("gates_dve"), ["bias_if", "bias_a", "negabs", "lnb", "sp", "g", "cs0", "cs1", "as", "gam", "rs0",
                                       "rs1", "rs2", "kd", "rt", "scan", "negm", "ems", "neb", "hb"])
        ML_PE = steps_of(sem("ml_pe"), ["q", "k", "scores", "pv", "out0", "out1"])
        ML_ACT = steps_of(sem("ml_act"), ["to", "tz", "q", "k", "expw", "sq", "ln", "exp"])
        ML_V = steps_of(sem("ml_dve"), ["arg", "g1", "g2", "mask", "p", "den0", "den", "rden", "h", "ss", "fr", "fg"])
        LVS = range(1, 7)
        DN_PE = steps_of(sem("dn_pe"), ["q", "k", "v", "ssq", "ssk", "vt0", "vt1", "k0t", "kk0", "kk1", "qk0", "qk1", "x0"]
                      + [f"{n}{l}{p}" for l in LVS for n in "xt" for p in (0, 1)]
                      + ["u0", "s1", "o0", "qs", "ks", "u1", "o1", "out0", "out1"])
        DN_ACT = steps_of(sem("dn_act"), ["tz", "tq", "decay", "tk", "sqq", "tv", "sqk", "lnq", "lnk", "expq", "expk"]
                       + [f"x{l}{p}" for l in LVS for p in (0, 1)]
                       + ["u0", "s1", "f0", "u1", "sq", "ln", "exp"])

        def conv_names(c):
            return [f"conv{c}{j}{h}" for p in (0, 1) for j in range(4) for h in (2 * p, 2 * p + 1)]

        DN_V = steps_of(sem("dn_dve"), ["g"] + conv_names(0) + ["subr", "subg"] + conv_names(1) + ["silu0", "maskr", "maskg"]
                     + conv_names(2) + ["silu1", "silu2", "nq", "nk", "v0", "v1", "ke", "at0", "at1", "qkt0", "qkt1",
                                        "ut0", "tt0", "ut1", "t0"]
                     + [n for l in LVS for n in ([f"ut{l + 1}"] if l < 6 else [])
                        + [f"{k}{l}{p}" for p in (0, 1) for k in (("t", "tt") if l < 6 else ("tt",))]]
                     + ["f1a", "r0", "r1", "r2", "r3", "f1b", "ss", "fr", "fg"])
        AT_PE = {k: steps_of(sem(f"{k}_pe"), ["k", "q", "scores", "pt", "pv", "out0", "out1"]) for k in "am"}
        AT_ACT = {k: steps_of(sem(f"{k}_act"), ["tz", "q", "exp", "pt"]) for k in "am"}
        AT_V = {k: steps_of(sem(f"{k}_dve"), ["k", "g", "max0", "max1", "neg", "pt", "rs", "f", "fg"]) for k in "am"}
        GL_PE = steps_of(sem("gla_pe"), ["q", "k", "lrt", "logit", "b", "d"] + [f"l{l}" for l in range(1, 9)] + ["pv", "out0", "out1"])
        GL_ACT = steps_of(sem("gla_act"), ["mini0", "mini1", "tz", "q", "k", "lrt", "absx", "expx", "lnx", "b"] + [f"e{l}" for l in range(1, 9)]
                       + ["at8", "f", "sq", "ln", "exp"])
        GL_V = steps_of(sem("gla_dve"), ["zero", "g", "lg", "cp00", "cp01"]
                     + [n for l in range(1, 9) for n in (f"d{l}", f"qe{l}") + ((f"cp{l}0", f"cp{l}1") if l < 8 else ())]
                     + ["ss", "fr", "fg"])
        LN_V = steps_of(sem("ln_dve"), [f"st{m}{n}" for n in range(4) for m in range(M)] + [f"ag{m}" for m in range(M)]
                     + [f"{n}{m}" for m in range(M) for n in ("xm", "xg")])
        x_tok, eps_ready, evac_tmp = sem("layer_input_ready"), sem("eps_ready"), sem("gated_product")

        N_MEM = 0
        N_GATE = N_MEM + 4 * NCH
        N_ML = N_GATE + RING
        N_GA = N_ML + 16 * NCH
        N_YA = N_GA + 4 * NCH
        N_DN = N_YA + 4 * NCH
        N_GB = N_DN + 16 * NCH
        N_YB = N_GB + 4 * NCH
        N_L = N_YB + 4 * NCH
        LSZ = 17 * NCH + RING
        L_LR, L_M, L_B, L_A0, L_A1, L_Y = 0, RING, RING + 2 * NCH, RING + 5 * NCH, RING + 9 * NCH, RING + 13 * NCH
        E_MEM, E_ML, E_GA, E_YA, E_DN, E_GB, E_YB, E_L = 0, 4, 20, 24, 28, 44, 48, 52
        EX_GATE, EX_LR = 48, 16

        def load_count(n, c, extra):
            return n * 4 + (16 * (c // RING) + 16 + extra)

        N_CONSTS = 9 + 3 * (7 + 2 * 6)

        block = ctx.enter_context(nc.Block())

        def wait_alone(eng, sem, value):
            eng.wait_ge(sem, value)
            eng.sem_inc(passed, 1)

        @block.sync
        def _(sp):
            def put(n, c, src, first=False):
                if not (isinstance(n, int) and n + c < RING):
                    wait_alone(sp, lo_done, n + (c - RING + 1))
                sp.dma_start(RAW[:, c % RING, :], src).then_inc(loaded[c % RING], 16)

            def rows_in_chunk(w, off, width, c, cols):
                return bass.AP(w.tensor, off + c * 256 * width, [[width, 256]] + cols)

            def group(n, w, off, width, blocks):
                for b, cols in enumerate(blocks):
                    for c in range(NCH):
                        put(n, b * NCH + c, rows_in_chunk(w, cols[0] + off, width, c, cols[1]))

            def wide(o):
                return (o, [[1, NBLK]])

            def out_group(n, w, off):
                for b in range(4):
                    for c in range(NCH):
                        put(n, b * NCH + c, bass.AP(w.tensor, off + (c * 256 * D + b * NBLK), [[D, P], [P * D, 2], [1, NBLK]]))

            def narrow(n, w, off, width, parts):
                for i in range(RING):
                    wait_alone(sp, lo_done, n + (i - RING + 1))
                    total = sum(k for _, k in parts)
                    dst = RAW[:, i, 0:4 * total].rearrange("p (c j n) -> p c j n", c=2, j=2)
                    for cc in range(2):
                        at = 0
                        for o, k in parts:
                            sp.dma_start(dst[:, cc, :, at:at + k],
                                         bass.AP(w.tensor, off + (o + (2 * i + cc) * 256 * width), [[2 * width, P], [width, 2], [1, k]])
                                         ).then_inc(loaded[i], 16)
                            at += k

            sp.dma_start(PR[:], mem2).then_inc(mem_in, 16)
            for l in range(2):
                for half in range(2):
                    for c in range(NCH):
                        put(N_MEM, (2 * l + half) * NCH + c, rows_in_chunk(w_mkv, l * D * 1024 + half * NBLK, 1024, c, [[1, NBLK]]))
            narrow(N_GATE, w_in, 0, IN1, [(C_IF, 16), (C_BA, 32)])
            with sp.Fori(0, 4) as g:
                group(N_ML + g * (4 * NCH), w_in, g * 256, IN1, [(C_MLQ, [[C_MLK - C_MLQ, 2], [1, 256]])])
                for b, o in ((1, C_MLO), (2, C_MLZ), (3, C_MLV)):
                    for c in range(NCH):
                        put(N_ML + g * (4 * NCH), b * NCH + c, rows_in_chunk(w_in, g * NBLK + o, IN1, c, [[1, NBLK]]))
            group(N_GA, w_in, 0, IN1, [wide(C_GA + b * NBLK) for b in range(4)])
            out_group(N_YA, w_out, 0)
            with sp.Fori(0, 4) as g:
                group(N_DN + g * (4 * NCH), w_in, g * NBLK, IN1,
                      [wide(C_DN), wide(C_DN + 2048), wide(C_DN + 4096), wide(C_DNZ)])
            group(N_GB, w_in, 0, IN1, [wide(C_GB + b * NBLK) for b in range(4)])
            out_group(N_YB, w_out, D * D)
            with sp.Fori(0, 2) as l:
                n = N_L + l * LSZ
                off = l * (D * IN2)
                narrow(n + L_LR, w_in2, off, IN2, [(C_LR, 16)])
                group(n + L_M, w_in2, off, IN2, [wide(C_MQ), wide(C_MZ)])
                group(n + L_B, w_in2, off, IN2, [wide(C_BQ), wide(C_BZ), wide(C_BV)])
                group(n + L_A0, w_in2, off, IN2, [wide(o) for o in (C_AQ, C_AK, C_AV, C_AZ)])
                group(n + L_A1, w_in2, off, IN2, [wide(o + NBLK) for o in (C_AQ, C_AK, C_AV, C_AZ)])
                out_group(n + L_Y, w_out2, l * (D * D))

        @block.gpsimd
        def _(pool):
            k = [0]

            def c(ins):
                k[0] += 1
                ins.then_inc(consts, 1)
                pool.wait_ge(consts, k[0])

            c(pool.memset(ident[:], 0.0))
            c(pool.affine_select(out=ident[:], in_=ident[:], compare_op=ALU.not_equal, fill=1.0, base=0,
                                 pattern=[[-1, P]], channel_multiplier=1))
            pool.dma_start(wk(8, 256)[0:8, :], norm_w.rearrange("a (c n) -> (a c) n", n=256)).then_inc(small_in, 16)
            pool.dma_start(wk(8.25, P)[0:16, :], ml_norm_w.rearrange("a (c n) -> (a c) n", n=P)).then_inc(small_in, 16)
            pool.dma_start(wk(8.5, P)[0:1, :], dn_norm_w).then_inc(small_in, 16)
            pool.dma_start(wk(8.75, P)[0:2, :], gla_g).then_inc(small_in, 16)
            for i in range(2):
                pool.dma_start(wk(9 + i / 8, P)[0:96, :], bass.AP(dn_conv_w.tensor, i * 2 * 6144, [[P, 96], [1, P]])).then_inc(small_in, 16)
            for o, t, n in ((0, ml_i_bias, 8), (8, ml_f_bias, 8), (16, dn_dt_bias, 16), (32, dn_a_log, 16)):
                pool.dma_start(BIA[:, o:o + n], bass.AP(t.tensor, 0, [[0, P], [1, n]])).then_inc(small_in, 16)
            c(pool.memset(ones[:], 1.0))
            c(pool.memset(flip[:], 0.0))
            c(pool.affine_select(out=flip[:], in_=flip[:], compare_op=ALU.not_equal, fill=1.0, base=1 - P,
                                 pattern=[[1, P]], channel_multiplier=1))
            c(pool.affine_select(out=upper[:], in_=ones[:], compare_op=ALU.is_ge, fill=0.0, base=0,
                                 pattern=[[1, P]], channel_multiplier=-1))
            c(pool.affine_select(out=strict[:], in_=ones[:], compare_op=ALU.is_gt, fill=0.0, base=0,
                                 pattern=[[1, P]], channel_multiplier=-1))
            c(pool.memset(LV[:], 0.0))
            c(pool.memset(SY[:], 0.0))

            def half_mask(m, l, right, rows_right):
                size, hf = 2 ** (l + 1), 2 ** l
                v = m.rearrange("p (n s h) -> p n s h", s=2, h=hf)[:, :, 1 if right else 0, :]
                lo = hf if rows_right else 0
                c(pool.memset(v, 1.0))
                c(pool.affine_select(out=v, in_=v, compare_op=ALU.is_ge, fill=0.0, base=-lo,
                                     pattern=[[-size, P // size], [0, hf]], channel_multiplier=1))
                c(pool.affine_select(out=v, in_=v, compare_op=ALU.is_ge, fill=0.0, base=lo + hf - 1,
                                     pattern=[[size, P // size], [0, hf]], channel_multiplier=-1))

            for l in range(7):
                half_mask(LV[:, l, :], l, True, False)
            for l in range(6):
                half_mask(SY[:, l, :], l, True, False)
                half_mask(SY[:, l, :], l, False, True)

            assert k[0] == N_CONSTS

            for b in range(4):
                pool.wait_ge(evac, 2 * (E_MEM + b) + 2)
                pool.dma_start(mkv_d.rearrange("(m p) n -> p m n", p=P)[:, :, b * NBLK:(b + 1) * NBLK],
                               PR[:, :, b * NBLK:(b + 1) * NBLK]).then_inc(mkv_out[b], 16)
            pool.wait_ge(*done(G_V, "negm"))
            pool.dma_start(rows_d, RT[:, :]).then_inc(rows_out, 16)
            pool.wait_ge(rows_out, 16)

            def ml_rows(g):
                pool.dma_start(wk(1, 2 * S), bass.AP(rows_d.tensor, g * (2 * S) + 32 * S, [[0, P], [1, 2 * S]])).then_inc(rows_in, 16)

            def dn_rows(g):
                for i in range(2):
                    pool.dma_start(wk(4 + i), bass.AP(rows_d.tensor, g * (4 * S) + i * 16 * S, [[0, P], [1, 4 * S]])).then_inc(rows_in, 16)

            ml_rows(0)
            with pool.Fori(1, 4) as g:
                wait_alone(pool, *done(ML_V, "arg", g - 1))
                ml_rows(g)
            pool.wait_ge(out_lo, NCH + 16)
            pool.wait_ge(out_hi, NCH + 16)
            dn_rows(0)
            with pool.Fori(1, 4) as g:
                wait_alone(pool, *done(DN_PE, "o1", g - 1))
                wait_alone(pool, *done(DN_V, "ut6", g - 1))
                dn_rows(g)
            pool.wait_ge(out_lo, NCH + 32)
            pool.wait_ge(out_hi, NCH + 32)
            pool.dma_start(wk(0, D), bass.AP(final_norm_w.tensor, 0, [[0, P], [1, D]])).then_inc(lw_in, 16)

            with pool.Fori(0, 2) as l:
                pool.dma_start(wk(9, 2 * U).rearrange("p (m n) -> p m n", m=M),
                               mkv_d.rearrange("(m p) n -> p m n", p=P)[:, :, bass.ds(l * 1024, 1024)]).then_inc(kv_in, 16)
                pool.dma_start(RT[0:16, :], bass.AP(gate_w.tensor, l * (16 * S), [[S, 16], [1, S]])).then_inc(gw_in, 16)
                pool.dma_start(RT[16:17, :], bass.AP(gate_b.tensor, l * S, [[S, 1], [1, S]])).then_inc(gw_in, 16)
                pool.dma_start(wk(6, 257)[0:8, :], bass.AP(rel.tensor, l * (8 * 257), [[257, 8], [1, 257]])).then_inc(rel_in, 16)
                wait_alone(pool, rel_s, l * 2 + 2)
                pool.dma_start(rel_d, wk(6.5, BIASW)[0:8, :]).then_inc(rel_st, 16)
                pool.wait_ge(rel_st, l * 16 + 16)
                wait_alone(pool, out_lo, NCH + (l * 16 + 36))
                wait_alone(pool, out_hi, NCH + (l * 16 + 36))
                pool.dma_start(wk(9, 3 * U).rearrange("p (h n) -> p h n", h=A_H)[:, :, P:BIASW],
                               bass.AP(rel_d.tensor, 0, [[1, P], [BIASW, A_H], [1, S]])).then_inc(rel_bw, 16)
                wait_alone(pool, out_lo, NCH + (l * 16 + 48))
                wait_alone(pool, out_hi, NCH + (l * 16 + 48))
                pool.dma_start(wk(0, D), bass.AP(ln_g.tensor, l * D, [[0, P], [1, D]])).then_inc(lw_in, 16)
                pool.dma_start(wk(2, D), bass.AP(ln_b.tensor, l * D, [[0, P], [1, D]])).then_inc(lw_in, 16)
            pool.wait_ge(x_tok, 3)
            pool.dma_start(out2, RES[:]).then_inc(fin_out, 16)
            pool.wait_ge(fin_out, 16)

        def gap(n):
            for _ in range(n):
                yield

        def advance(side, n=1):
            for _ in range(n):
                next(side, None)

        def finish(side):
            for _ in side:
                pass

        def none():
            return iter(())

        def bank(i, n=1):
            return H[:, i:i + n, :].rearrange("p b n -> p (b n)")

        def cols(ap, n):
            return ap.unsqueeze(len(ap.shape)).broadcast_to(list(ap.shape) + [n])

        def over(ap, k):
            return ap.unsqueeze(1).broadcast_to([ap.shape[0], k, ap.shape[1]])

        def sl(i, n=P):
            return slice(i * n, (i + 1) * n)

        def after_side(eng, q):
            if not (isinstance(q, int) and q == 0):
                eng.wait_ge(out_hi, NCH + 4 * q)
                eng.wait_ge(out_lo, NCH + 4 * q)

        @block.tensor
        def _(pe):
            def tr(dst, src, n=P, b0=0):
                return pe.transpose(dst, src, ident[b0:b0 + n, b0:b0 + n])

            def stream(n, blocks_before, nblk, hi, lo, side, first_need=None):
                for b in range(nblk):
                    need = 2 * (blocks_before + b - 1) if first_need is None or b else 2 * first_need
                    if not (isinstance(need, int) and need <= 0):
                        pe.wait_ge(evac, need)
                    pair = 2 * (b % 2)
                    for c in range(NCH):
                        i = b * NCH + c
                        pe.wait_ge(lo_done, n + (i + 1))
                        for kk in range(CH):
                            k = c * CH + kk
                            w, wl = WH[:, i % RING, sl(kk, NBLK)], WL[:, i % RING, sl(kk, NBLK)]
                            for m in range(M):
                                acc = SP_[:, pair + m, :]
                                pe.matmul(acc, hi[:, k, sl(m)], w, start=(k == 0), stop=False)
                                pe.matmul(acc, hi[:, k, sl(m)], wl, start=False, stop=False)
                                last = pe.matmul(acc, lo[:, k, sl(m)], w, start=False, stop=(k == KT - 1))
                            if kk == CH - 1:
                                last.then_inc(used, 1)
                            advance(side)
                finish(side)

            def small_block(n, width):
                for i in range(RING):
                    pe.wait_ge(lo_done, n + (i + 1))
                    for m in range(M):
                        acc = H[:, m, 0:width]
                        for t in range(4):
                            k = 4 * i + t
                            w, wl = WH[:, i, sl(t, width)], WL[:, i, sl(t, width)]
                            pe.matmul(acc, XH[:, k, sl(m)], w, start=(k == 0), stop=False)
                            pe.matmul(acc, XH[:, k, sl(m)], wl, start=False, stop=False)
                            last = pe.matmul(acc, XL[:, k, sl(m)], w, start=False, stop=(k == KT - 1))
                    last.then_inc(used, 1)

            def feature_tiles(src, count, done, before):
                for c in range(NCH):
                    if c >= 4:
                        pe.wait_ge(count[0], count[1] * (c - 3) + before)
                    v = src[:, :, sl(c, 2 * P)].rearrange("p m (q j) -> p m q j", j=2)
                    for j in range(2):
                        for m in range(M):
                            last = tr(H[:, c % 4, j * S + m * P:j * S + (m + 1) * P], v[:, m, :, j])
                    last.then_inc(done, 1)
                    yield

            def x_prep():
                pe.wait_ge(small_in, 16 * 10)
                pe.wait_ge(m_lo, NCH)
                for i in range(2):
                    tr(H[:, 0, sl(i, 96)], wk(9 + i / 8, P)[0:96, :], 96)
                for j in range(2):
                    tr(H[:, 0, 192 + 8 * j:200 + 8 * j], wk(8, 256)[0:8, :].rearrange("c (q j) -> c q j", j=2)[:, :, j], 8)
                tr(H[:, 0, 208:224], wk(8.25, P)[0:16, :], 16)
                tr(H[:, 0, 224:225], wk(8.5, P)[0:1, :], 1)
                tr(H[:, 0, 226:228], wk(8.75, P)[0:2, :], 2).then_inc(cols_pe, 1)
                yield from gap(12)
                pe.wait_ge(cols_v, 5)
                pe.wait_ge(norm_s, 5)
                yield from feature_tiles(wk(0, 4 * U).rearrange("p (m d) -> p m d", m=M), (x_lo, 2), x_pe, 0)

            def gates():
                pe.wait_ge(*done(G_V, "g"))
                for z, w, first in ((0, LG[:, 0, :], True), (40, LG[:, 1, 8:24], True)):
                    pe.matmul(H[:, 2, z:z + w.shape[1]], upper[:], w, start=True, stop=True)
                pe.matmul(H[:, 2, 32:40], upper[:], LG[:, 1, 0:8], start=True, stop=False)
                pe.matmul(H[:, 2, 32:40], ones[:], LG[:, 0, 0:8], start=False, stop=True)
                pe.matmul(H[:, 2, 64:80], ones[:], LG[:, 0, 8:24], start=True, stop=True).then_inc(*signal(G_PE, "cumsum"))
                yield from gap(4)
                pe.wait_ge(*done(G_V, "rs2"))
                for m in range(M):
                    last = tr(H[0:40, 3, sl(m)], RS[:, m, :])
                last.then_inc(*signal(G_PE, "rows"))
                yield from gap(4)
                pe.wait_ge(*done(G_V, "negm"))
                for m in range(M):
                    last = tr(H[:, 0, 8 * m:8 * m + 8], RT[32:40, sl(m)], 8, 32)
                last.then_inc(*signal(G_PE, "negm"))
                yield

            def outputs(steps, fin, F, b0):
                pe.wait_ge(*fin)
                for j in range(4):
                    for m in range(M):
                        last = tr(H[:, b0 + j // 2, (j % 2) * S + m * P:(j % 2) * S + (m + 1) * P], F[:, m, sl(j)])
                    if j % 2:
                        last.then_inc(*signal(steps, f"out{j // 2}"))
                yield

            def ml(g):
                after_side(pe, g)
                pe.wait_ge(evac, 8 * g + (2 * (E_ML + 4)))
                for i, n in enumerate("qk"):
                    for h in range(2):
                        for m in range(M):
                            last = tr(H[:, i, h * S + m * P:h * S + (m + 1) * P], PR[:, m, i * S + h * P:i * S + (h + 1) * P])
                    last.then_inc(*signal(ML_PE, n))
                yield from gap(3)
                q, k, w, F = wk(0, 512), wk(0.5, 512), wk(2, 768), wk(10)
                pe.wait_ge(*done(ML_ACT, "k", g))
                for h in range(2):
                    pe.matmul(H[:, 2 + h, 0:S], k[:, h * S:h * S + P], q[:, sl(h, S)], start=True, stop=True)
                    last = pe.matmul(H[:, 2 + h, S:S + P], k[:, h * S + P:(h + 1) * S], q[:, h * S + P:(h + 1) * S], start=True, stop=True)
                last.then_inc(*signal(ML_PE, "scores"))
                yield from gap(4)
                pe.wait_ge(*done(ML_V, "p", g))
                for h in range(2):
                    for m in range(M):
                        for s in range(m + 1):
                            pt = w[:, h * 384 + s * S + (m - s) * P:h * 384 + s * S + (m - s + 1) * P]
                            pe.matmul(H[:, h, sl(m, S)], pt, PR[:, s, 3 * NBLK + h * S:3 * NBLK + (h + 1) * S], start=(s == 0), stop=(s == m))
                        for s in range(m + 1):
                            pt = w[:, h * 384 + s * S + (m - s) * P:h * 384 + s * S + (m - s + 1) * P]
                            last = pe.matmul(H[:, 2, 2 * h + m:2 * h + m + 1], pt, ones[:, 0:1], start=(s == 0), stop=(s == m))
                last.then_inc(*signal(ML_PE, "pv"))
                yield from gap(8)
                yield from outputs(ML_PE, done(ML_V, "fg", g), F.rearrange("p (m n) -> p m n", m=M), 0)

            def dn(g):
                after_side(pe, g + 4)
                pe.wait_ge(evac, 8 * g + (2 * (E_DN + 4)))
                CV = wk(0, 3 * U).rearrange("p (c h t) -> p c h t", c=3, h=4)
                QKd = wk(4).rearrange("p (h m t) -> p h m t", h=4, m=M)
                T = wk(6).rearrange("p (h m t) -> p h m t", h=4, m=M)
                TT = wk(7).rearrange("p (h m t) -> p h m t", h=4, m=M)
                UT = wk(8).rearrange("p (h m t) -> p h m t", h=4, m=M)
                X = wk(3).rearrange("p (h m t) -> p h m t", h=4, m=M)
                V = wk(2).rearrange("p (h m t) -> p h m t", h=4, m=M)
                KE = wk(11, 512).rearrange("p (h t) -> p h t", h=4)
                S1 = wk(11.5, 512).rearrange("p (h t) -> p h t", h=4)

                def project(c, b0):
                    for h in range(4):
                        for m in range(M):
                            last = tr(H[:, b0 + h // 2, (h % 2) * S + m * P:(h % 2) * S + (m + 1) * P], PR[:, m, c * NBLK + h * P:c * NBLK + (h + 1) * P])
                    return last

                project(0, 0).then_inc(*signal(DN_PE, "q"))
                yield
                project(1, 2).then_inc(*signal(DN_PE, "k"))
                yield from gap(4)
                pe.wait_ge(*done(DN_V, "conv033", g))
                project(2, 0).then_inc(*signal(DN_PE, "v"))
                yield from gap(4)
                pe.wait_ge(*done(DN_ACT, "sqq", g))
                for i in range(2):
                    last = pe.matmul(H[:, 2 + i, :], ones[:], wk(6 + i / 2, 512), start=True, stop=True)
                last.then_inc(*signal(DN_PE, "ssq"))
                yield from gap(5)
                pe.wait_ge(*done(DN_ACT, "sqk", g))
                for i in range(2):
                    last = pe.matmul(H[:, i, :], ones[:], wk(7 + i / 2, 512), start=True, stop=True)
                last.then_inc(*signal(DN_PE, "ssk"))
                yield
                pe.wait_ge(*done(DN_V, "silu2", g))
                pe.wait_ge(*done(DN_ACT, "lnq", g))
                for p in range(2):
                    for h in (0, 1):
                        for m in range(M):
                            last = tr(H[:, 2 + p, sl(2 * h + m)], CV[:, 2, 2 * p + h, sl(m)])
                    last.then_inc(*signal(DN_PE, f"vt{p}"))
                yield from gap(2)
                pe.wait_ge(*done(DN_V, "nk", g))
                for h in range(4):
                    last = tr(H[:, 1, sl(h)], CV[:, 1, h, 0:P])
                last.then_inc(*signal(DN_PE, "k0t"))
                yield
                pe.wait_ge(*done(DN_V, "ke", g))
                for i, n in enumerate(("kk", "qk")):
                    for p in range(2):
                        for h in (0, 1):
                            for m in range(M):
                                last = pe.matmul(H[:, 2 * i + p, sl(2 * h + m)], CV[:, 1, 2 * p + h, sl(m)],
                                                 CV[:, 1 - i, 2 * p + h, sl(m)], start=True, stop=True)
                        last.then_inc(*signal(DN_PE, f"{n}{p}"))
                    yield
                yield
                pe.wait_ge(*done(DN_V, "at1", g))
                pe.wait_ge(*done(DN_V, "ut0", g))
                for i in range(8):
                    last = tr(H[:, i // 4, sl(i % 4)], UT[:, i // 2, i % 2, :])
                last.then_inc(*signal(DN_PE, "x0"))
                yield from gap(1)
                for l in LVS:
                    for p in range(2):
                        pe.wait_ge(*(done(DN_V, "t0", g) if l == 1 else done(DN_V, f"tt{l - 1}{p}", g)))
                        pe.wait_ge(*done(DN_V, f"ut{l}", g))
                        for i in range(4 * p, 4 * p + 4):
                            last = pe.matmul(H[:, p, sl(i % 4)], UT[:, i // 2, i % 2, :], T[:, i // 2, i % 2, :], start=True, stop=True)
                        last.then_inc(*signal(DN_PE, f"x{l}{p}"))
                    yield
                    for p in range(2):
                        pe.wait_ge(*done(DN_ACT, f"x{l}{p}", g))
                        for i in range(4 * p, 4 * p + 4):
                            h, m = i // 2, i % 2
                            if l < 6:
                                pe.matmul(H[:, p, sl(i % 4)], TT[:, h, m, :], X[:, h, m, :], start=True, stop=True)
                            last = pe.matmul(H[:, 2 + p, sl(i % 4)], X[:, h, m, :], TT[:, h, m, :], start=True, stop=True)
                        last.then_inc(*signal(DN_PE, f"t{l}{p}"))
                    yield
                pe.wait_ge(*done(DN_V, "tt61", g))
                for h in range(4):
                    last = pe.matmul(H[:, 0, sl(h)], TT[:, h, 0, :], V[:, h, 0, :], start=True, stop=True)
                last.then_inc(*signal(DN_PE, "u0"))
                yield
                pe.wait_ge(*done(DN_ACT, "u0", g))
                for h in range(4):
                    last = pe.matmul(H[:, 1, sl(h)], KE[:, h, :], UT[:, h, 0, :], start=True, stop=True)
                last.then_inc(*signal(DN_PE, "s1"))
                for h in range(4):
                    last = pe.matmul(H[:, 0, sl(h)], QKd[:, h, 0, :], UT[:, h, 0, :], start=True, stop=True)
                last.then_inc(*signal(DN_PE, "o0"))
                yield
                pe.wait_ge(*done(DN_ACT, "s1", g))
                for c, b, n in ((0, 3, "qs"), (1, 2, "ks")):
                    for h in range(4):
                        last = pe.matmul(H[:, b, sl(h)], CV[:, c, h, P:S], S1[:, h, :], start=True, stop=True)
                    last.then_inc(*signal(DN_PE, n))
                yield
                pe.wait_ge(*done(DN_V, "r3", g))
                for h in range(4):
                    last = pe.matmul(H[:, 1, sl(h)], TT[:, h, 1, :], V[:, h, 1, :], start=True, stop=True)
                last.then_inc(*signal(DN_PE, "u1"))
                yield
                pe.wait_ge(*done(DN_ACT, "u1", g))
                for h in range(4):
                    last = pe.matmul(H[:, 0, sl(h)], QKd[:, h, 1, :], UT[:, h, 1, :], start=True, stop=True)
                last.then_inc(*signal(DN_PE, "o1"))
                yield from gap(5)
                yield from outputs(DN_PE, done(DN_V, "fg", g), wk(10).rearrange("p (m n) -> p m n", m=M), 2)

            def attend(kind, q, n, evac_need, h0=0, rel_need=None):
                steps, act, dve = AT_PE[kind], AT_ACT[kind], AT_V[kind]
                after_side(pe, q)
                pe.wait_ge(evac, evac_need)
                if kind == "m":
                    pe.wait_ge(kv_in, (q - 8) * 4 + 16)
                    ksrc = wk(9, 2 * U).rearrange("p (m n) -> p m n", m=M)
                    vsrc = ksrc[:, :, NBLK:]
                else:
                    ksrc, vsrc = PR[:, :, NBLK:2 * NBLK], PR[:, :, 2 * NBLK:3 * NBLK]
                for name, src, b0 in (("k", ksrc, 0), ("q", PR, 2)):
                    for h in range(4):
                        for m in range(M):
                            last = tr(H[:, b0 + h // 2, (h % 2) * S + m * P:(h % 2) * S + (m + 1) * P], src[:, m, sl(h)])
                    last.then_inc(*signal(steps, name))
                yield from gap(2)
                full = kind == "m"
                w = 512 if full else BIASW
                qT, kT = wk(0), wk(1)
                SC, PT = wk(2, 4 * w), wk(4, 4 * w)
                pe.wait_ge(*done(act, "q", n))
                pe.wait_ge(*done(dve, "k", n))
                if not full:
                    pe.wait_ge(rel_m, rel_need)
                for h in range(4):
                    n0 = S if full else P
                    for m, a, b in ((0, 0, n0), (1, n0, n0 + S)):
                        last = pe.matmul(H[:, h, a:b], qT[:, h * S + m * P:h * S + (m + 1) * P], kT[:, h * S:h * S + b - a], start=True, stop=full)
                        if not full:
                            last = pe.matmul(H[:, h, a:b], flip[:], wk(9, 3 * U)[:, (h0 + h) * BIASW + a:(h0 + h) * BIASW + b], start=False, stop=True)
                last.then_inc(*signal(steps, "scores"))
                yield from gap(6)
                pe.wait_ge(*done(act, "exp", n))
                for h in range(4):
                    if full:
                        for i in range(4):
                            last = tr(H[:, h, sl(i)], SC[:, h * w + i * P:h * w + (i + 1) * P])
                    else:
                        for i in range(3):
                            last = tr(H[:, h, sl(i)], SC[:, h * w + i * P:h * w + (i + 1) * P])
                last.then_inc(*signal(steps, "pt"))
                yield from gap(2)
                pe.wait_ge(*done(act, "pt", n))
                pe.wait_ge(*done(dve, "pt", n))
                parts = {0: ((0, 0), (1, 1)), 1: ((2, 0), (3, 1))} if full else {0: ((0, 0),), 1: ((1, 0), (2, 1))}
                for m in range(M):
                    for h in range(4):
                        for i, (blk, s) in enumerate(parts[m]):
                            last = pe.matmul(H[:, m, sl(h)], PT[:, h * w + blk * P:h * w + (blk + 1) * P], vsrc[:, s, sl(h)],
                                             start=(i == 0), stop=(i == len(parts[m]) - 1))
                last.then_inc(*signal(steps, "pv"))
                yield from gap(3)
                yield from outputs(steps, done(dve, "fg", n), wk(7).rearrange("p (m n) -> p m n", m=M), 2)

            def gla(l, q, evac_need):
                after_side(pe, q)
                pe.wait_ge(evac, evac_need)
                for i, name in enumerate("qk"):
                    for hp in range(2):
                        for m in range(M):
                            last = tr(H[:, i, hp * S + m * P:hp * S + (m + 1) * P], PR[:, m, i * S + hp * P:i * S + (hp + 1) * P])
                    last.then_inc(*signal(GL_PE, name))
                for m in range(M):
                    last = tr(H[0:17, 2, sl(m)], LR[:, m, :])
                last.then_inc(*signal(GL_PE, "lrt"))
                yield from gap(2)
                pe.wait_ge(*done(GL_ACT, "lrt", l))
                pe.wait_ge(gw_in, l * 32 + 32)
                for m in range(M):
                    last = pe.matmul(H[:, 3, sl(m, S)], LRT[:, sl(m)], GW, start=True, stop=True)
                last.then_inc(*signal(GL_PE, "logit"))
                yield from gap(3)
                LGG = wk(3.5, 512).rearrange("p (m n) -> p m n", m=M)
                pe.wait_ge(*done(GL_V, "lg", l))
                for hp in range(2):
                    pe.matmul(H[:, 2, hp * S:hp * S + P], LGG[:, 0, sl(hp)], upper[:], start=True, stop=True)
                    pe.matmul(H[:, 2, hp * S + P:(hp + 1) * S], LGG[:, 0, sl(hp)], ones[:], start=True, stop=False)
                    last = pe.matmul(H[:, 2, hp * S + P:(hp + 1) * S], LGG[:, 1, sl(hp)], upper[:], start=False, stop=True)
                last.then_inc(*signal(GL_PE, "b"))
                yield
                pe.wait_ge(*done(GL_ACT, "k", l))

                def pairs(QK, b, tiles):
                    for par in range(2):
                        for hh in range(2):
                            for i, (ms, mt) in enumerate(tiles):
                                r = slice(64 * par, 64 * par + 64)
                                last = pe.matmul(H[:, b + par, sl(hh * len(tiles) + i)], QK[r, 512 + hh * S + ms * P:512 + hh * S + (ms + 1) * P],
                                                 QK[r, hh * S + mt * P:hh * S + (mt + 1) * P], start=True, stop=True)
                    return last

                diagonal = ((0, 0), (1, 1))
                pairs(wk(0), 0, diagonal).then_inc(*signal(GL_PE, "d"))
                yield from gap(1)
                for lv in range(1, 9):
                    pe.wait_ge(*done(GL_V, f"qe{lv}", l))
                    if lv >= 3:
                        pe.wait_ge(*done(GL_V, f"cp{lv - 2}1", l))
                    elif lv == 2:
                        pe.wait_ge(*done(GL_V, "cp01", l))
                    pairs(wk(1 + lv % 2), 2 * (lv % 2), diagonal if lv < 8 else ((0, 1),)).then_inc(*signal(GL_PE, f"l{lv}"))
                    yield from gap(2)
                A = wk(5, 1536).rearrange("p (c h t) -> p c h t", c=3, h=4)
                pe.wait_ge(*done(GL_V, "cp71", l))
                pe.wait_ge(*done(GL_ACT, "at8", l))
                v = PR[:, :, 3 * NBLK:4 * NBLK]
                for m in range(M):
                    for h in range(4):
                        if m == 0:
                            last = pe.matmul(H[:, 2, sl(h)], A[:, 0, h, :], v[:, 0, sl(h)], start=True, stop=True)
                        else:
                            pe.matmul(H[:, 3, sl(h)], A[:, 2, h, :], v[:, 0, sl(h)], start=True, stop=False)
                            last = pe.matmul(H[:, 3, sl(h)], A[:, 1, h, :], v[:, 1, sl(h)], start=False, stop=True)
                last.then_inc(*signal(GL_PE, "pv"))
                yield from gap(5)
                yield from outputs(GL_PE, done(GL_V, "fg", l), wk(7).rearrange("p (m n) -> p m n", m=M), 0)

            pe.wait_ge(mem_in, 16)
            pe.wait_ge(consts, 2)
            finish(feature_tiles(PR, (m_lo, 1), m_pe, 0))
            pe.wait_ge(m_lo, NCH)
            pe.wait_ge(consts, N_CONSTS)
            stream(N_MEM, E_MEM, 4, YH, YL, x_prep())
            pe.wait_ge(x_lo, 16)
            small_block(N_GATE, 48)
            stream(N_ML, E_ML, 4, XH, XL, gates())
            with pe.Fori(1, 4) as g:
                stream(N_ML + g * (4 * NCH), E_ML + 4 * g, 4, XH, XL, ml(g - 1))
            stream(N_GA, E_GA, 4, XH, XL, ml(3))
            pe.wait_ge(out_lo, NCH + 16)
            stream(N_YA, E_YA, 4, YH, YL, none())
            stream(N_DN, E_DN, 4, XH, XL, none())
            with pe.Fori(1, 4) as g:
                stream(N_DN + g * (4 * NCH), E_DN + 4 * g, 4, XH, XL, dn(g - 1))
            stream(N_GB, E_GB, 4, XH, XL, dn(3))
            pe.wait_ge(out_lo, NCH + 32)
            stream(N_YB, E_YB, 4, YH, YL, none())
            with pe.Fori(0, 2) as l:
                n, e, q = N_L + l * LSZ, E_L + l * 17, 8 + 4 * l
                pe.wait_ge(x_tok, l + 1)
                pe.wait_ge(out_lo, NCH + 4 * q)
                finish(feature_tiles(RES, (x_lo, 2), x_pe, 16 * l + 16))
                pe.wait_ge(x_lo, 16 * l + 32)
                small_block(n + L_LR, 16)
                stream(n + L_M, e, 2, XH, XL, none(), first_need=e)
                stream(n + L_B, e + 2, 3, XH, XL, attend("m", q, l, 2 * (e + 2)))
                stream(n + L_A0, e + 5, 4, XH, XL, gla(l, q + 1, 2 * (e + 5)), first_need=e + 5)
                stream(n + L_A1, e + 9, 4, XH, XL, attend("a", q + 2, 2 * l, 2 * (e + 9), 0, l * 3 + 3))
                finish(attend("a", q + 3, 2 * l + 1, 2 * (e + 13), 4, l * 3 + 3))
                pe.wait_ge(out_lo, NCH + (4 * q + 16))
                stream(n + L_Y, e + 13, 4, YH, YL, none())

        @block.scalar
        def _(act):
            def f(dst, src, func, **kw):
                return act.activation(dst, src, func, **kw)

            def high(n, c, extra, width=CH * NBLK):
                act.wait_ge(loaded[c % RING], load_count(n, c, extra))
                if not (isinstance(n, int) and n + c < RING):
                    act.wait_ge(used, n + (c - RING + 1))
                f(WH[:, c % RING, 0:width], RAW[:, c % RING, 0:width], ACT.Copy).then_inc(hi_done, 1)

            def stream(n, nblk, extra, side, slots=(0, 1, 2, 3), free=(), ahead=(CH * NBLK, 0)):
                for b in range(nblk):
                    for c in range(NCH):
                        i = b * NCH + c + AHEAD
                        if i < nblk * NCH:
                            high(n, i, extra)
                        elif ahead:
                            high(n, i, extra + ahead[1], ahead[0])
                        advance(side, 2)
                    if slots is None:
                        continue
                    if b < len(free):
                        for w in free[b]:
                            act.wait_ge(*w)
                    act.wait_ge(used, n + (b + 1) * NCH)
                    for m in range(M):
                        f(PR[:, m, sl(slots[b], NBLK)], SP_[:, 2 * (b % 2) + m, :], ACT.Copy).then_inc(evac, 1)
                finish(side)

            def small_block(n, extra, width, steps, dst, own):
                for i in range(AHEAD, RING):
                    high(n, i, extra + own, 4 * width)
                for i in range(AHEAD):
                    high(n, RING + i, extra + own)
                act.wait_ge(used, n + RING)
                for m in range(M):
                    f(dst[:, m, 0:width], H[:, m, 0:width], ACT.Copy).then_inc(*signal(steps, f"mini{m}"))

            def x_prep():
                act.wait_ge(m_lo, NCH)
                act.wait_ge(x_in, 16)
                for m in range(M):
                    f(wk(4, D), RES[:, m, :], ACT.Square, accum_out=ST[:, m:m + 1]).then_inc(norm_s, 1)
                    act.wait_ge(norm_s, m + 1)
                yield
                f(ST[:, 2:4], ST[:, 0:2], ACT.Ln, scale=1.0 / D, bias=eps_c).then_inc(norm_s, 1)
                act.wait_ge(norm_s, 3)
                f(ST[:, 4:6], ST[:, 2:4], ACT.Exp, scale=-0.5).then_inc(norm_s, 1)
                act.wait_ge(norm_s, 4)
                yield from gap(2)
                act.wait_ge(cols_v, 5)
                for m in range(M):
                    last = f(wk(2 * m, D), RES[:, m, :], ACT.Copy, scale=ST[:, 4 + m:5 + m])
                last.then_inc(norm_s, 1)
                yield from gap(8)
                for c in range(NCH):
                    act.wait_ge(x_pe, c + 1)
                    for j in range(2):
                        k = 2 * c + j
                        f(XH[:, k, :], H[:, c % 4, sl(j, S)], ACT.Copy, scale=NC_[:, k:k + 1]).then_inc(x_hi, 1)
                    yield

            def gates():
                act.wait_ge(*done(G_V, "bias_if"))
                f(TI[:], GT[:, :, 0:16], ACT.Tanh, scale=1.0 / 15).then_inc(*signal(G_ACT, "tanh"))
                act.wait_ge(*done(G_ACT, "tanh"))
                f(LG[:, :, 0:8], TI[:, :, 8:16], ACT.Exp, scale=-15.0).then_inc(*signal(G_ACT, "expf"))
                act.wait_ge(*done(G_ACT, "expf"))
                f(LG[:, :, 0:8], LG[:, :, 0:8], ACT.Ln, bias=1.0).then_inc(*signal(G_ACT, "lnf"))
                act.wait_ge(*done(G_V, "negabs"))
                f(NA[:], NA[:], ACT.Exp).then_inc(*signal(G_ACT, "expab"))
                act.wait_ge(*done(G_ACT, "expab"))
                f(NA[:], NA[:], ACT.Ln, bias=1.0).then_inc(*signal(G_ACT, "lnab"))
                f(EA[:], BIA[:, 32:48], ACT.Exp).then_inc(*signal(G_ACT, "alog"))
                yield from gap(6)
                act.wait_ge(*done(G_V, "kd"))
                f(EG[:], GAM[:], ACT.Exp).then_inc(*signal(G_ACT, "eg"))
                f(NEB[:].rearrange("p h m -> p m h"), RS[:, :, 16:32], ACT.Exp).then_inc(*signal(G_ACT, "eb"))
                f(HB[:].rearrange("p h m -> p m h"), LNB[:], ACT.Exp).then_inc(*signal(G_ACT, "hb"))
                f(KD[:], KD[:], ACT.Exp).then_inc(*signal(G_ACT, "kd"))
                yield from gap(6)
                act.wait_ge(*done(G_V, "ems"))
                f(EMT[:], EMT[:], ACT.Exp).then_inc(*signal(G_ACT, "emt"))
                yield

            def outputs(steps, g, q, kt, col, b0):
                for j in range(4):
                    wait_alone(act, *done(steps, f"out{j // 2}", g))
                    kw = {} if col is None else {"scale": NC_[:, bass.ds(col(j), 1)]}
                    f(YH[:, bass.ds(kt + j, 1), :], H[:, b0 + j // 2:b0 + j // 2 + 1, sl(j % 2, S)], ACT.Copy, **kw).then_inc(out_hi, 1)
                yield

            def ml(g):
                after_side(act, g)
                to = wk(3)
                pr = PR[:, :, NBLK:3 * NBLK].rearrange("p m (s n) -> p m s n", s=2)
                f(to.rearrange("p (m n) -> p m n", m=M), pr[:, :, 0, :], ACT.Tanh, scale=0.5).then_inc(*signal(ML_ACT, "to"))
                f(wk(9).rearrange("p (m n) -> p m n", m=M), pr[:, :, 1, :], ACT.Tanh, scale=0.5).then_inc(*signal(ML_ACT, "tz"))
                act.wait_ge(*done(ML_PE, "q", g))
                f(wk(0, 512), bank(0), ACT.Copy, scale=float(P) ** -0.5).then_inc(*signal(ML_ACT, "q"))
                act.wait_ge(*done(ML_PE, "k", g))
                f(wk(0.5, 512), bank(1), ACT.Copy).then_inc(*signal(ML_ACT, "k"))
                yield from gap(3)
                act.wait_ge(*done(ML_V, "arg", g))
                f(wk(2, 768), wk(2, 768), ACT.Exp).then_inc(*signal(ML_ACT, "expw"))
                yield from gap(4)
                yield from gap(3)
                act.wait_ge(*done(ML_V, "h", g))
                f(to, wk(10), ACT.Square).then_inc(*signal(ML_ACT, "sq"))
                yield from gap(2)
                act.wait_ge(*done(ML_V, "ss", g))
                f(ST[:, 8:12], ST[:, 8:12], ACT.Ln, scale=16.0 / 256, bias=eps16_c).then_inc(*signal(ML_ACT, "ln"))
                act.wait_ge(*done(ML_ACT, "ln", g))
                f(ST[:, 8:12], ST[:, 8:12], ACT.Exp, scale=-0.5).then_inc(*signal(ML_ACT, "exp"))
                yield from gap(3)
                yield from outputs(ML_PE, g, g, g * 4, lambda j: g * 4 + (16 + j), 0)

            def dn(g):
                after_side(act, g + 4)
                act.wait_ge(evac, 8 * g + (2 * (E_DN + 4)))
                f(wk(9).rearrange("p (m n) -> p m n", m=M), PR[:, :, 3 * NBLK:], ACT.Tanh, scale=0.5).then_inc(*signal(DN_ACT, "tz"))
                yield from gap(4)
                act.wait_ge(*done(DN_V, "conv033", g))
                f(wk(3), wk(0), ACT.Tanh, scale=0.5).then_inc(*signal(DN_ACT, "tq"))
                act.wait_ge(*done(DN_V, "subg", g))
                f(wk(4, 2 * U), wk(4, 2 * U), ACT.Exp).then_inc(*signal(DN_ACT, "decay"))
                yield from gap(4)
                act.wait_ge(*done(DN_V, "conv133", g))
                f(wk(8), wk(1), ACT.Tanh, scale=0.5).then_inc(*signal(DN_ACT, "tk"))
                act.wait_ge(*done(DN_V, "silu0", g))
                f(wk(6), wk(0), ACT.Square).then_inc(*signal(DN_ACT, "sqq"))
                yield from gap(4)
                act.wait_ge(*done(DN_V, "conv233", g))
                f(wk(3), wk(2), ACT.Tanh, scale=0.5).then_inc(*signal(DN_ACT, "tv"))
                act.wait_ge(*done(DN_V, "silu1", g))
                f(wk(7), wk(1), ACT.Square).then_inc(*signal(DN_ACT, "sqk"))
                yield
                act.wait_ge(*done(DN_PE, "ssq", g))
                f(wk(6), bank(2, 2), ACT.Ln, scale=float(P), bias=eps512_c).then_inc(*signal(DN_ACT, "lnq"))
                act.wait_ge(*done(DN_PE, "ssk", g))
                f(wk(7), bank(0, 2), ACT.Ln, bias=eps4_c).then_inc(*signal(DN_ACT, "lnk"))
                act.wait_ge(*done(DN_ACT, "lnq", g))
                f(wk(6), wk(6), ACT.Exp, scale=-0.5).then_inc(*signal(DN_ACT, "expq"))
                act.wait_ge(*done(DN_ACT, "lnk", g))
                f(wk(7), wk(7), ACT.Exp, scale=-0.5).then_inc(*signal(DN_ACT, "expk"))
                yield from gap(8)
                for l in LVS:
                    for p in range(2):
                        act.wait_ge(*done(DN_PE, f"x{l}{p}", g))
                        f(wk(3 + p / 2, 512), bank(p), ACT.Copy).then_inc(*signal(DN_ACT, f"x{l}{p}"))
                    yield from gap(2)
                u = wk(8).rearrange("p (h m t) -> p h m t", h=4, m=M)
                b4 = lambda i: H[:, i, :].rearrange("p (h t) -> p h t", h=4)
                act.wait_ge(*done(DN_PE, "u0", g))
                f(u[:, :, 0, :], b4(0), ACT.Copy).then_inc(*signal(DN_ACT, "u0"))
                yield
                act.wait_ge(*done(DN_PE, "s1", g))
                f(wk(11.5, 512), bank(1), ACT.Copy).then_inc(*signal(DN_ACT, "s1"))
                act.wait_ge(*done(DN_PE, "o0", g))
                f(wk(10, 512), bank(0), ACT.Copy).then_inc(*signal(DN_ACT, "f0"))
                yield from gap(2)
                act.wait_ge(*done(DN_PE, "u1", g))
                f(u[:, :, 1, :], b4(1), ACT.Copy).then_inc(*signal(DN_ACT, "u1"))
                yield
                act.wait_ge(*done(DN_V, "f1b", g))
                f(wk(3), wk(10), ACT.Square).then_inc(*signal(DN_ACT, "sq"))
                yield from gap(1)
                act.wait_ge(*done(DN_V, "ss", g))
                f(ST[:, 8:16], ST[:, 8:16], ACT.Ln, scale=4.0 / P, bias=eps4_c).then_inc(*signal(DN_ACT, "ln"))
                act.wait_ge(*done(DN_ACT, "ln", g))
                f(ST[:, 8:16], ST[:, 8:16], ACT.Exp, scale=-0.5).then_inc(*signal(DN_ACT, "exp"))
                yield from gap(2)
                yield from outputs(DN_PE, g, g + 4, g * 4, lambda j: 32, 2)

            def attend(kind, q, n, evac_need, zslot, kt):
                steps, act_s, dve = AT_PE[kind], AT_ACT[kind], AT_V[kind]
                full = kind == "m"
                w = 512 if full else BIASW
                after_side(act, q)
                act.wait_ge(evac, evac_need)
                f(wk(8).rearrange("p (m n) -> p m n", m=M), PR[:, :, sl(zslot, NBLK)], ACT.Tanh, scale=0.5).then_inc(*signal(act_s, "tz"))
                act.wait_ge(*done(steps, "q", n))
                f(wk(0), bank(2, 2), ACT.Copy, scale=float(P) ** -0.5).then_inc(*signal(act_s, "q"))
                yield from gap(4)
                act.wait_ge(*done(dve, "neg", n))
                for h in range(4):
                    for m in range(M):
                        n0 = S if full else P
                        a, b = (0, n0) if m == 0 else (n0, n0 + S)
                        last = f(wk(2, 4 * w)[:, h * w + a:h * w + b], H[:, h, a:b], ACT.Exp, bias=ST[:, 24 + 2 * h + m:25 + 2 * h + m],
                                 accum_out=ST[:, 32 + 2 * h + m:33 + 2 * h + m])
                last.then_inc(*signal(act_s, "exp"))
                yield from gap(4)
                act.wait_ge(*done(steps, "pt", n))
                f(wk(4, 2 * w).rearrange("p (h n) -> p h n", h=2), H[:, 0:2, 0:w], ACT.Copy).then_inc(*signal(act_s, "pt"))
                yield from gap(5)
                yield from outputs(steps, n, q, kt, None, 2)

            def gla(l, q, evac_need):
                after_side(act, q)
                act.wait_ge(evac, evac_need)
                f(wk(8).rearrange("p (m n) -> p m n", m=M), PR[:, :, sl(1, NBLK)], ACT.Tanh, scale=0.5).then_inc(*signal(GL_ACT, "tz"))
                act.wait_ge(*done(GL_PE, "q", l))
                f(wk(0, 512), bank(0), ACT.Copy, scale=64.0 ** -0.5).then_inc(*signal(GL_ACT, "q"))
                act.wait_ge(*done(GL_PE, "k", l))
                f(wk(0.5, 512), bank(1), ACT.Copy).then_inc(*signal(GL_ACT, "k"))
                act.wait_ge(*done(GL_PE, "lrt", l))
                f(LRT, H[0:17, 2, 0:S], ACT.Copy).then_inc(*signal(GL_ACT, "lrt"))
                yield from gap(3)
                x = wk(6.5, 512)
                act.wait_ge(rel_st, l * 16 + 16)
                act.wait_ge(*done(GL_PE, "logit", l))
                f(x, bank(3), ACT.Abs).then_inc(*signal(GL_ACT, "absx"))
                act.wait_ge(*done(GL_ACT, "absx", l))
                f(x, x, ACT.Exp, scale=-1.0).then_inc(*signal(GL_ACT, "expx"))
                act.wait_ge(*done(GL_ACT, "expx", l))
                f(x, x, ACT.Ln, bias=1.0).then_inc(*signal(GL_ACT, "lnx"))
                yield from gap(2)
                act.wait_ge(*done(GL_PE, "b", l))
                f(wk(3, 512), bank(2), ACT.Copy).then_inc(*signal(GL_ACT, "b"))
                yield from gap(1)
                for lv in range(1, 9):
                    hf = 2 ** (lv - 1)
                    e = wk(4 + (lv % 2) / 2, 512).rearrange("p (n s h) -> p n s h", s=2, h=hf)
                    act.wait_ge(*done(GL_V, f"d{lv}", l))
                    f(e[:, :, 0, :], e[:, :, 0, :], ACT.Exp, scale=-1.0 / 16)
                    f(e[:, :, 1, :], e[:, :, 1, :], ACT.Exp, scale=1.0 / 16).then_inc(*signal(GL_ACT, f"e{lv}"))
                    yield from gap(2)
                act.wait_ge(*done(GL_PE, "l8", l))
                f(wk(6, 512).rearrange("p (hh par t) -> p par hh t", hh=2, par=2), H[:, 0:2, 0:S].rearrange("p par (hh t) -> p par hh t", hh=2),
                  ACT.Copy).then_inc(*signal(GL_ACT, "at8"))
                yield
                act.wait_ge(*done(GL_PE, "pv", l))
                f(wk(7), bank(2, 2), ACT.Copy).then_inc(*signal(GL_ACT, "f"))
                act.wait_ge(*done(GL_ACT, "f", l))
                f(wk(1), wk(7), ACT.Square).then_inc(*signal(GL_ACT, "sq"))
                yield from gap(1)
                act.wait_ge(*done(GL_V, "ss", l))
                f(ST[:, 8:16], ST[:, 8:16], ACT.Ln, scale=4.0 / P, bias=eps4_c).then_inc(*signal(GL_ACT, "ln"))
                act.wait_ge(*done(GL_ACT, "ln", l))
                f(ST[:, 8:16], ST[:, 8:16], ACT.Exp, scale=-0.5).then_inc(*signal(GL_ACT, "exp"))
                yield from gap(2)
                yield from outputs(GL_PE, l, q, 8, lambda j: 33 + l, 0)

            act.dma_start(RES[:], x2).then_inc(x_in, 16)
            act.wait_ge(eps_ready, 1)
            for c in range(NCH):
                act.wait_ge(m_pe, c + 1)
                f(YH[:, 2 * c:2 * c + 2, :], H[:, c % 4:c % 4 + 1, :].rearrange("p b (j t) -> p (b j) t", j=2), ACT.Copy).then_inc(m_hi, 1)
            for c in range(AHEAD):
                high(N_MEM, c, 0)
            stream(N_MEM, 4, 0, x_prep(), ahead=(W_GATE, EX_GATE))
            small_block(N_GATE, 0, 48, G_ACT, GT, EX_GATE)
            X1 = EX_GATE
            mkv = [[(mkv_out[b], 16)] for b in range(4)]
            stream(N_ML, 4, X1, gates(), free=mkv)
            with act.Fori(1, 4) as g:
                stream(N_ML + g * (4 * NCH), 4, X1, ml(g - 1),
                       free=[[done(ML_PE, "k", g - 1)], [done(ML_V, "g2", g - 1)], [done(ML_V, "g1", g - 1)], [done(ML_PE, "pv", g - 1)]])
            stream(N_GA, 4, X1, ml(3), free=[[done(ML_PE, "k", 3)], [done(ML_V, "g2", 3)], [done(ML_V, "g1", 3)], [done(ML_PE, "pv", 3)]])
            act.wait_ge(evac, 2 * E_YA)
            for m in range(M):
                f(PR[:, m, :], PR[:, m, :], ACT.Tanh, scale=0.5).then_inc(g_tanh, 1)
            stream(N_YA, 4, X1, none(), slots=None)
            stream(N_DN, 4, X1, none(), free=[[(evac, 2 * E_DN)]])
            with act.Fori(1, 4) as g:
                stream(N_DN + g * (4 * NCH), 4, X1, dn(g - 1),
                       free=[[done(DN_PE, "q", g - 1)], [done(DN_PE, "k", g - 1)], [done(DN_PE, "v", g - 1)], [done(DN_V, "g", g - 1)]])
            stream(N_GB, 4, X1, dn(3), free=[[done(DN_PE, "q", 3)], [done(DN_PE, "k", 3)], [done(DN_PE, "v", 3)], [done(DN_V, "g", 3)]])
            act.wait_ge(evac, 2 * E_YB)
            for m in range(M):
                f(PR[:, m, :], PR[:, m, :], ACT.Tanh, scale=0.5).then_inc(g_tanh, 1)
            stream(N_YB, 4, X1, none(), slots=None, ahead=None)
            act.wait_ge(evac, 2 * E_L)
            for m in range(M):
                f(wk(4, D), RES[:, m, :], ACT.Square, accum_out=ST[:, m:m + 1]).then_inc(norm_s, 1)
                act.wait_ge(norm_s, 6 + m)
            f(ST[:, 2:4], ST[:, 0:2], ACT.Ln, scale=1.0 / D, bias=eps_c).then_inc(norm_s, 1)
            act.wait_ge(norm_s, 8)
            f(ST[:, 4:6], ST[:, 2:4], ACT.Exp, scale=-0.5).then_inc(norm_s, 1)
            with act.Fori(0, 2) as l:
                n, e, q = N_L + l * LSZ, E_L + l * 17, 8 + 4 * l
                ex = 16 * l + X1
                for c in range(AHEAD):
                    high(n, c, ex + EX_LR, 4 * 16)
                for c in range(NCH):
                    act.wait_ge(x_pe, 8 * l + (c + 9))
                    for j in range(2):
                        f(XH[:, 2 * c + j, :], H[:, c % 4, sl(j, S)], ACT.Copy).then_inc(x_hi, 1)
                small_block(n, ex, 16, GL_ACT, LR, EX_LR)
                ex = 16 * l + (X1 + EX_LR)
                stream(n + L_M, 2, ex, none())
                stream(n + L_B, 3, ex, attend("m", q, l, 2 * (e + 2), 1, 12), slots=(0, 1, 3), free=[[done(AT_PE["m"], "q", l)], [done(AT_V["m"], "g", l)]])
                stream(n + L_A0, 4, ex, gla(l, q + 1, 2 * (e + 5)), free=[[done(GL_PE, "k", l)], [done(GL_V, "g", l)], [], [done(GL_PE, "pv", l)]])
                stream(n + L_A1, 4, ex, attend("a", q + 2, 2 * l, 2 * (e + 9), 3, 0),
                       free=[[done(AT_PE["a"], "q", 2 * l)], [done(AT_PE["a"], "k", 2 * l)], [done(AT_PE["a"], "pv", 2 * l)], [done(AT_V["a"], "g", 2 * l)]])
                finish(attend("a", q + 3, 2 * l + 1, 2 * (e + 13), 3, 4))
                stream(n + L_Y, 4, ex, none(), slots=None, ahead=None)
                for m in range(M):
                    act.wait_ge(*done(LN_V, f"ag{m}", l))
                    f(ST[:, 50 + m:51 + m], ST[:, 41 + 2 * m:42 + 2 * m], ACT.Ln, bias=epsln_c).then_inc(norm_s, 1)
                    act.wait_ge(norm_s, l * 4 + (10 + 2 * m))
                    f(ST[:, 50 + m:51 + m], ST[:, 50 + m:51 + m], ACT.Exp, scale=-0.5).then_inc(norm_s, 1)

        @block.vector
        def _(dve):
            tt, ts, stt = dve.tensor_tensor, dve.tensor_scalar, dve.scalar_tensor_tensor

            def low(n, c, width=CH * NBLK):
                dve.wait_ge(hi_done, n + (c + 1))
                tt(WL[:, c % RING, 0:width], RAW[:, c % RING, 0:width], WH[:, c % RING, 0:width].bitcast(F32), ALU.subtract).then_inc(lo_done, 1)

            def stream(n, nblk, side, take=None, ahead=CH * NBLK):
                for b in range(nblk):
                    for c in range(NCH):
                        i = b * NCH + c + AHEAD
                        if i < nblk * NCH:
                            low(n, i)
                        elif ahead:
                            low(n, i, ahead)
                        advance(side, 2)
                    if take:
                        dve.wait_ge(used, n + (b + 1) * NCH)
                        for m in range(M):
                            take(b, m, SP_[:, 2 * (b % 2) + m, :])
                finish(side)

            def small_block(n, width):
                for i in range(AHEAD, RING):
                    low(n, i, 4 * width)
                for i in range(AHEAD):
                    low(n, RING + i)

            def x_prep():
                dve.wait_ge(cols_pe, 1)
                dve.tensor_copy(CW[:], H[:, 0, 0:192]).then_inc(cols_v, 1)
                nc16 = NC_[:, 0:16].rearrange("p (c j) -> p c j", j=2)
                for j in range(2):
                    dve.tensor_copy(nc16[:, :, j], H[:, 0, 192 + 8 * j:200 + 8 * j]).then_inc(cols_v, 1)
                dve.tensor_copy(NC_[:, 16:33], H[:, 0, 208:225]).then_inc(cols_v, 1)
                dve.tensor_copy(NC_[:, 33:35], H[:, 0, 226:228]).then_inc(cols_v, 1)
                yield from gap(11)
                for c in range(NCH):
                    for j in range(2):
                        k = 2 * c + j
                        dve.wait_ge(x_hi, 2 * c + 2)
                        stt(XL[:, k, :], H[:, c % 4, sl(j, S)], NC_[:, k:k + 1], XH[:, k, :].bitcast(F32), ALU.mult, ALU.subtract).then_inc(x_lo, 1)
                    yield

            def gates():
                b3 = lambda ap: ap.unsqueeze(1).broadcast_to([P, M, ap.shape[1]])
                dve.wait_ge(*done(G_ACT, "mini1"))
                tt(GT[:, :, 0:16], GT[:, :, 0:16], b3(BIA[:, 0:16]), ALU.add).then_inc(*signal(G_V, "bias_if"))
                tt(GT[:, :, 32:48], GT[:, :, 32:48], b3(BIA[:, 16:32]), ALU.add).then_inc(*signal(G_V, "bias_a"))
                dve.wait_ge(*done(G_V, "bias_a"))
                stt(NA[:], GT[:, :, 16:48], -1.0, GT[:, :, 16:48], ALU.mult, ALU.min).then_inc(*signal(G_V, "negabs"))
                dve.wait_ge(*done(G_ACT, "alog"))
                stt(LNB[:], GT[:, :, 16:32], 0.0, NA[:, :, 0:16], ALU.min, ALU.subtract).then_inc(*signal(G_V, "lnb"))
                stt(GT[:, :, 32:48], GT[:, :, 32:48], 0.0, NA[:, :, 16:32], ALU.max, ALU.add).then_inc(*signal(G_V, "sp"))
                dve.wait_ge(*done(G_V, "sp"))
                stt(LG[:, :, 8:24], GT[:, :, 32:48], -1.0, b3(EA[:]), ALU.mult, ALU.mult).then_inc(*signal(G_V, "g"))
                yield from gap(3)
                dve.wait_ge(*done(G_PE, "cumsum"))
                dve.tensor_copy(CS[:, 0, :], H[:, 2, 0:24]).then_inc(*signal(G_V, "cs0"))
                dve.tensor_copy(CS[:, 1, :], H[:, 2, 32:56]).then_inc(*signal(G_V, "cs1"))
                dve.wait_ge(*done(G_V, "cs1"))
                hm = lambda t: t[:].rearrange("p h m -> p m h")
                stt(hm(AS), TI[:, :, 0:8], 15.0, CS[:, :, 0:8], ALU.mult, ALU.add).then_inc(*signal(G_V, "as"))
                dve.tensor_copy(hm(GAM), CS[:, :, 8:24]).then_inc(*signal(G_V, "gam"))
                dve.tensor_copy(RS[:, :, 0:16], CS[:, :, 8:24]).then_inc(*signal(G_V, "rs0"))
                tt(RS[:, :, 16:32], CS[:, :, 8:24], LNB[:], ALU.add).then_inc(*signal(G_V, "rs1"))
                dve.wait_ge(*done(G_V, "as"))
                dve.tensor_copy(RS[:, :, 32:40], hm(AS)).then_inc(*signal(G_V, "rs2"))
                tt(KD[:], H[:, 2, 64:80], CS[:, 0, 8:24], ALU.subtract).then_inc(*signal(G_V, "kd"))
                yield from gap(5)
                dve.wait_ge(*done(G_PE, "rows"))
                dve.tensor_copy(RT[:], H[0:40, 3, 0:S]).then_inc(*signal(G_V, "rt"))
                dve.wait_ge(*done(G_V, "rt"))
                dve.tensor_tensor_scan(MT[32:40, :], RT[32:40, :], RT[32:40, :], 0.0, ALU.max, ALU.max).then_inc(*signal(G_V, "scan"))
                dve.wait_ge(*done(G_V, "scan"))
                ts(RT[32:40, :], MT[32:40, :], -1.0, None, ALU.mult).then_inc(*signal(G_V, "negm"))
                yield from gap(5)
                dve.wait_ge(*done(G_PE, "negm"))
                tt(hm(EMT), H[:, 0, 0:16].rearrange("p (m h) -> p m h", m=M), CS[:, :, 0:8], ALU.add).then_inc(*signal(G_V, "ems"))
                dve.wait_ge(*done(G_ACT, "kd"))
                ts(NEB[:], NEB[:], -1.0, None, ALU.mult).then_inc(*signal(G_V, "neb"))
                ts(HB[:], HB[:], 0.5, None, ALU.mult).then_inc(*signal(G_V, "hb"))
                yield

            def outputs(steps, g, q, kt, col, b0):
                for j in range(4):
                    dve.wait_ge(out_hi, NCH + (4 * q + (2 * (j // 2) + 2)))
                    src = H[:, b0 + j // 2:b0 + j // 2 + 1, sl(j % 2, S)]
                    yh, yl = YH[:, bass.ds(kt + j, 1), :].bitcast(F32), YL[:, bass.ds(kt + j, 1), :]
                    if col is None:
                        tt(yl, src, yh, ALU.subtract).then_inc(out_lo, 1)
                    else:
                        stt(yl, src, NC_[:, bass.ds(col(j), 1)], yh, ALU.mult, ALU.subtract).then_inc(out_lo, 1)
                yield

            def ml(g):
                w = wk(2, 768)
                after_side(dve, g)
                dve.wait_ge(rows_in, g * 16 + 16)
                for h in range(2):
                    for s in range(M):
                        last = ts(w[:, h * 384 + s * S:h * 384 + s * S + S - s * P], wk(1, 512)[:, h * S + s * P:(h + 1) * S],
                                  AS[:, bass.ds(g * 2 + h, 1), s], 0.0, ALU.add, ALU.min)
                last.then_inc(*signal(ML_V, "arg"))
                G, z = wk(9).rearrange("p (m n) -> p m n", m=M), PR[:, :, 2 * NBLK:3 * NBLK]
                dve.wait_ge(*done(ML_ACT, "tz", g))
                stt(G, G, 1.0, z, ALU.add, ALU.mult).then_inc(*signal(ML_V, "g1"))
                dve.wait_ge(*done(ML_V, "g1", g))
                stt(wk(9), wk(3), 1.0, wk(9), ALU.add, ALU.mult).then_inc(*signal(ML_V, "g2"))
                yield from gap(3)
                dve.wait_ge(*done(ML_ACT, "expw", g))
                diag = w.rearrange("p (h n) -> p h n", h=2)
                for h in range(2):
                    d = bass.AP(WK, w.offset + h * 384, [[12 * U, P], [S, 2], [1, P]])
                    last = tt(d, d, over(upper[:], 2), ALU.mult)
                last.then_inc(*signal(ML_V, "mask"))
                dve.wait_ge(*done(ML_V, "mask", g))
                dve.wait_ge(*done(ML_PE, "scores", g))
                tt(diag, diag, H[:, 2:4, 0:384], ALU.mult).then_inc(*signal(ML_V, "p"))
                yield from gap(4)
                dve.wait_ge(*done(ML_PE, "pv", g))
                dve.wait_ge(*done(G_ACT, "emt"))
                emt = EMT[:, bass.ds(g * 2, 2), :]
                hm4 = lambda ap: ap.rearrange("p (h m) -> p h m", h=2)
                stt(hm4(ST[:, 20:24]), hm4(H[:, 2, 0:4]), -1.0, emt, ALU.mult, ALU.max).then_inc(*signal(ML_V, "den0"))
                dve.wait_ge(*done(ML_V, "den0", g))
                tt(ST[:, 12:16], H[:, 2, 0:4], ST[:, 20:24], ALU.max).then_inc(*signal(ML_V, "den"))
                dve.wait_ge(*done(ML_V, "den", g))
                dve.reciprocal(ST[:, 16:20], ST[:, 12:16]).then_inc(*signal(ML_V, "rden"))
                dve.wait_ge(*done(ML_V, "rden", g))
                F = wk(10).rearrange("p (m h e) -> p h m e", m=M, h=2)
                r4 = ST[:, 16:20].rearrange("p (h m) -> p h m", h=2)
                tt(F, bank(0, 2).rearrange("p (h m e) -> p h m e", h=2, m=M), cols(r4, S), ALU.mult).then_inc(*signal(ML_V, "h"))
                yield from gap(4)
                dve.wait_ge(*done(ML_ACT, "sq", g))
                dve.reduce_sum(ST[:, 8:12], wk(3).rearrange("p (s e) -> p s e", s=4), axis=AX.X).then_inc(*signal(ML_V, "ss"))
                yield from gap(2)
                dve.wait_ge(*done(ML_ACT, "exp", g))
                F4 = wk(10).rearrange("p (s e) -> p s e", s=4)
                tt(F4, F4, cols(ST[:, 8:12], S), ALU.mult).then_inc(*signal(ML_V, "fr"))
                dve.wait_ge(*done(ML_V, "fr", g))
                tt(wk(10), wk(10), wk(9), ALU.mult).then_inc(*signal(ML_V, "fg"))
                yield from gap(2)
                yield from outputs(ML_PE, g, g, g * 4, lambda j: g * 4 + (16 + j), 0)

            def dn(g):
                after_side(dve, g + 4)
                G, z = wk(9).rearrange("p (m n) -> p m n", m=M), PR[:, :, 3 * NBLK:]
                dve.wait_ge(*done(DN_ACT, "tz", g))
                stt(G, G, 1.0, z, ALU.add, ALU.mult).then_inc(*signal(DN_V, "g"))
                CV = wk(0, 3 * U).rearrange("p (c h t) -> p c h t", c=3, h=4)

                def conv(c, b0):
                    dve.wait_ge(*done(DN_PE, "qkv"[c], g))
                    names = [nm for nm in conv_names(c)]
                    for p in (0, 1):
                        for j in range(4):
                            tap, d = 3 - j, j
                            for h in (2 * p, 2 * p + 1):
                                wcol = CW[:, bass.ds(g * 4 + (tap * 48 + c * 16 + h), 1)]
                                src = H[:, b0 + h // 2, sl(h % 2, S)]
                                if j == 0:
                                    ts(CV[:, c, h, :], src, wcol, None, ALU.mult).then_inc(*signal(DN_V, f"conv{c}0{h}"))
                                else:
                                    dve.wait_ge(*done(DN_V, f"conv{c}{j - 1}{h}", g))
                                    stt(CV[:, c, h, d:S], src[:, 0:S - d], wcol, CV[:, c, h, d:S], ALU.mult, ALU.add).then_inc(*signal(DN_V, f"conv{c}{j}{h}"))
                            if j % 2:
                                yield

                yield from conv(0, 0)
                dve.wait_ge(rows_in, g * 32 + (64 + 32))
                d3 = lambda u: wk(u).rearrange("p (s t) -> p s t", t=P)
                for u, name in ((5, "subr"), (4, "subg")):
                    for h in range(4):
                        for m in range(M):
                            e = wk(u + (2 * h + m) / 8, P)
                            last = ts(e, e, GAM[:, bass.ds(g * 4 + h, 1), m], 0.0, ALU.subtract, ALU.min)
                    last.then_inc(*signal(DN_V, name))
                yield from conv(1, 2)
                dve.wait_ge(*done(DN_ACT, "tq", g))
                stt(wk(0), wk(3), 1.0, wk(0), ALU.add, ALU.mult).then_inc(*signal(DN_V, "silu0"))
                dve.wait_ge(*done(DN_ACT, "decay", g))
                tt(d3(5), d3(5), over(strict[:], 8), ALU.mult).then_inc(*signal(DN_V, "maskr"))
                tt(d3(4), d3(4), over(upper[:], 8), ALU.mult).then_inc(*signal(DN_V, "maskg"))
                yield from conv(2, 0)
                dve.wait_ge(*done(DN_ACT, "tk", g))
                stt(wk(1), wk(8), 1.0, wk(1), ALU.add, ALU.mult).then_inc(*signal(DN_V, "silu1"))
                dve.wait_ge(*done(DN_ACT, "tv", g))
                stt(wk(2), wk(3), 1.0, wk(2), ALU.add, ALU.mult).then_inc(*signal(DN_V, "silu2"))
                yield from gap(2)
                dve.wait_ge(*done(DN_ACT, "expq", g))
                tt(wk(0), wk(0), wk(6), ALU.mult).then_inc(*signal(DN_V, "nq"))
                dve.wait_ge(*done(DN_ACT, "expk", g))
                tt(wk(1), wk(1), wk(7), ALU.mult).then_inc(*signal(DN_V, "nk"))
                hb = HB[:, bass.ds(g * 4, 4), :].rearrange("p h m -> p (h m)")
                for p in range(2):
                    dve.wait_ge(*done(DN_PE, f"vt{p}", g))
                    tt(wk(2 + p / 2, 512).rearrange("p (s t) -> p s t", t=P), bank(2 + p).rearrange("p (s t) -> p s t", t=P),
                       cols(HB[:, bass.ds(g * 4 + 2 * p, 2), :].rearrange("p h m -> p (h m)"), P), ALU.mult).then_inc(*signal(DN_V, f"v{p}"))
                yield
                dve.wait_ge(*done(DN_PE, "k0t", g))
                tt(wk(11, 512).rearrange("p (s t) -> p s t", t=P), bank(1).rearrange("p (s t) -> p s t", t=P),
                   cols(KD[:, bass.ds(g * 4, 4)], P), ALU.mult).then_inc(*signal(DN_V, "ke"))
                yield from gap(2)
                for n, b0, u in (("kk", 0, 5), ("qk", 2, 4)):
                    for p in range(2):
                        dve.wait_ge(*done(DN_PE, f"{n}{p}", g))
                        tt(wk(u + p / 2, 512), bank(b0 + p), wk(u + p / 2, 512), ALU.mult).then_inc(*signal(DN_V, ("at" if n == "kk" else "qkt") + str(p)))
                dve.wait_ge(*done(DN_V, "at1", g))
                tt(d3(8), d3(5), over(LV[:, 0, :], 8), ALU.mult).then_inc(*signal(DN_V, "ut0"))
                dve.wait_ge(*done(DN_V, "ut0", g))
                tt(d3(7), over(ident[:], 8), d3(8), ALU.subtract).then_inc(*signal(DN_V, "tt0"))
                yield
                dve.wait_ge(*done(DN_PE, "x0", g))
                dve.wait_ge(*done(DN_V, "tt0", g))
                tt(d3(8), d3(5), over(LV[:, 1, :], 8), ALU.mult).then_inc(*signal(DN_V, "ut1"))
                tt(d3(6), over(ident[:], 8), bank(0, 2).rearrange("p (s t) -> p s t", t=P), ALU.subtract).then_inc(*signal(DN_V, "t0"))
                yield
                for l in LVS:
                    if l < 6:
                        dve.wait_ge(*done(DN_PE, f"x{l}1", g))
                        tt(d3(8), d3(5), over(LV[:, l + 1, :], 8), ALU.mult).then_inc(*signal(DN_V, f"ut{l + 1}"))
                    yield
                    for p in range(2):
                        dve.wait_ge(*done(DN_PE, f"t{l}{p}", g))
                        if l < 6:
                            tt(wk(6 + p / 2, 512), wk(6 + p / 2, 512), bank(p), ALU.subtract).then_inc(*signal(DN_V, f"t{l}{p}"))
                        tt(wk(7 + p / 2, 512), wk(7 + p / 2, 512), bank(2 + p), ALU.subtract).then_inc(*signal(DN_V, f"tt{l}{p}"))
                    yield
                yield from gap(2)
                F1 = wk(10.5, 512).rearrange("p (s t) -> p s t", t=P)
                V = wk(2).rearrange("p (h m t) -> p h m t", h=4, m=M)
                dve.wait_ge(*done(DN_PE, "qs", g))
                tt(F1, bank(3).rearrange("p (s t) -> p s t", t=P), cols(EG[:, bass.ds(g * 4, 4), 1], P), ALU.mult).then_inc(*signal(DN_V, "f1a"))
                dve.wait_ge(*done(DN_PE, "ks", g))
                for h in range(4):
                    stt(V[:, h, 1, :], H[:, 2, sl(h)], NEB[:, bass.ds(g * 4 + h, 1), 1], V[:, h, 1, :], ALU.mult, ALU.add).then_inc(*signal(DN_V, f"r{h}"))
                yield from gap(2)
                dve.wait_ge(*done(DN_PE, "o1", g))
                dve.wait_ge(*done(DN_ACT, "f0", g))
                tt(wk(10.5, 512), bank(0), wk(10.5, 512), ALU.add).then_inc(*signal(DN_V, "f1b"))
                yield from gap(1)
                dve.wait_ge(*done(DN_ACT, "sq", g))
                dve.reduce_sum(ST[:, 8:16], wk(3).rearrange("p (s e) -> p s e", s=8), axis=AX.X).then_inc(*signal(DN_V, "ss"))
                yield from gap(1)
                dve.wait_ge(*done(DN_ACT, "exp", g))
                tt(d3(10), d3(10), cols(ST[:, 8:16], P), ALU.mult).then_inc(*signal(DN_V, "fr"))
                dve.wait_ge(*done(DN_V, "fr", g))
                tt(wk(10), wk(10), wk(9), ALU.mult).then_inc(*signal(DN_V, "fg"))
                yield from gap(2)
                yield from outputs(DN_PE, g, g + 4, g * 4, lambda j: 32, 2)

            def attend(kind, q, n, zslot, kt):
                steps, act_s = AT_PE[kind], AT_ACT[kind]
                full = kind == "m"
                w = 512 if full else BIASW
                after_side(dve, q)
                dve.wait_ge(*done(steps, "k", n))
                dve.tensor_copy(wk(1), bank(0, 2)).then_inc(*signal(AT_V[kind], "k"))
                G = wk(8).rearrange("p (m n) -> p m n", m=M)
                dve.wait_ge(*done(act_s, "tz", n))
                stt(G, G, 1.0, PR[:, :, sl(zslot, NBLK)], ALU.add, ALU.mult).then_inc(*signal(AT_V[kind], "g"))
                yield from gap(3)
                dve.wait_ge(*done(steps, "scores", n))
                mx = ST[:, 16:24]
                src = H
                n0 = S if full else P
                mv = mx.rearrange("p (h m) -> p h m", m=M)
                dve.reduce_max(mv[:, :, 0], src[:, :, 0:n0], axis=AX.X).then_inc(*signal(AT_V[kind], "max0"))
                dve.reduce_max(mv[:, :, 1], src[:, :, n0:n0 + S], axis=AX.X).then_inc(*signal(AT_V[kind], "max1"))
                dve.wait_ge(*done(AT_V[kind], "max1", n))
                ts(ST[:, 24:32], mx, -1.0, None, ALU.mult).then_inc(*signal(AT_V[kind], "neg"))
                yield from gap(5)
                dve.wait_ge(*done(steps, "pt", n))
                dve.tensor_copy(wk(4, 4 * w)[:, 2 * w:4 * w].rearrange("p (h n) -> p h n", h=2), H[:, 2:4, 0:w]).then_inc(*signal(AT_V[kind], "pt"))
                dve.reciprocal(ST[:, 16:24], ST[:, 32:40]).then_inc(*signal(AT_V[kind], "rs"))
                yield from gap(3)
                dve.wait_ge(*done(steps, "pv", n))
                dve.wait_ge(*done(AT_V[kind], "rs", n))
                for m in range(M):
                    last = tt(wk(7 + m / 2, 512).rearrange("p (s t) -> p s t", t=P), bank(m).rearrange("p (s t) -> p s t", t=P),
                              cols(mv[:, :, m], P), ALU.mult)
                last.then_inc(*signal(AT_V[kind], "f"))
                dve.wait_ge(*done(AT_V[kind], "f", n))
                stt(wk(7), wk(8), 0.5, wk(7), ALU.mult, ALU.mult).then_inc(*signal(AT_V[kind], "fg"))
                yield from gap(2)
                yield from outputs(steps, n, q, kt, None, 2)

            def gla(l, q):
                after_side(dve, q)
                A = wk(5, 1536).rearrange("p (c s) -> p c s", c=3)
                dve.memset(wk(5), 0.0).then_inc(*signal(GL_V, "zero"))
                G = wk(8).rearrange("p (m n) -> p m n", m=M)
                dve.wait_ge(*done(GL_ACT, "tz", l))
                stt(G, G, 1.0, PR[:, :, sl(1, NBLK)], ALU.add, ALU.mult).then_inc(*signal(GL_V, "g"))
                yield from gap(2)
                yield
                dve.wait_ge(*done(GL_ACT, "lnx", l))
                stt(wk(3.5, 512), bank(3), 0.0, wk(6.5, 512), ALU.min, ALU.subtract).then_inc(*signal(GL_V, "lg"))
                yield from gap(2)

                def put(par, b, mask):
                    a = wk(5).rearrange("p (m hh par t) -> p par hh m t", m=M, hh=2, par=2)[:, par]
                    m4 = bass.AP(mask.tensor, mask.offset, [list(mask.ap[0]), [0, 2], [0, 2], [1, P]]).bitcast(U32)
                    return dve.copy_predicated(a, m4, H[:, b, :].rearrange("p (hh m t) -> p hh m t", hh=2, m=M))

                wait_alone(dve, *done(GL_PE, "d", l))
                for par in range(2):
                    put(par, par, ident[:]).then_inc(*signal(GL_V, f"cp0{par}"))
                yield from gap(1)
                dve.wait_ge(*done(GL_ACT, "b", l))
                for lv in range(1, 9):
                    size, hf = 2 ** lv, 2 ** (lv - 1)
                    e = wk(4 + (lv % 2) / 2, 512)
                    B = wk(3, 512).rearrange("p (n s) -> p n s", s=size)
                    mid = B[:, :, hf - 1:hf].broadcast_to([P, 512 // size, size])
                    if lv >= 3:
                        dve.wait_ge(*done(GL_V, f"qe{lv - 2}", l))
                    tt(e.rearrange("p (n s) -> p n s", s=size), B, mid, ALU.subtract).then_inc(*signal(GL_V, f"d{lv}"))
                    dve.wait_ge(*done(GL_ACT, f"e{lv}", l))
                    if lv >= 3:
                        dve.wait_ge(*done(GL_PE, f"l{lv - 2}", l))
                    tt(wk(1 + lv % 2).rearrange("p (c n) -> p c n", c=2), wk(0).rearrange("p (c n) -> p c n", c=2), over(e, 2), ALU.mult).then_inc(*signal(GL_V, f"qe{lv}"))
                    if lv < 8:
                        dve.wait_ge(*done(GL_PE, f"l{lv}", l))
                        for par in range(2):
                            wait_alone(dve, *done(GL_V, f"cp{lv - 1}{par}", l))
                            put(par, 2 * (lv % 2) + par, SY[:, lv - 1, :] if lv < 7 else LV[:, 6, :]).then_inc(*signal(GL_V, f"cp{lv}{par}"))
                    yield from gap(2)
                yield from gap(2)
                dve.wait_ge(*done(GL_ACT, "sq", l))
                dve.reduce_sum(ST[:, 8:16], wk(1).rearrange("p (s e) -> p s e", s=8), axis=AX.X).then_inc(*signal(GL_V, "ss"))
                yield
                dve.wait_ge(*done(GL_ACT, "exp", l))
                F8 = wk(7).rearrange("p (s e) -> p s e", s=8)
                tt(F8, F8, cols(ST[:, 8:16], P), ALU.mult).then_inc(*signal(GL_V, "fr"))
                dve.wait_ge(*done(GL_V, "fr", l))
                tt(wk(7), wk(7), wk(8), ALU.mult).then_inc(*signal(GL_V, "fg"))
                yield from gap(2)
                yield from outputs(GL_PE, l, q, 8, lambda j: 33 + l, 0)

            def gated(base):
                def take(b, m, acc):
                    tmp = wk(11 + m / 2, 512)
                    k = 8 * base + 2 * b + m
                    dve.wait_ge(g_tanh, 2 * base + 2)
                    if b:
                        dve.wait_ge(evac, 2 * (E_YB if base else E_YA) + (2 * b + m - 1))
                    stt(tmp, PR[:, m, sl(b, NBLK)], 1.0, acc, ALU.add, ALU.mult).then_inc(evac_tmp, 1)
                    dve.wait_ge(evac_tmp, k + 1)
                    r = RES[:, m, sl(b, NBLK)]
                    stt(r, tmp, 0.5, r, ALU.mult, ALU.add).then_inc(evac, 1)
                return take

            dve.memset(LR[:, :, 16:17], 1.0)
            dve.memset(eps_c, EPS)
            dve.memset(eps16_c, 16 * EPS)
            dve.memset(eps512_c, 4 * P * EPS)
            dve.memset(eps4_c, 4 * EPS)
            dve.memset(epsln_c, LN_EPS).then_inc(eps_ready, 1)
            for c in range(NCH):
                dve.wait_ge(m_hi, c + 1)
                v = lambda t: t[:, 2 * c:2 * c + 2, :]
                tt(v(YL), H[:, c % 4:c % 4 + 1, :].rearrange("p b (j t) -> p (b j) t", j=2), v(YH).bitcast(F32), ALU.subtract).then_inc(m_lo, 1)
            for c in range(AHEAD):
                low(N_MEM, c)
            stream(N_MEM, 4, x_prep(), ahead=W_GATE)
            small_block(N_GATE, 48)
            stream(N_ML, 4, gates())
            with dve.Fori(1, 4) as g:
                stream(N_ML + g * (4 * NCH), 4, ml(g - 1))
            stream(N_GA, 4, ml(3))
            stream(N_YA, 4, none(), take=gated(0))
            stream(N_DN, 4, none())
            with dve.Fori(1, 4) as g:
                stream(N_DN + g * (4 * NCH), 4, dn(g - 1))
            stream(N_GB, 4, dn(3))
            stream(N_YB, 4, none(), take=gated(1), ahead=None)
            dve.wait_ge(norm_s, 9)
            dve.wait_ge(lw_in, 16)
            for m in range(M):
                last = stt(RES[:, m, :], RES[:, m, :], ST[:, 4 + m:5 + m], wk(0, D), ALU.mult, ALU.mult)
            last.then_inc(x_tok, 1)
            with dve.Fori(0, 2) as l:
                n, q = N_L + l * LSZ, 8 + 4 * l
                for c in range(AHEAD):
                    low(n, c, 4 * 16)
                for c in range(NCH):
                    for j in range(2):
                        k = 2 * c + j
                        dve.wait_ge(x_hi, 16 * l + (18 + 2 * c))
                        tt(XL[:, k, :], H[:, c % 4, sl(j, S)], XH[:, k, :].bitcast(F32), ALU.subtract).then_inc(x_lo, 1)
                small_block(n, 16)
                R, E = wk(6, 257)[0:8, :], wk(6.5, BIASW)[0:8, :]
                dve.wait_ge(rel_in, l * 16 + 16)
                dve.tensor_copy(E[:, 0:P], R[:, 256:257].broadcast_to([8, P])).then_inc(rel_s, 1)
                dve.tensor_copy(E[:, P:BIASW - 1], bass.AP(WK, R.offset + 255, [[12 * U, 8], [-1, 255]])).then_inc(rel_s, 1)
                stream(n + L_M, 2, none())
                stream(n + L_B, 3, attend("m", q, l, 1, 12))
                stream(n + L_A0, 4, gla(l, q + 1))
                BW = wk(9, 3 * U).rearrange("p (h n) -> p h n", h=A_H)
                dve.wait_ge(rel_bw, l * 16 + 16)
                dve.tensor_copy(BW[:, :, 0:P], BW[:, :, S:BIASW]).then_inc(rel_m, 1)
                dve.wait_ge(rel_m, l * 3 + 1)
                dve.memset(BW[64:P, :, 64:P], NEG).then_inc(rel_m, 1)
                dve.memset(BW[64:P, :, BIASW - 64:BIASW], NEG).then_inc(rel_m, 1)
                stream(n + L_A1, 4, attend("a", q + 2, 2 * l, 3, 0))
                finish(attend("a", q + 3, 2 * l + 1, 3, 4))

                def take(b, m, acc):
                    r = RES[:, m, sl(b, NBLK)]
                    stt(r, r, ALPHA, acc, ALU.mult, ALU.add).then_inc(evac, 1)
                    dve.wait_ge(evac, (E_L + 13) * 2 + 34 * l + (2 * b + m + 1))
                    dve.bn_stats(BN[:, m, b, :], r).then_inc(*signal(LN_V, f"st{m}{b}"))

                stream(n + L_Y, 4, none(), take=take, ahead=None)
                for m in range(M):
                    wait_alone(dve, *done(LN_V, "st13", l))
                    dve.bn_aggr(ST[:, 40 + 2 * m:42 + 2 * m], BN[:, m, :, :].rearrange("p a b -> p (a b)")).then_inc(*signal(LN_V, f"ag{m}"))
                dve.wait_ge(lw_in, 32 * l + 48)
                for m in range(M):
                    r = RES[:, m, :]
                    dve.wait_ge(norm_s, l * 4 + (11 + 2 * m))
                    ts(r, r, ST[:, 40 + 2 * m:41 + 2 * m], ST[:, 50 + m:51 + m], ALU.subtract, ALU.mult).then_inc(*signal(LN_V, f"xm{m}"))
                    dve.wait_ge(*done(LN_V, f"xm{m}", l))
                    tt(r, r, wk(0, D), ALU.mult).then_inc(*signal(LN_V, f"xg{m}"))
                    dve.wait_ge(*done(LN_V, f"xg{m}", l))
                    last = tt(r, r, wk(2, D), ALU.add)
                last.then_inc(x_tok, 1)


INPUTS = ["x", "norm_w", "w_in", "ml_i_bias", "ml_f_bias", "ml_norm_w", "dn_conv_w", "dn_a_log", "dn_dt_bias", "dn_norm_w",
          "w_out", "final_norm_w", "mem_2", "w_in_2", "a_rel_bias_2", "b_gate_w_2", "b_gate_b_2", "b_norm_g_2", "w_mem_kv_2",
          "w_out_2", "ln_g_2", "ln_b_2"]


def kernel(**inputs):
    import concourse.bacc as bacc
    from concourse.bass_utils import run_bass_kernel_spmd

    nc = bacc.Bacc("TRN2", target_bir_lowering=False, num_devices=1)
    arrays, args = {}, []
    for name in INPUTS:
        a = np.ascontiguousarray(inputs[name])
        arrays[f"in_{name}"] = a
        args.append(nc.dram_tensor(f"in_{name}", a.shape, mybir.dt.from_np(a.dtype), kind="ExternalInput").ap())
    args.append(nc.dram_tensor("out", (1, S, D), F32, kind="ExternalOutput").ap())
    build(nc, *args)
    result = run_bass_kernel_spmd(nc, [arrays], core_ids=[0])
    return result.results[0]["out"]
```

```python
from contextlib import ExitStack

import numpy as np
import concourse.bass as bass
from concourse import mybir

F32 = mybir.dt.float32
F32R = mybir.dt.float32r
U32 = mybir.dt.uint32
ACT = mybir.ActivationFunctionType
ALU = mybir.AluOpType
AX = mybir.AxisListType

P = 128
S = 256
M = S // P
D = 2048
KT = D // P
NBLK = 512
CH = 2
NCH = KT // CH
RING = 4
AHEAD = 2
U = 1024
EPS = 1e-6
LN_EPS = 1e-5
NEG = -1e30
ML_H, DN_H, A_H = 8, 16, 8
ALPHA = (2.0 * 2) ** 0.25

C_MLQ, C_MLK, C_MLV, C_MLO, C_MLZ, C_IF = 0, 1024, 2048, 4096, 6144, 8192
C_DN, C_DNZ, C_BA, C_GA, C_GB = 8208, 14352, 16400, 16432, 18480
C_AQ, C_AK, C_AV, C_AZ, C_BQ, C_BV, C_BZ, C_LR, C_MQ, C_MZ = 0, 1024, 2048, 3072, 4096, 4608, 5120, 5632, 5648, 6160
BIASW = 384


def steps_of(sem, names):
    return sem, {name: i + 1 for i, name in enumerate(names)}, [0]


def signal(steps, name):
    sem, place, at = steps
    assert place[name] == at[0] + 1, name
    at[0] = (at[0] + 1) % len(place)
    return sem, 1


def done(steps, name, g=0):
    sem, place, _ = steps
    return sem, g * len(place) + place[name]


def build(nc, x, norm_w, w_in, ml_i_bias, ml_f_bias, ml_norm_w, dn_conv_w, dn_a_log, dn_dt_bias, dn_norm_w,
          w_out, final_norm_w, mem, w_in2, rel, gate_w, gate_b, gla_g, w_mkv, w_out2, ln_g, ln_b, out):
    IN1, IN2 = w_in.shape[2], w_in2.shape[2]
    x2 = x.rearrange("b (m p) d -> p (b m) d", p=P)
    mem2 = mem.rearrange("b (m p) d -> p (b m) d", p=P)
    out2 = out.rearrange("b (m p) d -> p (b m) d", p=P)
    rows_d = nc.dram_tensor("rows_scratch", (40, S), F32, kind="Internal").ap()
    mkv_d = nc.dram_tensor("mkv_scratch", (S, 2048), F32, kind="Internal").ap()
    rel_d = nc.dram_tensor("rel_scratch", (A_H, BIASW), F32, kind="Internal").ap()

    with ExitStack() as ctx:
        def sb(name, shape, dt=F32):
            return ctx.enter_context(nc.sbuf_tensor(name, shape, dt))

        def sem(name):
            return ctx.enter_context(nc.semaphore(name))

        XH = sb("x_high", [P, KT, S], F32R)
        XL = sb("x_low", [P, KT, S], F32R)
        YH = sb("y_high", [P, KT, S], F32R)
        YL = sb("y_low", [P, KT, S], F32R)
        RAW = sb("w_raw", [P, RING, CH * NBLK])
        WH = sb("w_high", [P, RING, CH * NBLK], F32R)
        WL = sb("w_low", [P, RING, CH * NBLK], F32R)
        RES = sb("residual", [P, M, D])
        PR = sb("proj", [P, M, 4 * NBLK])
        WK = sb("work", [P, 12 * U])
        ident = sb("ident", [P, P])
        ones = sb("ones", [P, P])
        flip = sb("flip", [P, P])
        upper = sb("upper", [P, P])
        strict = sb("strict", [P, P])
        LV = sb("level_masks", [P, 7, P])
        SY = sb("sym_masks", [P, 6, P])
        CW = sb("conv_cols", [P, 4 * 48])
        NC_ = sb("norm_cols", [P, 40])
        GT = sb("gates", [P, M, 48])
        BIA = sb("gate_bias", [P, 48])
        TI = sb("tanh_if", [P, M, 16])
        NA = sb("neg_abs", [P, M, 32])
        LNB = sb("ln_beta", [P, M, 16])
        LG = sb("log_gates", [P, M, 24])
        EA = sb("exp_alog", [P, 16])
        CS = sb("cumsums", [P, M, 24])
        AS = sb("a_cols", [P, ML_H, M])
        EMT = sb("exp_neg_m", [P, ML_H, M])
        GAM = sb("gamma_cols", [P, DN_H, M])
        EG = sb("exp_gamma", [P, DN_H, M])
        NEB = sb("neg_beta_exp_gamma", [P, DN_H, M])
        HB = sb("half_beta", [P, DN_H, M])
        KD = sb("key_end_decay", [P, DN_H])
        RS = sb("row_sources", [P, M, 40])
        RT = sb("rows", [40, S])
        MT = sb("cummax", [40, S])
        ST = sb("stats", [P, 64])
        BN = sb("bn_stats", [P, M, 4, 6])
        LRT, GW = MT[0:17, :], RT[0:17, :]
        SP_ = ctx.enter_context(nc.psum_tensor("stream_psum", [P, 4, NBLK], F32))
        H = ctx.enter_context(nc.psum_tensor("heads_psum", [P, 4, NBLK], F32))

        EPSC = sb("eps_consts", [P, 5])
        eps_c, eps16_c, eps512_c, eps4_c, epsln_c = [EPSC[:, i:i + 1] for i in range(5)]

        def wk(u, n=U):
            return WK[:, int(u * U):int(u * U) + n]

        loaded = [sem(f"chunk_loaded{i}") for i in range(RING)]
        hi_done, lo_done, used, evac = sem("w_high_done"), sem("w_low_done"), sem("chunk_used"), sem("block_evacuated")
        consts, small_in, x_in = sem("consts"), sem("small_in"), sem("x_in")
        mem_in = [sem(f"mem_half{i}_in") for i in range(2)]
        cols_pe, cols_v = sem("cols_transposed"), sem("cols_copied")
        m_pe = sem("mem_transposed")
        x_pe, x_hi, x_lo = sem("x_transposed"), sem("x_high_done"), sem("x_low_done")
        out_hi, out_lo = sem("y_high_done"), sem("y_low_done")
        m_hi, m_lo = out_hi, out_lo
        mkv_out = [sem(f"mkv_block{b}_stored") for b in range(4)]
        rows_out, rows_in, kv_in = sem("rows_stored"), sem("rows_loaded"), sem("kv_loaded")
        rel_in, rel_s, rel_st, rel_bw, rel_m = [sem(n) for n in ("rel_in", "rel_reversed", "rel_stored", "rel_loaded", "rel_masked")]
        lw_in, gw_in, fin_out = sem("ln_rows_in"), sem("gate_w_in"), sem("out_stored")
        passed = sem("waits_passed")
        g_tanh, norm_s = sem("gates_tanh"), sem("norm_act")

        G_PE = steps_of(sem("gates_pe"), ["gt", "cumsum", "rows", "negm"])
        W_GATE = 4 * 48
        G_ACT = steps_of(sem("gates_act"), ["mini", "tanh", "expf", "lnf", "expab", "lnab", "alog", "eg", "eb",
                                         "hb", "kd", "emt"])
        G_V = steps_of(sem("gates_dve"), ["gt", "bias_if", "bias_a", "negabs", "lnb", "sp", "g", "cs0", "cs1", "as", "gam", "rs0",
                                       "rs1", "rs2", "kd", "rt", "scan", "negm", "ems", "neb", "hb"])
        ML_PE = steps_of(sem("ml_pe"), ["q", "k", "scores", "pv", "out0", "out1"])
        ML_ACT = steps_of(sem("ml_act"), ["to", "tz", "q", "k", "expw", "sq", "ln", "exp"])
        ML_V = steps_of(sem("ml_dve"), ["arg", "g1", "g2", "mask", "p", "den0", "den", "rden", "h", "ss", "fr", "fg"])
        LVS = range(1, 7)
        DN_PE = steps_of(sem("dn_pe"), ["k", "q", "v", "ssk", "k0t", "kk0", "kk1", "ssq", "vt0", "vt1", "x0", "qk0", "qk1"]
                      + [f"{n}{l}{p}" for l in LVS for n in "xt" for p in (0, 1)]
                      + ["u0", "s1", "o0", "qs", "ks", "u1", "o1", "out0", "out1"])
        DN_ACT = steps_of(sem("dn_act"), ["tz", "cv10", "cv11", "cv00", "cv01", "tk", "cv20", "cv21", "args5", "tq", "decay5", "sqk",
                                          "lnk", "expk", "tv", "sqq", "args4", "decay4", "lnq", "expq"]
                          + [f"x{l}{p}" for l in LVS for p in (0, 1)]
                          + ["u0", "s1", "f0", "u1", "sq", "ln", "exp"])

        def conv_names(c):
            return [f"conv{c}{j}{h}" for p in (0, 1) for j in range(1, 4) for h in (2 * p, 2 * p + 1)]

        DN_V = steps_of(sem("dn_dve"), ["g"] + conv_names(1) + conv_names(0) + ["silu1"] + conv_names(2)
                        + ["nk", "silu0", "silu2", "ke", "at0", "at1", "nq", "v0", "v1", "tt0", "qkt0", "qkt1", "t0"]
                        + [f"{k}{l}{p}" for l in LVS for p in (0, 1) for k in (("t", "tt") if l < 6 else ("tt",))]
                        + ["f1a", "r0", "r1", "r2", "r3", "f1b", "ss", "fr", "fg"])
        DN_PL = steps_of(sem("dn_pool"), ["maskr", "maskg"] + [f"ut{l}" for l in range(7)])
        AT_PE = {k: steps_of(sem(f"{k}_pe"), ["k", "q", "scores", "pt", "pv", "out0", "out1"]) for k in "am"}
        AT_ACT = {k: steps_of(sem(f"{k}_act"), ["tz", "q", "exp", "pt"]) for k in "am"}
        AT_V = {k: steps_of(sem(f"{k}_dve"), ["k", "g", "max0", "max1", "neg", "pt", "rs", "f", "fg"]) for k in "am"}
        GL_PE = steps_of(sem("gla_pe"), ["q", "k", "logit", "b", "d"] + [f"l{l}" for l in range(1, 9)] + ["pv", "out0", "out1"])
        GL_ACT = steps_of(sem("gla_act"), ["mini", "tz", "q", "k", "absx", "expx", "lnx", "b"] + [f"e{l}" for l in range(1, 9)]
                       + ["at8", "f", "sq", "ln", "exp"])
        GL_V = steps_of(sem("gla_dve"), ["zero", "g", "lg", "cp00", "cp01"]
                     + [n for l in range(1, 9) for n in (f"d{l}", f"qe{l}") + ((f"cp{l}0", f"cp{l}1") if l < 8 else ())]
                     + ["ss", "fr", "fg"])
        LN_V = steps_of(sem("ln_dve"), [f"st{m}{n}" for n in range(4) for m in range(M)] + [f"ag{m}" for m in range(M)] + ["shift"])
        x_tok, eps_ready, evac_tmp = sem("layer_input_ready"), sem("eps_ready"), sem("gated_product")
        ln_scaled, ln_gamma = sem("ln_scaled"), sem("ln_gamma_done")

        N_MEM = 0
        N_GATE = N_MEM + 4 * NCH
        N_ML = N_GATE + RING
        N_GA = N_ML + 16 * NCH
        N_YA = N_GA + 4 * NCH
        N_DN = N_YA + 4 * NCH
        N_GB = N_DN + 16 * NCH
        N_YB = N_GB + 4 * NCH
        N_L = N_YB + 4 * NCH
        LSZ = 17 * NCH + RING
        L_LR, L_M, L_B, L_A0, L_A1, L_Y1 = 0, RING, RING + 2 * NCH, RING + 5 * NCH, RING + 9 * NCH, RING + 13 * NCH
        Y1_TILES, Y2_TILES = (0, 2, 8, 10, 12, 14), (4, 6)
        L_Y2 = L_Y1 + 4 * len(Y1_TILES)
        LBL = 21
        E_MEM, E_ML, E_GA, E_YA, E_DN, E_GB, E_YB, E_L = 0, 4, 20, 24, 28, 44, 48, 52
        EX_GATE, EX_LR = 48, 16

        def load_count(n, c, extra):
            return n * 4 + (16 * (c // RING) + 16 + extra)

        N_CONSTS = 9 + 3 * (7 + 2 * 6)

        block = ctx.enter_context(nc.Block())

        def wait_alone(eng, sem, value):
            eng.wait_ge(sem, value)
            eng.sem_inc(passed, 1)

        def gap(n):
            for _ in range(n):
                yield

        def advance(side, n=1):
            for _ in range(n):
                next(side, None)

        def finish(side):
            for _ in side:
                pass

        def none():
            return iter(())

        def bank(i, n=1):
            return H[:, i:i + n, :].rearrange("p b n -> p (b n)")

        def cols(ap, n):
            return ap.unsqueeze(len(ap.shape)).broadcast_to(list(ap.shape) + [n])

        def over(ap, k):
            return ap.unsqueeze(1).broadcast_to([ap.shape[0], k, ap.shape[1]])

        def sl(i, n=P):
            return slice(i * n, (i + 1) * n)

        def after_side(eng, q):
            if not (isinstance(q, int) and q == 0):
                eng.wait_ge(out_hi, NCH + 4 * q)
                eng.wait_ge(out_lo, NCH + 4 * q)

        @block.sync
        def _(sp):
            def put(n, c, src, first=False):
                if not (isinstance(n, int) and n + c < RING):
                    wait_alone(sp, lo_done, n + (c - RING + 1))
                sp.dma_start(RAW[:, c % RING, :], src).then_inc(loaded[c % RING], 16)

            def rows_in_chunk(w, off, width, c, cols):
                return bass.AP(w.tensor, off + c * 256 * width, [[width, 256]] + cols)

            def group(n, w, off, width, blocks):
                for b, cols in enumerate(blocks):
                    for c in range(NCH):
                        put(n, b * NCH + c, rows_in_chunk(w, cols[0] + off, width, c, cols[1]))

            def wide(o):
                return (o, [[1, NBLK]])

            def out_group(n, w, off, tiles=tuple(range(0, KT, CH))):
                for b in range(4):
                    for i, kt in enumerate(tiles):
                        put(n, b * len(tiles) + i, bass.AP(w.tensor, off + (kt * P * D + b * NBLK), [[D, P], [P * D, 2], [1, NBLK]]))

            def narrow(n, w, off, width, parts):
                for i in range(RING):
                    wait_alone(sp, lo_done, n + (i - RING + 1))
                    total = sum(k for _, k in parts)
                    dst = RAW[:, i, 0:4 * total].rearrange("p (c j n) -> p c j n", c=2, j=2)
                    for cc in range(2):
                        at = 0
                        for o, k in parts:
                            sp.dma_start(dst[:, cc, :, at:at + k],
                                         bass.AP(w.tensor, off + (o + (2 * i + cc) * 256 * width), [[2 * width, P], [width, 2], [1, k]])
                                         ).then_inc(loaded[i], 16)
                            at += k

            for i in range(2):
                sp.dma_start(PR[:, :, sl(i, D // 2)], mem2[:, :, sl(i, D // 2)]).then_inc(mem_in[i], 16)
            for l in range(2):
                for half in range(2):
                    for c in range(NCH):
                        put(N_MEM, (2 * l + half) * NCH + c, rows_in_chunk(w_mkv, l * D * 1024 + half * NBLK, 1024, c, [[1, NBLK]]))
            narrow(N_GATE, w_in, 0, IN1, [(C_IF, 16), (C_BA, 32)])
            with sp.Fori(0, 4) as g:
                group(N_ML + g * (4 * NCH), w_in, g * 256, IN1, [(C_MLQ, [[C_MLK - C_MLQ, 2], [1, 256]])])
                for b, o in ((1, C_MLO), (2, C_MLZ), (3, C_MLV)):
                    for c in range(NCH):
                        put(N_ML + g * (4 * NCH), b * NCH + c, rows_in_chunk(w_in, g * NBLK + o, IN1, c, [[1, NBLK]]))
            group(N_GA, w_in, 0, IN1, [wide(C_GA + b * NBLK) for b in range(4)])
            out_group(N_YA, w_out, 0)
            with sp.Fori(0, 4) as g:
                group(N_DN + g * (4 * NCH), w_in, g * NBLK, IN1,
                      [wide(C_DN), wide(C_DN + 2048), wide(C_DN + 4096), wide(C_DNZ)])
            group(N_GB, w_in, 0, IN1, [wide(C_GB + b * NBLK) for b in range(4)])
            out_group(N_YB, w_out, D * D)
            with sp.Fori(0, 2) as l:
                n = N_L + l * LSZ
                off = l * (D * IN2)
                narrow(n + L_LR, w_in2, off, IN2, [(C_LR, 16)])
                group(n + L_M, w_in2, off, IN2, [wide(C_MQ), wide(C_MZ)])
                group(n + L_B, w_in2, off, IN2, [wide(C_BQ), wide(C_BZ), wide(C_BV)])
                group(n + L_A0, w_in2, off, IN2, [wide(o) for o in (C_AQ, C_AK, C_AV, C_AZ)])
                group(n + L_A1, w_in2, off, IN2, [wide(o + NBLK) for o in (C_AQ, C_AK, C_AV, C_AZ)])
                out_group(n + L_Y1, w_out2, l * (D * D), Y1_TILES)
                out_group(n + L_Y2, w_out2, l * (D * D), Y2_TILES)
            for i in range(4):
                sp.wait_ge(x_tok, 2 * NCH + 2 * (i + 1))
                sp.dma_start(out2[:, :, sl(i, NBLK)], RES[:, :, sl(i, NBLK)]).then_inc(fin_out, 16)
            sp.wait_ge(fin_out, 64)

        @block.gpsimd
        def _(pool):
            k = [0]

            def c(ins):
                k[0] += 1
                ins.then_inc(consts, 1)
                pool.wait_ge(consts, k[0])

            c(pool.memset(ident[:], 0.0))
            c(pool.affine_select(out=ident[:], in_=ident[:], compare_op=ALU.not_equal, fill=1.0, base=0,
                                 pattern=[[-1, P]], channel_multiplier=1))
            pool.dma_start(wk(8, 256)[0:8, :], norm_w.rearrange("a (c n) -> (a c) n", n=256)).then_inc(small_in, 16)
            pool.dma_start(wk(8.25, P)[0:16, :], ml_norm_w.rearrange("a (c n) -> (a c) n", n=P)).then_inc(small_in, 16)
            pool.dma_start(wk(8.5, P)[0:1, :], dn_norm_w).then_inc(small_in, 16)
            pool.dma_start(wk(8.75, P)[0:2, :], gla_g).then_inc(small_in, 16)
            for i in range(2):
                pool.dma_start(wk(9 + i / 8, P)[0:96, :], bass.AP(dn_conv_w.tensor, i * 2 * 6144, [[P, 96], [1, P]])).then_inc(small_in, 16)
            for o, t, n in ((0, ml_i_bias, 8), (8, ml_f_bias, 8), (16, dn_dt_bias, 16), (32, dn_a_log, 16)):
                pool.dma_start(BIA[:, o:o + n], bass.AP(t.tensor, 0, [[0, P], [1, n]])).then_inc(small_in, 16)
            c(pool.memset(ones[:], 1.0))
            c(pool.memset(flip[:], 0.0))
            c(pool.affine_select(out=flip[:], in_=flip[:], compare_op=ALU.not_equal, fill=1.0, base=1 - P,
                                 pattern=[[1, P]], channel_multiplier=1))
            c(pool.affine_select(out=upper[:], in_=ones[:], compare_op=ALU.is_ge, fill=0.0, base=0,
                                 pattern=[[1, P]], channel_multiplier=-1))
            c(pool.affine_select(out=strict[:], in_=ones[:], compare_op=ALU.is_gt, fill=0.0, base=0,
                                 pattern=[[1, P]], channel_multiplier=-1))
            c(pool.memset(LV[:], 0.0))
            c(pool.memset(SY[:], 0.0))

            def half_mask(m, l, right, rows_right):
                size, hf = 2 ** (l + 1), 2 ** l
                v = m.rearrange("p (n s h) -> p n s h", s=2, h=hf)[:, :, 1 if right else 0, :]
                lo = hf if rows_right else 0
                c(pool.memset(v, 1.0))
                c(pool.affine_select(out=v, in_=v, compare_op=ALU.is_ge, fill=0.0, base=-lo,
                                     pattern=[[-size, P // size], [0, hf]], channel_multiplier=1))
                c(pool.affine_select(out=v, in_=v, compare_op=ALU.is_ge, fill=0.0, base=lo + hf - 1,
                                     pattern=[[size, P // size], [0, hf]], channel_multiplier=-1))

            for l in range(7):
                half_mask(LV[:, l, :], l, True, False)
            for l in range(6):
                half_mask(SY[:, l, :], l, True, False)
                half_mask(SY[:, l, :], l, False, True)

            assert k[0] == N_CONSTS

            for b in range(4):
                pool.wait_ge(evac, 2 * (E_MEM + b) + 2)
                pool.dma_start(mkv_d.rearrange("(m p) n -> p m n", p=P)[:, :, b * NBLK:(b + 1) * NBLK],
                               PR[:, :, b * NBLK:(b + 1) * NBLK]).then_inc(mkv_out[b], 16)
            pool.wait_ge(*done(G_V, "negm"))
            pool.dma_start(rows_d, RT[:, :]).then_inc(rows_out, 16)
            pool.wait_ge(rows_out, 16)

            def ml_rows(g):
                pool.dma_start(wk(1, 2 * S), bass.AP(rows_d.tensor, g * (2 * S) + 32 * S, [[0, P], [1, 2 * S]])).then_inc(rows_in, 16)

            def dn_rows(g):
                for i in range(2):
                    pool.dma_start(wk(4 + i), bass.AP(rows_d.tensor, g * (4 * S) + i * 16 * S, [[0, P], [1, 4 * S]])).then_inc(rows_in, 16)

            ml_rows(0)
            with pool.Fori(1, 4) as g:
                wait_alone(pool, *done(ML_V, "arg", g - 1))
                ml_rows(g)
            pool.wait_ge(out_lo, NCH + 16)
            pool.wait_ge(out_hi, NCH + 16)
            dn_rows(0)

            def dn_masks(g):
                ptt = pool.tensor_tensor
                a, ut = wk(5).rearrange("p (s t) -> p s t", t=P), wk(8).rearrange("p (s t) -> p s t", t=P)
                qk = wk(4).rearrange("p (s t) -> p s t", t=P)
                pool.wait_ge(*done(DN_ACT, "decay5", g))
                ptt(a, a, over(strict[:], 8), ALU.mult).then_inc(*signal(DN_PL, "maskr"))
                pool.wait_ge(*done(DN_ACT, "decay4", g))
                ptt(qk, qk, over(upper[:], 8), ALU.mult).then_inc(*signal(DN_PL, "maskg"))
                for l in range(7):
                    if l == 0:
                        pool.wait_ge(*done(DN_V, "at1", g))
                    elif l == 1:
                        pool.wait_ge(*done(DN_V, "tt0", g))
                        pool.wait_ge(*done(DN_PE, "x0", g))
                    else:
                        pool.wait_ge(*done(DN_PE, f"x{l - 1}1", g))
                    ptt(ut, a, over(LV[:, l, :], 8), ALU.mult).then_inc(*signal(DN_PL, f"ut{l}"))

            with pool.Fori(0, 3) as g:
                dn_masks(g)
                wait_alone(pool, *done(DN_PE, "o1", g))
                dn_rows(g + 1)
            dn_masks(3)
            pool.wait_ge(out_lo, NCH + 32)
            pool.wait_ge(out_hi, NCH + 32)
            pool.dma_start(wk(0, D), bass.AP(final_norm_w.tensor, 0, [[0, P], [1, D]])).then_inc(lw_in, 16)

            with pool.Fori(0, 2) as l:
                pool.dma_start(wk(9, 2 * U).rearrange("p (m n) -> p m n", m=M),
                               mkv_d.rearrange("(m p) n -> p m n", p=P)[:, :, bass.ds(l * 1024, 1024)]).then_inc(kv_in, 16)
                pool.dma_start(RT[0:16, :], bass.AP(gate_w.tensor, l * (16 * S), [[S, 16], [1, S]])).then_inc(gw_in, 16)
                pool.dma_start(RT[16:17, :], bass.AP(gate_b.tensor, l * S, [[S, 1], [1, S]])).then_inc(gw_in, 16)
                pool.dma_start(wk(6, 257)[0:8, :], bass.AP(rel.tensor, l * (8 * 257), [[257, 8], [1, 257]])).then_inc(rel_in, 16)
                wait_alone(pool, rel_s, l * 2 + 2)
                pool.dma_start(rel_d, wk(6.5, BIASW)[0:8, :]).then_inc(rel_st, 16)
                pool.wait_ge(rel_st, l * 16 + 16)
                wait_alone(pool, out_lo, NCH + (l * 16 + 36))
                wait_alone(pool, out_hi, NCH + (l * 16 + 36))
                pool.dma_start(wk(9, 3 * U).rearrange("p (h n) -> p h n", h=A_H)[:, :, P:BIASW],
                               bass.AP(rel_d.tensor, 0, [[1, P], [BIASW, A_H], [1, S]])).then_inc(rel_bw, 16)
                wait_alone(pool, out_lo, NCH + (l * 16 + 48))
                wait_alone(pool, out_hi, NCH + (l * 16 + 48))
                pool.dma_start(wk(0, D), bass.AP(ln_g.tensor, l * D, [[0, P], [1, D]])).then_inc(lw_in, 16)
                pool.dma_start(wk(2, D), bass.AP(ln_b.tensor, l * D, [[0, P], [1, D]])).then_inc(lw_in, 16)
                pool.wait_ge(lw_in, 32 * l + 48)
                for c in range(NCH):
                    pool.wait_ge(ln_gamma, l * 8 + (c + 1))
                    r = RES[:, :, sl(c, S)]
                    pool.tensor_tensor(r, r, over(wk(2, D)[:, sl(c, S)], M), ALU.add).then_inc(x_tok, 1)

        @block.tensor
        def _(pe):
            def tr(dst, src, n=P, b0=0):
                return pe.transpose(dst, src, ident[b0:b0 + n, b0:b0 + n])

            def stream(n, blocks_before, nblk, hi, lo, side, first_need=None, tiles=tuple(range(0, KT, CH)), small=None):
                per = len(tiles)
                for b in range(nblk):
                    need = 2 * (blocks_before + b - 1) if first_need is None or b else 2 * first_need
                    if not (isinstance(need, int) and need <= 0):
                        pe.wait_ge(evac, need)
                    if b == 1 and small:
                        pe.wait_ge(*small)
                    pair = 2 * (b % 2)
                    for c in range(per):
                        i = b * per + c
                        pe.wait_ge(lo_done, n + (i + 1))
                        for kk in range(CH):
                            k = tiles[c] + kk
                            first, final = (c, kk) == (0, 0), (c, kk) == (per - 1, CH - 1)
                            w, wl = WH[:, i % RING, sl(kk, NBLK)], WL[:, i % RING, sl(kk, NBLK)]
                            for m in range(M):
                                acc = SP_[:, pair + m, :]
                                pe.matmul(acc, hi[:, k, sl(m)], w, start=first, stop=False)
                                pe.matmul(acc, hi[:, k, sl(m)], wl, start=False, stop=False)
                                last = pe.matmul(acc, lo[:, k, sl(m)], w, start=False, stop=final)
                            if kk == CH - 1:
                                last.then_inc(used, 1)
                            advance(side)
                finish(side)

            def small_block(n, width, x_before):
                acc = SP_[0:width, 2, 0:S]
                for i in range(RING):
                    pe.wait_ge(x_lo, x_before + (4 * i + 4))
                    pe.wait_ge(lo_done, n + (i + 1))
                    for t in range(4):
                        k = 4 * i + t
                        w, wl = WH[:, i, sl(t, width)], WL[:, i, sl(t, width)]
                        pe.matmul(acc, w, XH[:, k, :], start=(k == 0), stop=False)
                        pe.matmul(acc, w, XL[:, k, :], start=False, stop=False)
                        last = pe.matmul(acc, wl, XH[:, k, :], start=False, stop=(k == KT - 1))
                    last.then_inc(used, 1)

            def feature_tiles(src, count, through, before, ready=None, second=None):
                for c in range(NCH):
                    if c >= 4:
                        pe.wait_ge(count[0], count[1] * (c - 3) + before)
                    if second and c == NCH // 2:
                        pe.wait_ge(*second)
                    if ready:
                        pe.wait_ge(ready[0], ready[1] + (c + 1))
                    v = src[:, :, sl(c, 2 * P)].rearrange("p m (q j) -> p m q j", j=2)
                    for j in range(2):
                        for m in range(M):
                            last = tr(H[:, c % 4, j * S + m * P:j * S + (m + 1) * P], v[:, m, :, j])
                    last.then_inc(through, 1)
                    yield

            def x_prep():
                yield from gap(3)
                pe.wait_ge(small_in, 16 * 10)
                pe.wait_ge(m_lo, NCH)
                for i in range(2):
                    tr(H[:, 0, sl(i, 96)], wk(9 + i / 8, P)[0:96, :], 96)
                for j in range(2):
                    tr(H[:, 0, 192 + 8 * j:200 + 8 * j], wk(8, 256)[0:8, :].rearrange("c (q j) -> c q j", j=2)[:, :, j], 8)
                tr(H[:, 0, 208:224], wk(8.25, P)[0:16, :], 16)
                tr(H[:, 0, 224:225], wk(8.5, P)[0:1, :], 1)
                tr(H[:, 0, 226:228], wk(8.75, P)[0:2, :], 2).then_inc(cols_pe, 1)
                yield from gap(9)
                pe.wait_ge(cols_v, 5)
                pe.wait_ge(norm_s, 5)
                yield from feature_tiles(wk(0, 4 * U).rearrange("p (m d) -> p m d", m=M), (x_lo, 2), x_pe, 0)

            def gates():
                pe.wait_ge(*done(G_ACT, "mini"))
                for m in range(M):
                    last = tr(H[:, 0, sl(m, 48)], wk(11, S)[0:48, sl(m)], 48)
                last.then_inc(*signal(G_PE, "gt"))
                yield from gap(5)
                pe.wait_ge(*done(G_V, "g"))
                for z, w, first in ((0, LG[:, 0, :], True), (40, LG[:, 1, 8:24], True)):
                    pe.matmul(H[:, 2, z:z + w.shape[1]], upper[:], w, start=True, stop=True)
                pe.matmul(H[:, 2, 32:40], upper[:], LG[:, 1, 0:8], start=True, stop=False)
                pe.matmul(H[:, 2, 32:40], ones[:], LG[:, 0, 0:8], start=False, stop=True)
                pe.matmul(H[:, 2, 64:80], ones[:], LG[:, 0, 8:24], start=True, stop=True).then_inc(*signal(G_PE, "cumsum"))
                yield from gap(4)
                pe.wait_ge(*done(G_V, "rs2"))
                for m in range(M):
                    last = tr(H[0:40, 3, sl(m)], RS[:, m, :])
                last.then_inc(*signal(G_PE, "rows"))
                yield from gap(4)
                pe.wait_ge(*done(G_V, "negm"))
                for m in range(M):
                    last = tr(H[:, 0, 8 * m:8 * m + 8], RT[32:40, sl(m)], 8, 32)
                last.then_inc(*signal(G_PE, "negm"))
                yield

            def outputs(steps, fin, F, b0):
                pe.wait_ge(*fin)
                for j in range(4):
                    for m in range(M):
                        last = tr(H[:, b0 + j // 2, (j % 2) * S + m * P:(j % 2) * S + (m + 1) * P], F[:, m, sl(j)])
                    if j % 2:
                        last.then_inc(*signal(steps, f"out{j // 2}"))
                yield

            def ml(g):
                yield from gap(2)
                after_side(pe, g)
                pe.wait_ge(evac, 8 * g + (2 * (E_ML + 4)))
                for i, n in enumerate("qk"):
                    for h in range(2):
                        for m in range(M):
                            last = tr(H[:, i, h * S + m * P:h * S + (m + 1) * P], PR[:, m, i * S + h * P:i * S + (h + 1) * P])
                    last.then_inc(*signal(ML_PE, n))
                yield from gap(3)
                q, k, w, F = wk(0, 512), wk(0.5, 512), wk(2, 768), wk(10)
                pe.wait_ge(*done(ML_ACT, "k", g))
                for h in range(2):
                    pe.matmul(H[:, 2 + h, 0:S], k[:, h * S:h * S + P], q[:, sl(h, S)], start=True, stop=True)
                    last = pe.matmul(H[:, 2 + h, S:S + P], k[:, h * S + P:(h + 1) * S], q[:, h * S + P:(h + 1) * S], start=True, stop=True)
                last.then_inc(*signal(ML_PE, "scores"))
                yield from gap(4)
                pe.wait_ge(*done(ML_V, "p", g))
                for h in range(2):
                    for m in range(M):
                        for s in range(m + 1):
                            pt = w[:, h * 384 + s * S + (m - s) * P:h * 384 + s * S + (m - s + 1) * P]
                            pe.matmul(H[:, h, sl(m, S)], pt, PR[:, s, 3 * NBLK + h * S:3 * NBLK + (h + 1) * S], start=(s == 0), stop=(s == m))
                        for s in range(m + 1):
                            pt = w[:, h * 384 + s * S + (m - s) * P:h * 384 + s * S + (m - s + 1) * P]
                            last = pe.matmul(H[:, 2, 2 * h + m:2 * h + m + 1], pt, ones[:, 0:1], start=(s == 0), stop=(s == m))
                last.then_inc(*signal(ML_PE, "pv"))
                yield from gap(8)
                yield from outputs(ML_PE, done(ML_V, "fg", g), F.rearrange("p (m n) -> p m n", m=M), 0)

            def dn(g):
                yield
                after_side(pe, g + 4)
                pe.wait_ge(evac, 8 * g + (2 * (E_DN + 4)))
                CV = wk(0, 3 * U).rearrange("p (c h t) -> p c h t", c=3, h=4)
                QKd = wk(4).rearrange("p (h m t) -> p h m t", h=4, m=M)
                T = wk(6).rearrange("p (h m t) -> p h m t", h=4, m=M)
                TT = wk(7).rearrange("p (h m t) -> p h m t", h=4, m=M)
                UT = wk(8).rearrange("p (h m t) -> p h m t", h=4, m=M)
                X = wk(3).rearrange("p (h m t) -> p h m t", h=4, m=M)
                V = wk(2).rearrange("p (h m t) -> p h m t", h=4, m=M)
                KE = wk(11, 512).rearrange("p (h t) -> p h t", h=4)
                S1 = wk(11.5, 512).rearrange("p (h t) -> p h t", h=4)

                def project(c, b0):
                    for h in range(4):
                        for m in range(M):
                            last = tr(H[:, b0 + h // 2, (h % 2) * S + m * P:(h % 2) * S + (m + 1) * P], PR[:, m, c * NBLK + h * P:c * NBLK + (h + 1) * P])
                    return last

                project(1, 0).then_inc(*signal(DN_PE, "k"))
                yield
                project(0, 2).then_inc(*signal(DN_PE, "q"))
                yield from gap(6)
                pe.wait_ge(*done(DN_V, "conv133", g))
                project(2, 0).then_inc(*signal(DN_PE, "v"))
                yield from gap(9)
                pe.wait_ge(*done(DN_ACT, "sqk", g))
                pe.wait_ge(*done(DN_V, "conv033", g))
                for i in range(2):
                    last = pe.matmul(H[:, 2 + i, :], ones[:], wk(7 + i / 2, 512), start=True, stop=True)
                last.then_inc(*signal(DN_PE, "ssk"))
                yield from gap(6)
                pe.wait_ge(*done(DN_V, "nk", g))
                for h in range(4):
                    last = tr(H[:, 2, sl(h)], CV[:, 1, h, 0:P])
                last.then_inc(*signal(DN_PE, "k0t"))
                yield from gap(2)

                def products(name, b0, c):
                    for p in range(2):
                        for h in (0, 1):
                            for m in range(M):
                                last = pe.matmul(H[:, b0 + p, sl(2 * h + m)], CV[:, 1, 2 * p + h, sl(m)], CV[:, c, 2 * p + h, sl(m)],
                                                 start=True, stop=True)
                        last.then_inc(*signal(DN_PE, f"{name}{p}"))

                pe.wait_ge(*done(DN_V, "conv233", g))
                products("kk", 0, 1)
                yield
                pe.wait_ge(*done(DN_ACT, "sqq", g))
                pe.wait_ge(*done(DN_V, "ke", g))
                for i in range(2):
                    last = pe.matmul(H[:, 2 + i, :], ones[:], wk(6 + i / 2, 512), start=True, stop=True)
                last.then_inc(*signal(DN_PE, "ssq"))
                yield from gap(2)
                pe.wait_ge(*done(DN_V, "silu2", g))
                pe.wait_ge(*done(DN_ACT, "lnq", g))
                for p in range(2):
                    for h in (0, 1):
                        for m in range(M):
                            last = tr(H[:, 2 + p, sl(2 * h + m)], CV[:, 2, 2 * p + h, sl(m)])
                    last.then_inc(*signal(DN_PE, f"vt{p}"))
                yield from gap(2)
                pe.wait_ge(*done(DN_V, "at1", g))
                pe.wait_ge(*done(DN_PL, "ut0", g))
                for i in range(8):
                    last = tr(H[:, i // 4, sl(i % 4)], UT[:, i // 2, i % 2, :])
                last.then_inc(*signal(DN_PE, "x0"))
                yield
                pe.wait_ge(*done(DN_V, "v1", g))
                products("qk", 2, 0)
                yield from gap(3)
                for l in LVS:
                    for p in range(2):
                        pe.wait_ge(*(done(DN_V, "t0", g) if l == 1 else done(DN_V, f"tt{l - 1}{p}", g)))
                        pe.wait_ge(*done(DN_PL, f"ut{l}", g))
                        for i in range(4 * p, 4 * p + 4):
                            last = pe.matmul(H[:, p, sl(i % 4)], UT[:, i // 2, i % 2, :], T[:, i // 2, i % 2, :], start=True, stop=True)
                        last.then_inc(*signal(DN_PE, f"x{l}{p}"))
                    yield
                    for p in range(2):
                        pe.wait_ge(*done(DN_ACT, f"x{l}{p}", g))
                        if l == 1:
                            pe.wait_ge(*done(DN_V, "qkt1", g))
                        for i in range(4 * p, 4 * p + 4):
                            h, m = i // 2, i % 2
                            if l < 6:
                                pe.matmul(H[:, p, sl(i % 4)], TT[:, h, m, :], X[:, h, m, :], start=True, stop=True)
                            last = pe.matmul(H[:, 2 + p, sl(i % 4)], X[:, h, m, :], TT[:, h, m, :], start=True, stop=True)
                        last.then_inc(*signal(DN_PE, f"t{l}{p}"))
                    yield from gap(2)
                pe.wait_ge(*done(DN_V, "tt61", g))
                for h in range(4):
                    last = pe.matmul(H[:, 0, sl(h)], TT[:, h, 0, :], V[:, h, 0, :], start=True, stop=True)
                last.then_inc(*signal(DN_PE, "u0"))
                yield
                pe.wait_ge(*done(DN_ACT, "u0", g))
                for h in range(4):
                    last = pe.matmul(H[:, 1, sl(h)], KE[:, h, :], UT[:, h, 0, :], start=True, stop=True)
                last.then_inc(*signal(DN_PE, "s1"))
                for h in range(4):
                    last = pe.matmul(H[:, 0, sl(h)], QKd[:, h, 0, :], UT[:, h, 0, :], start=True, stop=True)
                last.then_inc(*signal(DN_PE, "o0"))
                yield
                pe.wait_ge(*done(DN_ACT, "s1", g))
                for c, b, n in ((0, 3, "qs"), (1, 2, "ks")):
                    for h in range(4):
                        last = pe.matmul(H[:, b, sl(h)], CV[:, c, h, P:S], S1[:, h, :], start=True, stop=True)
                    last.then_inc(*signal(DN_PE, n))
                yield
                pe.wait_ge(*done(DN_V, "r3", g))
                for h in range(4):
                    last = pe.matmul(H[:, 1, sl(h)], TT[:, h, 1, :], V[:, h, 1, :], start=True, stop=True)
                last.then_inc(*signal(DN_PE, "u1"))
                yield
                pe.wait_ge(*done(DN_ACT, "u1", g))
                for h in range(4):
                    last = pe.matmul(H[:, 0, sl(h)], QKd[:, h, 1, :], UT[:, h, 1, :], start=True, stop=True)
                last.then_inc(*signal(DN_PE, "o1"))
                yield from gap(6)
                yield from outputs(DN_PE, done(DN_V, "fg", g), wk(10).rearrange("p (m n) -> p m n", m=M), 2)

            def attend(kind, q, n, evac_need, h0=0, rel_need=None):
                steps, act, dve = AT_PE[kind], AT_ACT[kind], AT_V[kind]
                yield from gap(2)
                after_side(pe, q)
                pe.wait_ge(evac, evac_need)
                if kind == "m":
                    pe.wait_ge(kv_in, (q - 8) * 4 + 16)
                    ksrc = wk(9, 2 * U).rearrange("p (m n) -> p m n", m=M)
                    vsrc = ksrc[:, :, NBLK:]
                else:
                    ksrc, vsrc = PR[:, :, NBLK:2 * NBLK], PR[:, :, 2 * NBLK:3 * NBLK]
                for name, src, b0 in (("k", ksrc, 0), ("q", PR, 2)):
                    for h in range(4):
                        for m in range(M):
                            last = tr(H[:, b0 + h // 2, (h % 2) * S + m * P:(h % 2) * S + (m + 1) * P], src[:, m, sl(h)])
                    last.then_inc(*signal(steps, name))
                yield from gap(2)
                full = kind == "m"
                w = 512 if full else BIASW
                qT, kT = wk(0), wk(1)
                SC, PT = wk(2, 4 * w), wk(4, 4 * w)
                pe.wait_ge(*done(act, "q", n))
                pe.wait_ge(*done(dve, "k", n))
                if not full:
                    pe.wait_ge(rel_m, rel_need)
                for h in range(4):
                    n0 = S if full else P
                    for m, a, b in ((0, 0, n0), (1, n0, n0 + S)):
                        last = pe.matmul(H[:, h, a:b], qT[:, h * S + m * P:h * S + (m + 1) * P], kT[:, h * S:h * S + b - a], start=True, stop=full)
                        if not full:
                            last = pe.matmul(H[:, h, a:b], flip[:], wk(9, 3 * U)[:, (h0 + h) * BIASW + a:(h0 + h) * BIASW + b], start=False, stop=True)
                last.then_inc(*signal(steps, "scores"))
                yield from gap(6)
                pe.wait_ge(*done(act, "exp", n))
                for h in range(4):
                    if full:
                        for i in range(4):
                            last = tr(H[:, h, sl(i)], SC[:, h * w + i * P:h * w + (i + 1) * P])
                    else:
                        for i in range(3):
                            last = tr(H[:, h, sl(i)], SC[:, h * w + i * P:h * w + (i + 1) * P])
                last.then_inc(*signal(steps, "pt"))
                yield from gap(2)
                pe.wait_ge(*done(act, "pt", n))
                pe.wait_ge(*done(dve, "pt", n))
                parts = {0: ((0, 0), (1, 1)), 1: ((2, 0), (3, 1))} if full else {0: ((0, 0),), 1: ((1, 0), (2, 1))}
                for m in range(M):
                    for h in range(4):
                        for i, (blk, s) in enumerate(parts[m]):
                            last = pe.matmul(H[:, m, sl(h)], PT[:, h * w + blk * P:h * w + (blk + 1) * P], vsrc[:, s, sl(h)],
                                             start=(i == 0), stop=(i == len(parts[m]) - 1))
                last.then_inc(*signal(steps, "pv"))
                yield from gap(3)
                yield from outputs(steps, done(dve, "fg", n), wk(7).rearrange("p (m n) -> p m n", m=M), 2)

            def gla(l, q, evac_need):
                yield from gap(2)
                after_side(pe, q)
                pe.wait_ge(evac, evac_need)
                for i, name in enumerate("qk"):
                    for hp in range(2):
                        for m in range(M):
                            last = tr(H[:, i, hp * S + m * P:hp * S + (m + 1) * P], PR[:, m, i * S + hp * P:i * S + (hp + 1) * P])
                    last.then_inc(*signal(GL_PE, name))
                yield from gap(2)
                pe.wait_ge(gw_in, l * 32 + 32)
                for m in range(M):
                    last = pe.matmul(H[:, 3, sl(m, S)], LRT[:, sl(m)], GW, start=True, stop=True)
                last.then_inc(*signal(GL_PE, "logit"))
                yield from gap(3)
                LGG = wk(3.5, 512).rearrange("p (m n) -> p m n", m=M)
                pe.wait_ge(*done(GL_V, "lg", l))
                for hp in range(2):
                    pe.matmul(H[:, 2, hp * S:hp * S + P], LGG[:, 0, sl(hp)], upper[:], start=True, stop=True)
                    pe.matmul(H[:, 2, hp * S + P:(hp + 1) * S], LGG[:, 0, sl(hp)], ones[:], start=True, stop=False)
                    last = pe.matmul(H[:, 2, hp * S + P:(hp + 1) * S], LGG[:, 1, sl(hp)], upper[:], start=False, stop=True)
                last.then_inc(*signal(GL_PE, "b"))
                yield
                pe.wait_ge(*done(GL_ACT, "k", l))

                def pairs(QK, b, tiles):
                    for par in range(2):
                        for hh in range(2):
                            for i, (ms, mt) in enumerate(tiles):
                                r = slice(64 * par, 64 * par + 64)
                                last = pe.matmul(H[:, b + par, sl(hh * len(tiles) + i)], QK[r, 512 + hh * S + ms * P:512 + hh * S + (ms + 1) * P],
                                                 QK[r, hh * S + mt * P:hh * S + (mt + 1) * P], start=True, stop=True)
                    return last

                diagonal = ((0, 0), (1, 1))
                pairs(wk(0), 0, diagonal).then_inc(*signal(GL_PE, "d"))
                yield from gap(4)
                for lv in range(1, 9):
                    pe.wait_ge(*done(GL_V, f"qe{lv}", l))
                    if lv >= 3:
                        pe.wait_ge(*done(GL_V, f"cp{lv - 2}1", l))
                    elif lv == 2:
                        pe.wait_ge(*done(GL_V, "cp01", l))
                    pairs(wk(1 + lv % 2), 2 * (lv % 2), diagonal if lv < 8 else ((0, 1),)).then_inc(*signal(GL_PE, f"l{lv}"))
                    yield from gap(5)
                A = wk(5, 1536).rearrange("p (c h t) -> p c h t", c=3, h=4)
                pe.wait_ge(*done(GL_V, "cp71", l))
                pe.wait_ge(*done(GL_ACT, "at8", l))
                v = PR[:, :, 3 * NBLK:4 * NBLK]
                for m in range(M):
                    for h in range(4):
                        if m == 0:
                            last = pe.matmul(H[:, 2, sl(h)], A[:, 0, h, :], v[:, 0, sl(h)], start=True, stop=True)
                        else:
                            pe.matmul(H[:, 3, sl(h)], A[:, 2, h, :], v[:, 0, sl(h)], start=True, stop=False)
                            last = pe.matmul(H[:, 3, sl(h)], A[:, 1, h, :], v[:, 1, sl(h)], start=False, stop=True)
                last.then_inc(*signal(GL_PE, "pv"))
                yield from gap(5)
                yield from outputs(GL_PE, done(GL_V, "fg", l), wk(7).rearrange("p (m n) -> p m n", m=M), 0)

            pe.wait_ge(mem_in[0], 16)
            pe.wait_ge(consts, 2)
            finish(feature_tiles(PR, (m_lo, 1), m_pe, 0, second=(mem_in[1], 16)))
            pe.wait_ge(m_lo, NCH)
            stream(N_MEM, E_MEM, 4, YH, YL, x_prep())
            pe.wait_ge(evac, 2 * E_ML)
            small_block(N_GATE, 48, 0)
            pe.wait_ge(consts, N_CONSTS)
            stream(N_ML, E_ML, 4, XH, XL, gates(), small=done(G_ACT, "mini"))
            with pe.Fori(1, 4) as g:
                stream(N_ML + g * (4 * NCH), E_ML + 4 * g, 4, XH, XL, ml(g - 1))
            stream(N_GA, E_GA, 4, XH, XL, ml(3))
            pe.wait_ge(out_lo, NCH + 16)
            stream(N_YA, E_YA, 4, YH, YL, none())
            stream(N_DN, E_DN, 4, XH, XL, none())
            with pe.Fori(1, 4) as g:
                stream(N_DN + g * (4 * NCH), E_DN + 4 * g, 4, XH, XL, dn(g - 1))
            stream(N_GB, E_GB, 4, XH, XL, dn(3))
            pe.wait_ge(out_lo, NCH + 32)
            stream(N_YB, E_YB, 4, YH, YL, none())
            with pe.Fori(0, 2) as l:
                n, e, q = N_L + l * LSZ, E_L + l * LBL, 8 + 4 * l
                pe.wait_ge(out_lo, NCH + 4 * q)
                finish(feature_tiles(RES, (x_lo, 2), x_pe, 16 * l + 16, (x_tok, 8 * l)))
                small_block(n + L_LR, 16, 16 * l + 16)
                stream(n + L_M, e, 2, XH, XL, none(), first_need=e, small=done(GL_ACT, "mini", l))
                stream(n + L_B, e + 2, 3, XH, XL, attend("m", q, l, 2 * (e + 2)))
                stream(n + L_A0, e + 5, 4, XH, XL, gla(l, q + 1, 2 * (e + 5)), first_need=e + 5)
                stream(n + L_A1, e + 9, 4, XH, XL, attend("a", q + 2, 2 * l, 2 * (e + 9), 0, l * 3 + 3))
                pe.wait_ge(out_lo, NCH + (4 * q + 12))
                stream(n + L_Y1, e + 13, 4, YH, YL, attend("a", q + 3, 2 * l + 1, 2 * (e + 13), 4, l * 3 + 3), tiles=Y1_TILES)
                pe.wait_ge(out_lo, NCH + (4 * q + 16))
                stream(n + L_Y2, e + 17, 4, YH, YL, none(), tiles=Y2_TILES)

        @block.scalar
        def _(act):
            def f(dst, src, func, **kw):
                return act.activation(dst, src, func, **kw)

            def high(n, c, extra, width=CH * NBLK):
                act.wait_ge(loaded[c % RING], load_count(n, c, extra))
                if not (isinstance(n, int) and n + c < RING):
                    act.wait_ge(used, n + (c - RING + 1))
                f(WH[:, c % RING, 0:width], RAW[:, c % RING, 0:width], ACT.Copy).then_inc(hi_done, 1)

            def stream(n, nblk, extra, side, slots=(0, 1, 2, 3), free=(), ahead=(CH * NBLK, 0), per=NCH):
                for b in range(nblk):
                    for c in range(per):
                        i = b * per + c + AHEAD
                        if i < nblk * per:
                            high(n, i, extra)
                        elif ahead:
                            high(n, i, extra + ahead[1], ahead[0])
                        advance(side, 2)
                    if slots is None:
                        continue
                    if b < len(free):
                        for w in free[b]:
                            act.wait_ge(*w)
                    act.wait_ge(used, n + (b + 1) * per)
                    for m in range(M):
                        f(PR[:, m, sl(slots[b], NBLK)], SP_[:, 2 * (b % 2) + m, :], ACT.Copy).then_inc(evac, 1)
                finish(side)

            def small_block(n, extra, width, steps, dst, own):
                for i in range(AHEAD, RING):
                    high(n, i, extra + own, 4 * width)
                for i in range(AHEAD):
                    high(n, RING + i, extra + own)
                act.wait_ge(used, n + RING)
                f(dst, SP_[0:width, 2, 0:S], ACT.Copy).then_inc(*signal(steps, "mini"))

            def x_prep():
                yield from gap(3)
                act.wait_ge(m_lo, NCH)
                act.wait_ge(x_in, 16)
                for m in range(M):
                    f(wk(4, D), RES[:, m, :], ACT.Square, accum_out=ST[:, m:m + 1]).then_inc(norm_s, 1)
                    act.wait_ge(norm_s, m + 1)
                yield
                f(ST[:, 2:4], ST[:, 0:2], ACT.Ln, scale=1.0 / D, bias=eps_c).then_inc(norm_s, 1)
                act.wait_ge(norm_s, 3)
                f(ST[:, 4:6], ST[:, 2:4], ACT.Exp, scale=-0.5).then_inc(norm_s, 1)
                act.wait_ge(norm_s, 4)
                yield from gap(2)
                act.wait_ge(cols_v, 5)
                for m in range(M):
                    last = f(wk(2 * m, D), RES[:, m, :], ACT.Copy, scale=ST[:, 4 + m:5 + m])
                last.then_inc(norm_s, 1)
                yield from gap(5)
                for c in range(NCH):
                    act.wait_ge(x_pe, c + 1)
                    for j in range(2):
                        k = 2 * c + j
                        f(XH[:, k, :], H[:, c % 4, sl(j, S)], ACT.Copy, scale=NC_[:, k:k + 1]).then_inc(x_hi, 1)
                    yield

            def gates():
                act.wait_ge(*done(G_V, "bias_if"))
                f(TI[:], GT[:, :, 0:16], ACT.Tanh, scale=1.0 / 15).then_inc(*signal(G_ACT, "tanh"))
                act.wait_ge(*done(G_ACT, "tanh"))
                f(LG[:, :, 0:8], TI[:, :, 8:16], ACT.Exp, scale=-15.0).then_inc(*signal(G_ACT, "expf"))
                act.wait_ge(*done(G_ACT, "expf"))
                f(LG[:, :, 0:8], LG[:, :, 0:8], ACT.Ln, bias=1.0).then_inc(*signal(G_ACT, "lnf"))
                act.wait_ge(*done(G_V, "negabs"))
                f(NA[:], NA[:], ACT.Exp).then_inc(*signal(G_ACT, "expab"))
                act.wait_ge(*done(G_ACT, "expab"))
                f(NA[:], NA[:], ACT.Ln, bias=1.0).then_inc(*signal(G_ACT, "lnab"))
                f(EA[:], BIA[:, 32:48], ACT.Exp).then_inc(*signal(G_ACT, "alog"))
                yield from gap(6)
                act.wait_ge(*done(G_V, "kd"))
                f(EG[:], GAM[:], ACT.Exp).then_inc(*signal(G_ACT, "eg"))
                f(NEB[:].rearrange("p h m -> p m h"), RS[:, :, 16:32], ACT.Exp).then_inc(*signal(G_ACT, "eb"))
                f(HB[:].rearrange("p h m -> p m h"), LNB[:], ACT.Exp).then_inc(*signal(G_ACT, "hb"))
                f(KD[:], KD[:], ACT.Exp).then_inc(*signal(G_ACT, "kd"))
                yield from gap(6)
                act.wait_ge(*done(G_V, "ems"))
                f(EMT[:], EMT[:], ACT.Exp).then_inc(*signal(G_ACT, "emt"))
                yield

            def outputs(steps, g, q, kt, col, b0):
                for j in range(4):
                    wait_alone(act, *done(steps, f"out{j // 2}", g))
                    kw = {} if col is None else {"scale": NC_[:, bass.ds(col(j), 1)]}
                    f(YH[:, bass.ds(kt + j, 1), :], H[:, b0 + j // 2:b0 + j // 2 + 1, sl(j % 2, S)], ACT.Copy, **kw).then_inc(out_hi, 1)
                yield

            def ml(g):
                yield from gap(2)
                after_side(act, g)
                to = wk(3)
                pr = PR[:, :, NBLK:3 * NBLK].rearrange("p m (s n) -> p m s n", s=2)
                f(to.rearrange("p (m n) -> p m n", m=M), pr[:, :, 0, :], ACT.Tanh, scale=0.5).then_inc(*signal(ML_ACT, "to"))
                f(wk(9).rearrange("p (m n) -> p m n", m=M), pr[:, :, 1, :], ACT.Tanh, scale=0.5).then_inc(*signal(ML_ACT, "tz"))
                act.wait_ge(*done(ML_PE, "q", g))
                f(wk(0, 512), bank(0), ACT.Copy, scale=float(P) ** -0.5).then_inc(*signal(ML_ACT, "q"))
                act.wait_ge(*done(ML_PE, "k", g))
                f(wk(0.5, 512), bank(1), ACT.Copy).then_inc(*signal(ML_ACT, "k"))
                yield from gap(3)
                act.wait_ge(*done(ML_V, "arg", g))
                f(wk(2, 768), wk(2, 768), ACT.Exp).then_inc(*signal(ML_ACT, "expw"))
                yield from gap(4)
                yield from gap(3)
                act.wait_ge(*done(ML_V, "h", g))
                f(to, wk(10), ACT.Square).then_inc(*signal(ML_ACT, "sq"))
                yield from gap(2)
                act.wait_ge(*done(ML_V, "ss", g))
                f(ST[:, 8:12], ST[:, 8:12], ACT.Ln, scale=16.0 / 256, bias=eps16_c).then_inc(*signal(ML_ACT, "ln"))
                act.wait_ge(*done(ML_ACT, "ln", g))
                f(ST[:, 8:12], ST[:, 8:12], ACT.Exp, scale=-0.5).then_inc(*signal(ML_ACT, "exp"))
                yield from gap(3)
                yield from outputs(ML_PE, g, g, g * 4, lambda j: g * 4 + (16 + j), 0)

            def dn(g):
                after_side(act, g + 4)
                act.wait_ge(evac, 8 * g + (2 * (E_DN + 4)))
                f(wk(9).rearrange("p (m n) -> p m n", m=M), PR[:, :, 3 * NBLK:], ACT.Tanh, scale=0.5).then_inc(*signal(DN_ACT, "tz"))
                CV = wk(0, 3 * U).rearrange("p (c h t) -> p c h t", c=3, h=4)

                def last_tap(c, b0, p):
                    if p == 0:
                        wait_alone(act, *done(DN_PE, "qkv"[c], g))
                    for h in (2 * p, 2 * p + 1):
                        last = f(CV[:, c, h, :], H[:, b0 + h // 2, sl(h % 2, S)], ACT.Copy, scale=CW[:, bass.ds(g * 4 + (3 * 48 + c * 16 + h), 1)])
                    last.then_inc(*signal(DN_ACT, f"cv{c}{p}"))

                def decays(u):
                    wait_alone(act, rows_in, g * 32 + (64 + 32))
                    for h in range(4):
                        for m in range(M):
                            e = wk(u + (2 * h + m) / 8, P)
                            last = f(e, e, ACT.Relu, scale=-1.0, bias=GAM[:, bass.ds(g * 4 + h, 1), m])
                        if h == 3:
                            last.then_inc(*signal(DN_ACT, f"args{u}"))
                        yield

                def decays_exp(u):
                    act.wait_ge(*done(DN_ACT, f"args{u}", g))
                    f(wk(u), wk(u), ACT.Exp, scale=-1.0).then_inc(*signal(DN_ACT, f"decay{u}"))

                last_tap(1, 0, 0)
                last_tap(1, 0, 1)
                yield from gap(4)
                last_tap(0, 2, 0)
                last_tap(0, 2, 1)
                yield from gap(3)
                act.wait_ge(*done(DN_V, "conv133", g))
                f(wk(8), wk(1), ACT.Tanh, scale=0.5).then_inc(*signal(DN_ACT, "tk"))
                yield from gap(2)
                last_tap(2, 0, 0)
                last_tap(2, 0, 1)
                yield
                yield from decays(5)
                act.wait_ge(*done(DN_V, "conv033", g))
                f(wk(3), wk(0), ACT.Tanh, scale=0.5).then_inc(*signal(DN_ACT, "tq"))
                decays_exp(5)
                yield
                act.wait_ge(*done(DN_V, "silu1", g))
                f(wk(7), wk(1), ACT.Square).then_inc(*signal(DN_ACT, "sqk"))
                yield from gap(3)
                act.wait_ge(*done(DN_PE, "ssk", g))
                f(wk(7), bank(2, 2), ACT.Ln, bias=eps4_c).then_inc(*signal(DN_ACT, "lnk"))
                act.wait_ge(*done(DN_ACT, "lnk", g))
                f(wk(7), wk(7), ACT.Exp, scale=-0.5).then_inc(*signal(DN_ACT, "expk"))
                yield from gap(2)
                act.wait_ge(*done(DN_V, "conv233", g))
                f(wk(8), wk(2), ACT.Tanh, scale=0.5).then_inc(*signal(DN_ACT, "tv"))
                yield from gap(2)
                act.wait_ge(*done(DN_V, "silu0", g))
                f(wk(6), wk(0), ACT.Square).then_inc(*signal(DN_ACT, "sqq"))
                yield from decays(4)
                decays_exp(4)
                yield
                act.wait_ge(*done(DN_PE, "ssq", g))
                f(wk(6), bank(2, 2), ACT.Ln, scale=float(P), bias=eps512_c).then_inc(*signal(DN_ACT, "lnq"))
                act.wait_ge(*done(DN_ACT, "lnq", g))
                f(wk(6), wk(6), ACT.Exp, scale=-0.5).then_inc(*signal(DN_ACT, "expq"))
                yield from gap(7)
                for l in LVS:
                    for p in range(2):
                        act.wait_ge(*done(DN_PE, f"x{l}{p}", g))
                        f(wk(3 + p / 2, 512), bank(p), ACT.Copy).then_inc(*signal(DN_ACT, f"x{l}{p}"))
                    yield from gap(3)
                u = wk(8).rearrange("p (h m t) -> p h m t", h=4, m=M)
                b4 = lambda i: H[:, i, :].rearrange("p (h t) -> p h t", h=4)
                act.wait_ge(*done(DN_PE, "u0", g))
                f(u[:, :, 0, :], b4(0), ACT.Copy).then_inc(*signal(DN_ACT, "u0"))
                yield
                act.wait_ge(*done(DN_PE, "s1", g))
                f(wk(11.5, 512), bank(1), ACT.Copy).then_inc(*signal(DN_ACT, "s1"))
                act.wait_ge(*done(DN_PE, "o0", g))
                f(wk(10, 512), bank(0), ACT.Copy).then_inc(*signal(DN_ACT, "f0"))
                yield from gap(2)
                act.wait_ge(*done(DN_PE, "u1", g))
                f(u[:, :, 1, :], b4(1), ACT.Copy).then_inc(*signal(DN_ACT, "u1"))
                yield from gap(2)
                act.wait_ge(*done(DN_V, "f1b", g))
                f(wk(3), wk(10), ACT.Square).then_inc(*signal(DN_ACT, "sq"))
                yield from gap(2)
                act.wait_ge(*done(DN_V, "ss", g))
                f(ST[:, 8:16], ST[:, 8:16], ACT.Ln, scale=4.0 / P, bias=eps4_c).then_inc(*signal(DN_ACT, "ln"))
                act.wait_ge(*done(DN_ACT, "ln", g))
                f(ST[:, 8:16], ST[:, 8:16], ACT.Exp, scale=-0.5).then_inc(*signal(DN_ACT, "exp"))
                yield from gap(2)
                yield from outputs(DN_PE, g, g + 4, g * 4, lambda j: 32, 2)

            def attend(kind, q, n, evac_need, zslot, kt):
                steps, act_s, dve = AT_PE[kind], AT_ACT[kind], AT_V[kind]
                full = kind == "m"
                w = 512 if full else BIASW
                yield from gap(2)
                after_side(act, q)
                act.wait_ge(evac, evac_need)
                f(wk(8).rearrange("p (m n) -> p m n", m=M), PR[:, :, sl(zslot, NBLK)], ACT.Tanh, scale=0.5).then_inc(*signal(act_s, "tz"))
                act.wait_ge(*done(steps, "q", n))
                f(wk(0), bank(2, 2), ACT.Copy, scale=float(P) ** -0.5).then_inc(*signal(act_s, "q"))
                yield from gap(4)
                act.wait_ge(*done(dve, "neg", n))
                for h in range(4):
                    for m in range(M):
                        n0 = S if full else P
                        a, b = (0, n0) if m == 0 else (n0, n0 + S)
                        last = f(wk(2, 4 * w)[:, h * w + a:h * w + b], H[:, h, a:b], ACT.Exp, bias=ST[:, 24 + 2 * h + m:25 + 2 * h + m],
                                 accum_out=ST[:, 32 + 2 * h + m:33 + 2 * h + m])
                last.then_inc(*signal(act_s, "exp"))
                yield from gap(4)
                act.wait_ge(*done(steps, "pt", n))
                f(wk(4, 2 * w).rearrange("p (h n) -> p h n", h=2), H[:, 0:2, 0:w], ACT.Copy).then_inc(*signal(act_s, "pt"))
                yield from gap(5)
                yield from outputs(steps, n, q, kt, None, 2)

            def gla(l, q, evac_need):
                yield from gap(2)
                after_side(act, q)
                act.wait_ge(evac, evac_need)
                f(wk(8).rearrange("p (m n) -> p m n", m=M), PR[:, :, sl(1, NBLK)], ACT.Tanh, scale=0.5).then_inc(*signal(GL_ACT, "tz"))
                act.wait_ge(*done(GL_PE, "q", l))
                f(wk(0, 512), bank(0), ACT.Copy, scale=64.0 ** -0.5).then_inc(*signal(GL_ACT, "q"))
                act.wait_ge(*done(GL_PE, "k", l))
                f(wk(0.5, 512), bank(1), ACT.Copy).then_inc(*signal(GL_ACT, "k"))
                yield from gap(3)
                x = wk(6.5, 512)
                act.wait_ge(rel_st, l * 16 + 16)
                act.wait_ge(*done(GL_PE, "logit", l))
                f(x, bank(3), ACT.Abs).then_inc(*signal(GL_ACT, "absx"))
                act.wait_ge(*done(GL_ACT, "absx", l))
                f(x, x, ACT.Exp, scale=-1.0).then_inc(*signal(GL_ACT, "expx"))
                act.wait_ge(*done(GL_ACT, "expx", l))
                f(x, x, ACT.Ln, bias=1.0).then_inc(*signal(GL_ACT, "lnx"))
                yield from gap(2)
                act.wait_ge(*done(GL_PE, "b", l))
                f(wk(3, 512), bank(2), ACT.Copy).then_inc(*signal(GL_ACT, "b"))
                yield from gap(1)
                for lv in range(1, 9):
                    hf = 2 ** (lv - 1)
                    e = wk(4 + (lv % 2) / 2, 512).rearrange("p (n s h) -> p n s h", s=2, h=hf)
                    act.wait_ge(*done(GL_V, f"d{lv}", l))
                    f(e[:, :, 0, :], e[:, :, 0, :], ACT.Exp, scale=-1.0 / 16)
                    f(e[:, :, 1, :], e[:, :, 1, :], ACT.Exp, scale=1.0 / 16).then_inc(*signal(GL_ACT, f"e{lv}"))
                    yield from gap(5)
                act.wait_ge(*done(GL_PE, "l8", l))
                f(wk(6, 512).rearrange("p (hh par t) -> p par hh t", hh=2, par=2), H[:, 0:2, 0:S].rearrange("p par (hh t) -> p par hh t", hh=2),
                  ACT.Copy).then_inc(*signal(GL_ACT, "at8"))
                yield from gap(4)
                act.wait_ge(*done(GL_PE, "pv", l))
                f(wk(7), bank(2, 2), ACT.Copy).then_inc(*signal(GL_ACT, "f"))
                act.wait_ge(*done(GL_ACT, "f", l))
                f(wk(1), wk(7), ACT.Square).then_inc(*signal(GL_ACT, "sq"))
                yield from gap(1)
                act.wait_ge(*done(GL_V, "ss", l))
                f(ST[:, 8:16], ST[:, 8:16], ACT.Ln, scale=4.0 / P, bias=eps4_c).then_inc(*signal(GL_ACT, "ln"))
                act.wait_ge(*done(GL_ACT, "ln", l))
                f(ST[:, 8:16], ST[:, 8:16], ACT.Exp, scale=-0.5).then_inc(*signal(GL_ACT, "exp"))
                yield from gap(2)
                yield from outputs(GL_PE, l, q, 8, lambda j: 33 + l, 0)

            act.wait_ge(eps_ready, 1)
            for c in range(NCH):
                if c == NCH // 2:
                    act.wait_ge(mem_in[1], 16)
                    act.dma_start(RES[:], x2).then_inc(x_in, 16)
                act.wait_ge(m_pe, c + 1)
                f(YH[:, 2 * c:2 * c + 2, :], H[:, c % 4:c % 4 + 1, :].rearrange("p b (j t) -> p (b j) t", j=2), ACT.Copy).then_inc(m_hi, 1)
            for c in range(AHEAD):
                high(N_MEM, c, 0)
            stream(N_MEM, 4, 0, x_prep(), ahead=(W_GATE, EX_GATE))
            small_block(N_GATE, 0, 48, G_ACT, wk(11, S)[0:48, :], EX_GATE)
            X1 = EX_GATE
            mkv = [[(mkv_out[b], 16)] for b in range(4)]
            stream(N_ML, 4, X1, gates(), free=mkv)
            with act.Fori(1, 4) as g:
                stream(N_ML + g * (4 * NCH), 4, X1, ml(g - 1),
                       free=[[done(ML_PE, "k", g - 1)], [done(ML_V, "g2", g - 1)], [done(ML_V, "g1", g - 1)], [done(ML_PE, "pv", g - 1)]])
            stream(N_GA, 4, X1, ml(3), free=[[done(ML_PE, "k", 3)], [done(ML_V, "g2", 3)], [done(ML_V, "g1", 3)], [done(ML_PE, "pv", 3)]])
            act.wait_ge(evac, 2 * E_YA)
            for m in range(M):
                f(PR[:, m, :], PR[:, m, :], ACT.Tanh, scale=0.5).then_inc(g_tanh, 1)
            stream(N_YA, 4, X1, none(), slots=None)
            stream(N_DN, 4, X1, none(), free=[[(evac, 2 * E_DN)]])
            with act.Fori(1, 4) as g:
                stream(N_DN + g * (4 * NCH), 4, X1, dn(g - 1),
                       free=[[done(DN_PE, "q", g - 1)], [done(DN_PE, "q", g - 1)], [done(DN_PE, "v", g - 1)], [done(DN_V, "g", g - 1)]])
            stream(N_GB, 4, X1, dn(3), free=[[done(DN_PE, "q", 3)], [done(DN_PE, "k", 3)], [done(DN_PE, "v", 3)], [done(DN_V, "g", 3)]])
            act.wait_ge(evac, 2 * E_YB)
            for m in range(M):
                f(PR[:, m, :], PR[:, m, :], ACT.Tanh, scale=0.5).then_inc(g_tanh, 1)

            def squares():
                for b in range(4):
                    yield from gap(20 if b == 0 else 16)
                    act.wait_ge(evac, 2 * (E_YB + b + 1))
                    for m in range(M):
                        f(wk(4, NBLK), RES[:, m, sl(b, NBLK)], ACT.Square, accum_out=ST[:, 56 + 4 * m + b:57 + 4 * m + b]).then_inc(norm_s, 1)
                        act.wait_ge(norm_s, 6 + 2 * b + m)

            stream(N_YB, 4, X1, squares(), slots=None, ahead=None)
            act.wait_ge(norm_s, 14)
            f(ST[:, 2:4], ST[:, 0:2], ACT.Ln, scale=1.0 / D, bias=eps_c).then_inc(norm_s, 1)
            act.wait_ge(norm_s, 15)
            f(ST[:, 4:6], ST[:, 2:4], ACT.Exp, scale=-0.5).then_inc(norm_s, 1)
            with act.Fori(0, 2) as l:
                n, e, q = N_L + l * LSZ, E_L + l * LBL, 8 + 4 * l
                ex = 16 * l + X1
                for c in range(AHEAD):
                    high(n, c, ex + EX_LR, 4 * 16)
                for c in range(NCH):
                    act.wait_ge(x_pe, 8 * l + (c + 9))
                    for j in range(2):
                        f(XH[:, 2 * c + j, :], H[:, c % 4, sl(j, S)], ACT.Copy).then_inc(x_hi, 1)
                small_block(n, ex, 16, GL_ACT, LRT[0:16, :], EX_LR)
                ex = 16 * l + (X1 + EX_LR)
                stream(n + L_M, 2, ex, none())
                stream(n + L_B, 3, ex, attend("m", q, l, 2 * (e + 2), 1, 12), slots=(0, 1, 3), free=[[done(AT_PE["m"], "q", l)], [done(AT_V["m"], "g", l)]])
                stream(n + L_A0, 4, ex, gla(l, q + 1, 2 * (e + 5)), free=[[done(GL_PE, "k", l)], [done(GL_V, "g", l)], [], [done(GL_PE, "pv", l)]])
                stream(n + L_A1, 4, ex, attend("a", q + 2, 2 * l, 2 * (e + 9), 3, 0),
                       free=[[done(AT_PE["a"], "q", 2 * l)], [done(AT_PE["a"], "k", 2 * l)], [done(AT_PE["a"], "pv", 2 * l)], [done(AT_V["a"], "g", 2 * l)]])
                stream(n + L_Y1, 4, ex, attend("a", q + 3, 2 * l + 1, 2 * (e + 13), 3, 4), slots=None, per=len(Y1_TILES))
                stream(n + L_Y2, 4, ex, none(), slots=None, ahead=None, per=len(Y2_TILES))
                for m in range(M):
                    act.wait_ge(*done(LN_V, f"ag{m}", l))
                    f(ST[:, 50 + m:51 + m], ST[:, 41 + 2 * m:42 + 2 * m], ACT.Ln, bias=epsln_c).then_inc(norm_s, 1)
                act.wait_ge(norm_s, l * 3 + 18)
                f(ST[:, 50:52], ST[:, 50:52], ACT.Exp, scale=-0.5).then_inc(norm_s, 1)
                act.wait_ge(*done(LN_V, "shift", l))
                for c in range(NCH):
                    for m in range(M):
                        last = f(RES[:, m, sl(c, S)], RES[:, m, sl(c, S)], ACT.Identity, scale=ST[:, 50 + m:51 + m], bias=ST[:, 52 + m:53 + m])
                    last.then_inc(ln_scaled, 1)

        @block.vector
        def _(dve):
            tt, ts, stt = dve.tensor_tensor, dve.tensor_scalar, dve.scalar_tensor_tensor

            def low(n, c, width=CH * NBLK):
                dve.wait_ge(hi_done, n + (c + 1))
                tt(WL[:, c % RING, 0:width], RAW[:, c % RING, 0:width], WH[:, c % RING, 0:width].bitcast(F32), ALU.subtract).then_inc(lo_done, 1)

            def stream(n, nblk, side, take=None, ahead=CH * NBLK, per=NCH):
                for b in range(nblk):
                    for c in range(per):
                        i = b * per + c + AHEAD
                        if i < nblk * per:
                            low(n, i)
                        elif ahead:
                            low(n, i, ahead)
                        advance(side, 2)
                    if take:
                        dve.wait_ge(used, n + (b + 1) * per)
                        for m in range(M):
                            take(b, m, SP_[:, 2 * (b % 2) + m, :])
                finish(side)

            def small_block(n, width):
                for i in range(AHEAD, RING):
                    low(n, i, 4 * width)
                for i in range(AHEAD):
                    low(n, RING + i)

            def x_prep():
                yield from gap(3)
                dve.wait_ge(cols_pe, 1)
                dve.tensor_copy(CW[:], H[:, 0, 0:192]).then_inc(cols_v, 1)
                nc16 = NC_[:, 0:16].rearrange("p (c j) -> p c j", j=2)
                for j in range(2):
                    dve.tensor_copy(nc16[:, :, j], H[:, 0, 192 + 8 * j:200 + 8 * j]).then_inc(cols_v, 1)
                dve.tensor_copy(NC_[:, 16:33], H[:, 0, 208:225]).then_inc(cols_v, 1)
                dve.tensor_copy(NC_[:, 33:35], H[:, 0, 226:228]).then_inc(cols_v, 1)
                yield from gap(8)
                for c in range(NCH):
                    for j in range(2):
                        k = 2 * c + j
                        dve.wait_ge(x_hi, 2 * c + 2)
                        stt(XL[:, k, :], H[:, c % 4, sl(j, S)], NC_[:, k:k + 1], XH[:, k, :].bitcast(F32), ALU.mult, ALU.subtract).then_inc(x_lo, 1)
                    yield

            def gates():
                b3 = lambda ap: ap.unsqueeze(1).broadcast_to([P, M, ap.shape[1]])
                dve.wait_ge(*done(G_PE, "gt"))
                dve.tensor_copy(GT[:], H[:, 0, 0:96].rearrange("p (m n) -> p m n", m=M)).then_inc(*signal(G_V, "gt"))
                dve.wait_ge(*done(G_V, "gt"))
                tt(GT[:, :, 0:16], GT[:, :, 0:16], b3(BIA[:, 0:16]), ALU.add).then_inc(*signal(G_V, "bias_if"))
                tt(GT[:, :, 32:48], GT[:, :, 32:48], b3(BIA[:, 16:32]), ALU.add).then_inc(*signal(G_V, "bias_a"))
                dve.wait_ge(*done(G_V, "bias_a"))
                stt(NA[:], GT[:, :, 16:48], -1.0, GT[:, :, 16:48], ALU.mult, ALU.min).then_inc(*signal(G_V, "negabs"))
                dve.wait_ge(*done(G_ACT, "alog"))
                stt(LNB[:], GT[:, :, 16:32], 0.0, NA[:, :, 0:16], ALU.min, ALU.subtract).then_inc(*signal(G_V, "lnb"))
                stt(GT[:, :, 32:48], GT[:, :, 32:48], 0.0, NA[:, :, 16:32], ALU.max, ALU.add).then_inc(*signal(G_V, "sp"))
                dve.wait_ge(*done(G_V, "sp"))
                stt(LG[:, :, 8:24], GT[:, :, 32:48], -1.0, b3(EA[:]), ALU.mult, ALU.mult).then_inc(*signal(G_V, "g"))
                yield from gap(3)
                dve.wait_ge(*done(G_PE, "cumsum"))
                dve.tensor_copy(CS[:, 0, :], H[:, 2, 0:24]).then_inc(*signal(G_V, "cs0"))
                dve.tensor_copy(CS[:, 1, :], H[:, 2, 32:56]).then_inc(*signal(G_V, "cs1"))
                dve.wait_ge(*done(G_V, "cs1"))
                hm = lambda t: t[:].rearrange("p h m -> p m h")
                stt(hm(AS), TI[:, :, 0:8], 15.0, CS[:, :, 0:8], ALU.mult, ALU.add).then_inc(*signal(G_V, "as"))
                dve.tensor_copy(hm(GAM), CS[:, :, 8:24]).then_inc(*signal(G_V, "gam"))
                dve.tensor_copy(RS[:, :, 0:16], CS[:, :, 8:24]).then_inc(*signal(G_V, "rs0"))
                tt(RS[:, :, 16:32], CS[:, :, 8:24], LNB[:], ALU.add).then_inc(*signal(G_V, "rs1"))
                dve.wait_ge(*done(G_V, "as"))
                dve.tensor_copy(RS[:, :, 32:40], hm(AS)).then_inc(*signal(G_V, "rs2"))
                tt(KD[:], H[:, 2, 64:80], CS[:, 0, 8:24], ALU.subtract).then_inc(*signal(G_V, "kd"))
                yield from gap(5)
                dve.wait_ge(*done(G_PE, "rows"))
                dve.tensor_copy(RT[:], H[0:40, 3, 0:S]).then_inc(*signal(G_V, "rt"))
                dve.wait_ge(*done(G_V, "rt"))
                dve.tensor_tensor_scan(MT[32:40, :], RT[32:40, :], RT[32:40, :], 0.0, ALU.max, ALU.max).then_inc(*signal(G_V, "scan"))
                dve.wait_ge(*done(G_V, "scan"))
                ts(RT[32:40, :], MT[32:40, :], -1.0, None, ALU.mult).then_inc(*signal(G_V, "negm"))
                yield from gap(5)
                dve.wait_ge(*done(G_PE, "negm"))
                tt(hm(EMT), H[:, 0, 0:16].rearrange("p (m h) -> p m h", m=M), CS[:, :, 0:8], ALU.add).then_inc(*signal(G_V, "ems"))
                dve.wait_ge(*done(G_ACT, "kd"))
                ts(NEB[:], NEB[:], -1.0, None, ALU.mult).then_inc(*signal(G_V, "neb"))
                ts(HB[:], HB[:], 0.5, None, ALU.mult).then_inc(*signal(G_V, "hb"))
                yield

            def outputs(steps, g, q, kt, col, b0):
                for j in range(4):
                    dve.wait_ge(out_hi, NCH + (4 * q + (2 * (j // 2) + 2)))
                    src = H[:, b0 + j // 2:b0 + j // 2 + 1, sl(j % 2, S)]
                    yh, yl = YH[:, bass.ds(kt + j, 1), :].bitcast(F32), YL[:, bass.ds(kt + j, 1), :]
                    if col is None:
                        tt(yl, src, yh, ALU.subtract).then_inc(out_lo, 1)
                    else:
                        stt(yl, src, NC_[:, bass.ds(col(j), 1)], yh, ALU.mult, ALU.subtract).then_inc(out_lo, 1)
                yield

            def ml(g):
                w = wk(2, 768)
                yield from gap(2)
                after_side(dve, g)
                dve.wait_ge(rows_in, g * 16 + 16)
                for h in range(2):
                    for s in range(M):
                        last = ts(w[:, h * 384 + s * S:h * 384 + s * S + S - s * P], wk(1, 512)[:, h * S + s * P:(h + 1) * S],
                                  AS[:, bass.ds(g * 2 + h, 1), s], 0.0, ALU.add, ALU.min)
                last.then_inc(*signal(ML_V, "arg"))
                G, z = wk(9).rearrange("p (m n) -> p m n", m=M), PR[:, :, 2 * NBLK:3 * NBLK]
                dve.wait_ge(*done(ML_ACT, "tz", g))
                stt(G, G, 1.0, z, ALU.add, ALU.mult).then_inc(*signal(ML_V, "g1"))
                dve.wait_ge(*done(ML_V, "g1", g))
                stt(wk(9), wk(3), 1.0, wk(9), ALU.add, ALU.mult).then_inc(*signal(ML_V, "g2"))
                yield from gap(3)
                dve.wait_ge(*done(ML_ACT, "expw", g))
                diag = w.rearrange("p (h n) -> p h n", h=2)
                for h in range(2):
                    d = bass.AP(WK, w.offset + h * 384, [[12 * U, P], [S, 2], [1, P]])
                    last = tt(d, d, over(upper[:], 2), ALU.mult)
                last.then_inc(*signal(ML_V, "mask"))
                dve.wait_ge(*done(ML_V, "mask", g))
                dve.wait_ge(*done(ML_PE, "scores", g))
                tt(diag, diag, H[:, 2:4, 0:384], ALU.mult).then_inc(*signal(ML_V, "p"))
                yield from gap(4)
                dve.wait_ge(*done(ML_PE, "pv", g))
                dve.wait_ge(*done(G_ACT, "emt"))
                emt = EMT[:, bass.ds(g * 2, 2), :]
                hm4 = lambda ap: ap.rearrange("p (h m) -> p h m", h=2)
                stt(hm4(ST[:, 20:24]), hm4(H[:, 2, 0:4]), -1.0, emt, ALU.mult, ALU.max).then_inc(*signal(ML_V, "den0"))
                dve.wait_ge(*done(ML_V, "den0", g))
                tt(ST[:, 12:16], H[:, 2, 0:4], ST[:, 20:24], ALU.max).then_inc(*signal(ML_V, "den"))
                dve.wait_ge(*done(ML_V, "den", g))
                dve.reciprocal(ST[:, 16:20], ST[:, 12:16]).then_inc(*signal(ML_V, "rden"))
                dve.wait_ge(*done(ML_V, "rden", g))
                F = wk(10).rearrange("p (m h e) -> p h m e", m=M, h=2)
                r4 = ST[:, 16:20].rearrange("p (h m) -> p h m", h=2)
                tt(F, bank(0, 2).rearrange("p (h m e) -> p h m e", h=2, m=M), cols(r4, S), ALU.mult).then_inc(*signal(ML_V, "h"))
                yield from gap(4)
                dve.wait_ge(*done(ML_ACT, "sq", g))
                dve.reduce_sum(ST[:, 8:12], wk(3).rearrange("p (s e) -> p s e", s=4), axis=AX.X).then_inc(*signal(ML_V, "ss"))
                yield from gap(2)
                dve.wait_ge(*done(ML_ACT, "exp", g))
                F4 = wk(10).rearrange("p (s e) -> p s e", s=4)
                tt(F4, F4, cols(ST[:, 8:12], S), ALU.mult).then_inc(*signal(ML_V, "fr"))
                dve.wait_ge(*done(ML_V, "fr", g))
                tt(wk(10), wk(10), wk(9), ALU.mult).then_inc(*signal(ML_V, "fg"))
                yield from gap(2)
                yield from outputs(ML_PE, g, g, g * 4, lambda j: g * 4 + (16 + j), 0)

            def dn(g):
                after_side(dve, g + 4)
                G, z = wk(9).rearrange("p (m n) -> p m n", m=M), PR[:, :, 3 * NBLK:]
                dve.wait_ge(*done(DN_ACT, "tz", g))
                stt(G, G, 1.0, z, ALU.add, ALU.mult).then_inc(*signal(DN_V, "g"))
                CV = wk(0, 3 * U).rearrange("p (c h t) -> p c h t", c=3, h=4)

                def conv(c, b0):
                    for p in (0, 1):
                        dve.wait_ge(*done(DN_ACT, f"cv{c}{p}", g))
                        for j in range(1, 4):
                            for h in (2 * p, 2 * p + 1):
                                wcol = CW[:, bass.ds(g * 4 + ((3 - j) * 48 + c * 16 + h), 1)]
                                src = H[:, b0 + h // 2, sl(h % 2, S)]
                                if j > 1:
                                    dve.wait_ge(*done(DN_V, f"conv{c}{j - 1}{h}", g))
                                stt(CV[:, c, h, j:S], src[:, 0:S - j], wcol, CV[:, c, h, j:S], ALU.mult, ALU.add).then_inc(*signal(DN_V, f"conv{c}{j}{h}"))
                            yield

                yield
                yield from conv(1, 0)
                yield from conv(0, 2)
                d3 = lambda u: wk(u).rearrange("p (s t) -> p s t", t=P)
                dve.wait_ge(*done(DN_ACT, "tk", g))
                stt(wk(1), wk(8), 1.0, wk(1), ALU.add, ALU.mult).then_inc(*signal(DN_V, "silu1"))
                yield
                yield from conv(2, 0)
                dve.wait_ge(*done(DN_ACT, "expk", g))
                tt(wk(1), wk(1), wk(7), ALU.mult).then_inc(*signal(DN_V, "nk"))
                yield
                dve.wait_ge(*done(DN_ACT, "tq", g))
                stt(wk(0), wk(3), 1.0, wk(0), ALU.add, ALU.mult).then_inc(*signal(DN_V, "silu0"))
                yield
                dve.wait_ge(*done(DN_ACT, "tv", g))
                stt(wk(2), wk(8), 1.0, wk(2), ALU.add, ALU.mult).then_inc(*signal(DN_V, "silu2"))
                yield from gap(2)
                dve.wait_ge(*done(DN_PE, "k0t", g))
                tt(wk(11, 512).rearrange("p (s t) -> p s t", t=P), bank(2).rearrange("p (s t) -> p s t", t=P),
                   cols(KD[:, bass.ds(g * 4, 4)], P), ALU.mult).then_inc(*signal(DN_V, "ke"))
                yield from gap(2)

                def decayed(name, b0, u, mask, step):
                    dve.wait_ge(*done(DN_PL, mask, g))
                    for p in range(2):
                        dve.wait_ge(*done(DN_PE, f"{name}{p}", g))
                        tt(wk(u + p / 2, 512), bank(b0 + p), wk(u + p / 2, 512), ALU.mult).then_inc(*signal(DN_V, f"{step}{p}"))

                decayed("kk", 0, 5, "maskr", "at")
                yield from gap(2)
                dve.wait_ge(*done(DN_ACT, "expq", g))
                tt(wk(0), wk(0), wk(6), ALU.mult).then_inc(*signal(DN_V, "nq"))
                yield
                for p in range(2):
                    dve.wait_ge(*done(DN_PE, f"vt{p}", g))
                    tt(wk(2 + p / 2, 512).rearrange("p (s t) -> p s t", t=P), bank(2 + p).rearrange("p (s t) -> p s t", t=P),
                       cols(HB[:, bass.ds(g * 4 + 2 * p, 2), :].rearrange("p h m -> p (h m)"), P), ALU.mult).then_inc(*signal(DN_V, f"v{p}"))
                yield
                dve.wait_ge(*done(DN_PL, "ut0", g))
                tt(d3(7), over(ident[:], 8), d3(8), ALU.subtract).then_inc(*signal(DN_V, "tt0"))
                yield from gap(2)
                decayed("qk", 2, 4, "maskg", "qkt")
                yield
                dve.wait_ge(*done(DN_PE, "x0", g))
                tt(d3(6), over(ident[:], 8), bank(0, 2).rearrange("p (s t) -> p s t", t=P), ALU.subtract).then_inc(*signal(DN_V, "t0"))
                yield
                for l in LVS:
                    yield from gap(2)
                    for p in range(2):
                        dve.wait_ge(*done(DN_PE, f"t{l}{p}", g))
                        if l < 6:
                            tt(wk(6 + p / 2, 512), wk(6 + p / 2, 512), bank(p), ALU.subtract).then_inc(*signal(DN_V, f"t{l}{p}"))
                        tt(wk(7 + p / 2, 512), wk(7 + p / 2, 512), bank(2 + p), ALU.subtract).then_inc(*signal(DN_V, f"tt{l}{p}"))
                    yield
                yield from gap(2)
                F1 = wk(10.5, 512).rearrange("p (s t) -> p s t", t=P)
                V = wk(2).rearrange("p (h m t) -> p h m t", h=4, m=M)
                dve.wait_ge(*done(DN_PE, "qs", g))
                tt(F1, bank(3).rearrange("p (s t) -> p s t", t=P), cols(EG[:, bass.ds(g * 4, 4), 1], P), ALU.mult).then_inc(*signal(DN_V, "f1a"))
                dve.wait_ge(*done(DN_PE, "ks", g))
                for h in range(4):
                    stt(V[:, h, 1, :], H[:, 2, sl(h)], NEB[:, bass.ds(g * 4 + h, 1), 1], V[:, h, 1, :], ALU.mult, ALU.add).then_inc(*signal(DN_V, f"r{h}"))
                yield from gap(2)
                dve.wait_ge(*done(DN_PE, "o1", g))
                dve.wait_ge(*done(DN_ACT, "f0", g))
                tt(wk(10.5, 512), bank(0), wk(10.5, 512), ALU.add).then_inc(*signal(DN_V, "f1b"))
                yield from gap(1)
                dve.wait_ge(*done(DN_ACT, "sq", g))
                dve.reduce_sum(ST[:, 8:16], wk(3).rearrange("p (s e) -> p s e", s=8), axis=AX.X).then_inc(*signal(DN_V, "ss"))
                yield from gap(2)
                dve.wait_ge(*done(DN_ACT, "exp", g))
                tt(d3(10), d3(10), cols(ST[:, 8:16], P), ALU.mult).then_inc(*signal(DN_V, "fr"))
                dve.wait_ge(*done(DN_V, "fr", g))
                tt(wk(10), wk(10), wk(9), ALU.mult).then_inc(*signal(DN_V, "fg"))
                yield from gap(2)
                yield from outputs(DN_PE, g, g + 4, g * 4, lambda j: 32, 2)

            def attend(kind, q, n, zslot, kt):
                steps, act_s = AT_PE[kind], AT_ACT[kind]
                full = kind == "m"
                w = 512 if full else BIASW
                yield from gap(2)
                after_side(dve, q)
                dve.wait_ge(*done(steps, "k", n))
                dve.tensor_copy(wk(1), bank(0, 2)).then_inc(*signal(AT_V[kind], "k"))
                G = wk(8).rearrange("p (m n) -> p m n", m=M)
                dve.wait_ge(*done(act_s, "tz", n))
                stt(G, G, 1.0, PR[:, :, sl(zslot, NBLK)], ALU.add, ALU.mult).then_inc(*signal(AT_V[kind], "g"))
                yield from gap(3)
                dve.wait_ge(*done(steps, "scores", n))
                mx = ST[:, 16:24]
                src = H
                n0 = S if full else P
                mv = mx.rearrange("p (h m) -> p h m", m=M)
                dve.reduce_max(mv[:, :, 0], src[:, :, 0:n0], axis=AX.X).then_inc(*signal(AT_V[kind], "max0"))
                dve.reduce_max(mv[:, :, 1], src[:, :, n0:n0 + S], axis=AX.X).then_inc(*signal(AT_V[kind], "max1"))
                dve.wait_ge(*done(AT_V[kind], "max1", n))
                ts(ST[:, 24:32], mx, -1.0, None, ALU.mult).then_inc(*signal(AT_V[kind], "neg"))
                yield from gap(5)
                dve.wait_ge(*done(steps, "pt", n))
                dve.tensor_copy(wk(4, 4 * w)[:, 2 * w:4 * w].rearrange("p (h n) -> p h n", h=2), H[:, 2:4, 0:w]).then_inc(*signal(AT_V[kind], "pt"))
                dve.reciprocal(ST[:, 16:24], ST[:, 32:40]).then_inc(*signal(AT_V[kind], "rs"))
                yield from gap(3)
                dve.wait_ge(*done(steps, "pv", n))
                dve.wait_ge(*done(AT_V[kind], "rs", n))
                for m in range(M):
                    last = tt(wk(7 + m / 2, 512).rearrange("p (s t) -> p s t", t=P), bank(m).rearrange("p (s t) -> p s t", t=P),
                              cols(mv[:, :, m], P), ALU.mult)
                last.then_inc(*signal(AT_V[kind], "f"))
                dve.wait_ge(*done(AT_V[kind], "f", n))
                stt(wk(7), wk(8), 0.5, wk(7), ALU.mult, ALU.mult).then_inc(*signal(AT_V[kind], "fg"))
                yield from gap(2)
                yield from outputs(steps, n, q, kt, None, 2)

            def gla(l, q):
                yield from gap(2)
                after_side(dve, q)
                A = wk(5, 1536).rearrange("p (c s) -> p c s", c=3)
                dve.memset(wk(5), 0.0).then_inc(*signal(GL_V, "zero"))
                G = wk(8).rearrange("p (m n) -> p m n", m=M)
                dve.wait_ge(*done(GL_ACT, "tz", l))
                stt(G, G, 1.0, PR[:, :, sl(1, NBLK)], ALU.add, ALU.mult).then_inc(*signal(GL_V, "g"))
                yield from gap(2)
                yield
                dve.wait_ge(*done(GL_ACT, "lnx", l))
                stt(wk(3.5, 512), bank(3), 0.0, wk(6.5, 512), ALU.min, ALU.subtract).then_inc(*signal(GL_V, "lg"))
                yield from gap(2)

                def put(par, b, mask):
                    a = wk(5).rearrange("p (m hh par t) -> p par hh m t", m=M, hh=2, par=2)[:, par]
                    m4 = bass.AP(mask.tensor, mask.offset, [list(mask.ap[0]), [0, 2], [0, 2], [1, P]]).bitcast(U32)
                    return dve.copy_predicated(a, m4, H[:, b, :].rearrange("p (hh m t) -> p hh m t", hh=2, m=M))

                wait_alone(dve, *done(GL_PE, "d", l))
                for par in range(2):
                    put(par, par, ident[:]).then_inc(*signal(GL_V, f"cp0{par}"))
                yield from gap(1)
                dve.wait_ge(*done(GL_ACT, "b", l))
                for lv in range(1, 9):
                    size, hf = 2 ** lv, 2 ** (lv - 1)
                    e = wk(4 + (lv % 2) / 2, 512)
                    B = wk(3, 512).rearrange("p (n s) -> p n s", s=size)
                    mid = B[:, :, hf - 1:hf].broadcast_to([P, 512 // size, size])
                    if lv >= 3:
                        dve.wait_ge(*done(GL_V, f"qe{lv - 2}", l))
                    tt(e.rearrange("p (n s) -> p n s", s=size), B, mid, ALU.subtract).then_inc(*signal(GL_V, f"d{lv}"))
                    dve.wait_ge(*done(GL_ACT, f"e{lv}", l))
                    if lv >= 3:
                        dve.wait_ge(*done(GL_PE, f"l{lv - 2}", l))
                    tt(wk(1 + lv % 2).rearrange("p (c n) -> p c n", c=2), wk(0).rearrange("p (c n) -> p c n", c=2), over(e, 2), ALU.mult).then_inc(*signal(GL_V, f"qe{lv}"))
                    yield from gap(3)
                    if lv < 8:
                        dve.wait_ge(*done(GL_PE, f"l{lv}", l))
                        for par in range(2):
                            wait_alone(dve, *done(GL_V, f"cp{lv - 1}{par}", l))
                            put(par, 2 * (lv % 2) + par, SY[:, lv - 1, :] if lv < 7 else LV[:, 6, :]).then_inc(*signal(GL_V, f"cp{lv}{par}"))
                    yield from gap(2)
                yield from gap(5)
                dve.wait_ge(*done(GL_ACT, "sq", l))
                dve.reduce_sum(ST[:, 8:16], wk(1).rearrange("p (s e) -> p s e", s=8), axis=AX.X).then_inc(*signal(GL_V, "ss"))
                yield
                dve.wait_ge(*done(GL_ACT, "exp", l))
                F8 = wk(7).rearrange("p (s e) -> p s e", s=8)
                tt(F8, F8, cols(ST[:, 8:16], P), ALU.mult).then_inc(*signal(GL_V, "fr"))
                dve.wait_ge(*done(GL_V, "fr", l))
                tt(wk(7), wk(7), wk(8), ALU.mult).then_inc(*signal(GL_V, "fg"))
                yield from gap(2)
                yield from outputs(GL_PE, l, q, 8, lambda j: 33 + l, 0)

            def gated(base):
                def take(b, m, acc):
                    tmp = wk(11 + m / 2, 512)
                    k = 8 * base + 2 * b + m
                    dve.wait_ge(g_tanh, 2 * base + 2)
                    if b:
                        dve.wait_ge(evac, 2 * (E_YB if base else E_YA) + (2 * b + m - 1))
                    stt(tmp, PR[:, m, sl(b, NBLK)], 1.0, acc, ALU.add, ALU.mult).then_inc(evac_tmp, 1)
                    dve.wait_ge(evac_tmp, k + 1)
                    r = RES[:, m, sl(b, NBLK)]
                    stt(r, tmp, 0.5, r, ALU.mult, ALU.add).then_inc(evac, 1)
                return take

            dve.memset(LRT, 1.0)
            dve.memset(eps_c, EPS)
            dve.memset(eps16_c, 16 * EPS)
            dve.memset(eps512_c, 4 * P * EPS)
            dve.memset(eps4_c, 4 * EPS)
            dve.memset(epsln_c, LN_EPS).then_inc(eps_ready, 1)
            for c in range(NCH):
                dve.wait_ge(m_hi, c + 1)
                v = lambda t: t[:, 2 * c:2 * c + 2, :]
                tt(v(YL), H[:, c % 4:c % 4 + 1, :].rearrange("p b (j t) -> p (b j) t", j=2), v(YH).bitcast(F32), ALU.subtract).then_inc(m_lo, 1)
            for c in range(AHEAD):
                low(N_MEM, c)
            stream(N_MEM, 4, x_prep(), ahead=W_GATE)
            small_block(N_GATE, 48)
            stream(N_ML, 4, gates())
            with dve.Fori(1, 4) as g:
                stream(N_ML + g * (4 * NCH), 4, ml(g - 1))
            stream(N_GA, 4, ml(3))
            stream(N_YA, 4, none(), take=gated(0))
            stream(N_DN, 4, none())
            with dve.Fori(1, 4) as g:
                stream(N_DN + g * (4 * NCH), 4, dn(g - 1))
            stream(N_GB, 4, dn(3))
            stream(N_YB, 4, none(), take=gated(1), ahead=None)
            dve.wait_ge(norm_s, 13)
            dve.reduce_sum(ST[:, 0:2], ST[:, 56:64].rearrange("p (m b) -> p m b", m=M), axis=AX.X).then_inc(norm_s, 1)
            dve.wait_ge(norm_s, 16)
            dve.wait_ge(lw_in, 16)
            for c in range(NCH):
                for m in range(M):
                    r = RES[:, m, sl(c, S)]
                    last = stt(r, r, ST[:, 4 + m:5 + m], wk(0, D)[:, sl(c, S)], ALU.mult, ALU.mult)
                last.then_inc(x_tok, 1)
            with dve.Fori(0, 2) as l:
                n, q = N_L + l * LSZ, 8 + 4 * l
                for c in range(AHEAD):
                    low(n, c, 4 * 16)
                for c in range(NCH):
                    for j in range(2):
                        k = 2 * c + j
                        dve.wait_ge(x_hi, 16 * l + (18 + 2 * c))
                        tt(XL[:, k, :], H[:, c % 4, sl(j, S)], XH[:, k, :].bitcast(F32), ALU.subtract).then_inc(x_lo, 1)
                small_block(n, 16)
                R, E = wk(6, 257)[0:8, :], wk(6.5, BIASW)[0:8, :]
                dve.wait_ge(rel_in, l * 16 + 16)
                dve.tensor_copy(E[:, 0:P], R[:, 256:257].broadcast_to([8, P])).then_inc(rel_s, 1)
                dve.tensor_copy(E[:, P:BIASW - 1], bass.AP(WK, R.offset + 255, [[12 * U, 8], [-1, 255]])).then_inc(rel_s, 1)
                stream(n + L_M, 2, none())
                stream(n + L_B, 3, attend("m", q, l, 1, 12))
                stream(n + L_A0, 4, gla(l, q + 1))
                BW = wk(9, 3 * U).rearrange("p (h n) -> p h n", h=A_H)
                dve.wait_ge(rel_bw, l * 16 + 16)
                dve.tensor_copy(BW[:, :, 0:P], BW[:, :, S:BIASW]).then_inc(rel_m, 1)
                dve.wait_ge(rel_m, l * 3 + 1)
                dve.memset(BW[64:P, :, 64:P], NEG).then_inc(rel_m, 1)
                dve.memset(BW[64:P, :, BIASW - 64:BIASW], NEG).then_inc(rel_m, 1)
                stream(n + L_A1, 4, attend("a", q + 2, 2 * l, 3, 0))

                def take1(b, m, acc):
                    r = RES[:, m, sl(b, NBLK)]
                    stt(r, r, ALPHA, acc, ALU.mult, ALU.add).then_inc(evac, 1)

                def take2(b, m, acc):
                    r = RES[:, m, sl(b, NBLK)]
                    tt(r, r, acc, ALU.add).then_inc(evac, 1)
                    dve.wait_ge(evac, (E_L + 17) * 2 + 2 * LBL * l + (2 * b + m + 1))
                    dve.bn_stats(BN[:, m, b, :], r).then_inc(*signal(LN_V, f"st{m}{b}"))

                stream(n + L_Y1, 4, attend("a", q + 3, 2 * l + 1, 3, 4), take=take1, per=len(Y1_TILES))
                stream(n + L_Y2, 4, none(), take=take2, ahead=None, per=len(Y2_TILES))
                wait_alone(dve, *done(LN_V, "st13", l))
                for m in range(M):
                    dve.bn_aggr(ST[:, 40 + 2 * m:42 + 2 * m], BN[:, m, :, :].rearrange("p a b -> p (a b)")).then_inc(*signal(LN_V, f"ag{m}"))
                dve.wait_ge(norm_s, l * 3 + 19)
                stt(ST[:, 52:54], ST[:, 40:44].rearrange("p (m s) -> p s m", s=2)[:, 0, :], -1.0, ST[:, 50:52], ALU.mult, ALU.mult).then_inc(*signal(LN_V, "shift"))
                dve.wait_ge(lw_in, 32 * l + 48)
                for c in range(NCH):
                    dve.wait_ge(ln_scaled, l * 8 + (c + 1))
                    r = RES[:, :, sl(c, S)]
                    tt(r, r, over(wk(0, D)[:, sl(c, S)], M), ALU.mult).then_inc(ln_gamma, 1)


INPUTS = ["x", "norm_w", "w_in", "ml_i_bias", "ml_f_bias", "ml_norm_w", "dn_conv_w", "dn_a_log", "dn_dt_bias", "dn_norm_w",
          "w_out", "final_norm_w", "mem_2", "w_in_2", "a_rel_bias_2", "b_gate_w_2", "b_gate_b_2", "b_norm_g_2", "w_mem_kv_2",
          "w_out_2", "ln_g_2", "ln_b_2"]


def kernel(**inputs):
    import concourse.bacc as bacc
    from concourse.bass_utils import run_bass_kernel_spmd

    nc = bacc.Bacc("TRN2", target_bir_lowering=False, num_devices=1)
    arrays, args = {}, []
    for name in INPUTS:
        a = np.ascontiguousarray(inputs[name])
        arrays[f"in_{name}"] = a
        args.append(nc.dram_tensor(f"in_{name}", a.shape, mybir.dt.from_np(a.dtype), kind="ExternalInput").ap())
    args.append(nc.dram_tensor("out", (1, S, D), F32, kind="ExternalOutput").ap())
    build(nc, *args)
    result = run_bass_kernel_spmd(nc, [arrays], core_ids=[0])
    return result.results[0]["out"]
```
